# Optimizing a Trainium2 kernel written in Bass

```python
import math
import jax, jax.numpy as jnp
from jax import lax
import numpy as np

D_MODEL = 1024
BATCH = 1
SEQ = 512
DEPTH = 1

MEM_LEN = 256
CONV_W = 512
CONV_WIDTH = 3
ATT_HEADS = 8
ATT_DH = 64
ATT_W = ATT_HEADS * ATT_DH
MOBA_BLOCK = 256
MOBA_TOPK = 3
Q_CHUNK = 16
MEM_HEADS = 4
MEM_DH = 128
MEM_W = MEM_HEADS * MEM_DH
NUM_BUCKETS = 32
MAX_EXACT = NUM_BUCKETS // 2
MAX_DISTANCE = 1024
D_FF = 2816
FFN_CONV_WIDTH = 3
N_BRANCHES = 3
RMS_EPS = 1e-6
NEG = -1e30

IN_SPLITS = [CONV_W, CONV_W, CONV_W, ATT_W, ATT_W, ATT_W, MEM_W, D_MODEL, D_MODEL, D_MODEL]
IN_COLS = sum(IN_SPLITS)
IN_OFFSETS = list(np.cumsum(IN_SPLITS)[:-1])


def rmsnorm(x, g):
    x32 = x.astype(jnp.float32)
    y = x32 * lax.rsqrt(jnp.mean(x32 * x32, axis=-1, keepdims=True) + RMS_EPS)
    return (y * g.astype(jnp.float32)).astype(x.dtype)

def causal_dwconv(u, w, b=None):
    width, c = w.shape
    y = lax.conv_general_dilated(
        u, w.astype(u.dtype)[:, None, :], window_strides=(1,), padding=[(width - 1, 0)],
        dimension_numbers=("NWC", "WIO", "NWC"), feature_group_count=c)
    if b is not None:
        y = y + b.astype(u.dtype)
    return y

def rel_bucket(dist):
    n = jnp.maximum(dist, 0)
    is_small = n < MAX_EXACT
    n_f = jnp.maximum(n, MAX_EXACT).astype(jnp.float32)
    large = MAX_EXACT + (jnp.log(n_f / MAX_EXACT) / math.log(MAX_DISTANCE / MAX_EXACT)
                         * (NUM_BUCKETS - MAX_EXACT)).astype(jnp.int32)
    large = jnp.minimum(large, NUM_BUCKETS - 1)
    return jnp.where(is_small, n, large)

def moba_attention(q, k, v, rel_bias):
    b_, h_, s_, dh = q.shape
    nb = -(-s_ // MOBA_BLOCK)
    pad = nb * MOBA_BLOCK - s_
    k_pad = jnp.pad(k, ((0, 0), (0, 0), (0, pad), (0, 0)))
    v_pad = jnp.pad(v, ((0, 0), (0, 0), (0, pad), (0, 0)))
    kb = k_pad.reshape(b_, h_, nb, MOBA_BLOCK, dh)
    vb = v_pad.reshape(b_, h_, nb, MOBA_BLOCK, dh)
    scale = dh ** -0.5

    k_mean = jnp.mean(kb.astype(jnp.float32), axis=3)
    gate = jnp.einsum("bhsd,bhnd->bhsn", q.astype(jnp.float32), k_mean)
    q_blk = jnp.arange(s_) // MOBA_BLOCK
    past = jnp.arange(nb)[None, :] < q_blk[:, None]
    gate = jnp.where(past, gate, NEG)
    k_sel = max(1, min(MOBA_TOPK, nb - 1))
    _, sel = lax.top_k(gate, k_sel)

    bias_hb = rel_bias.astype(jnp.float32).T
    b_idx = jnp.arange(b_)[:, None, None, None]
    h_idx = jnp.arange(h_)[None, :, None, None]
    blk_off = jnp.arange(MOBA_BLOCK)

    def chunk(c):
        start = c * Q_CHUNK
        qc = lax.dynamic_slice_in_dim(q, start, Q_CHUNK, axis=2)
        selc = lax.dynamic_slice_in_dim(sel, start, Q_CHUNK, axis=2)
        t = start + jnp.arange(Q_CHUNK)
        valid = jnp.arange(k_sel)[None, :] < (t // MOBA_BLOCK)[:, None]
        kg = kb[b_idx, h_idx, selc]
        vg = vb[b_idx, h_idx, selc]
        s_sel = jnp.einsum("bhqd,bhqjkd->bhqjk", qc, kg).astype(jnp.float32) * scale
        k_pos = selc[..., None] * MOBA_BLOCK + blk_off
        bucket = rel_bucket(t[None, None, :, None, None] - k_pos)
        bias = bias_hb[h_idx[..., None], bucket]
        s_sel = jnp.where(valid[None, None, :, :, None], s_sel + bias, NEG)
        own = start // MOBA_BLOCK
        ko = lax.dynamic_slice_in_dim(k_pad, own * MOBA_BLOCK, MOBA_BLOCK, axis=2)
        vo = lax.dynamic_slice_in_dim(v_pad, own * MOBA_BLOCK, MOBA_BLOCK, axis=2)
        s_own = jnp.einsum("bhqd,bhkd->bhqk", qc, ko).astype(jnp.float32) * scale
        dist = t[:, None] - (own * MOBA_BLOCK + blk_off)[None, :]
        bias_own = bias_hb[:, rel_bucket(dist)]
        s_own = jnp.where(dist[None, None] >= 0, s_own + bias_own[None], NEG)
        logits = jnp.concatenate([s_sel.reshape(b_, h_, Q_CHUNK, k_sel * MOBA_BLOCK), s_own], axis=-1)
        p = jax.nn.softmax(logits, axis=-1).astype(v.dtype)
        p_sel = p[..., : k_sel * MOBA_BLOCK].reshape(b_, h_, Q_CHUNK, k_sel, MOBA_BLOCK)
        p_own = p[..., k_sel * MOBA_BLOCK:]
        return (jnp.einsum("bhqjk,bhqjkd->bhqd", p_sel, vg)
                + jnp.einsum("bhqk,bhkd->bhqd", p_own, vo))

    out = lax.map(chunk, jnp.arange(s_ // Q_CHUNK))
    return jnp.transpose(out, (1, 2, 0, 3, 4)).reshape(b_, h_, s_, dh)

def memory_attention(qm, mem_n, w_mem_kv):
    b_, s_, _ = qm.shape
    kv = mem_n @ w_mem_kv
    mk, mv = jnp.split(kv, 2, axis=-1)
    mk = mk.reshape(b_, -1, MEM_HEADS, MEM_DH)
    mv = mv.reshape(b_, -1, MEM_HEADS, MEM_DH)
    q4 = qm.reshape(b_, s_, MEM_HEADS, MEM_DH)
    s = jnp.einsum("bshd,bmhd->bhsm", q4, mk).astype(jnp.float32) * (MEM_DH ** -0.5)
    p = jax.nn.softmax(s, axis=-1).astype(qm.dtype)
    return jnp.einsum("bhsm,bmhd->bshd", p, mv).reshape(b_, s_, MEM_W)

def first_inputs(seed: int = 0) -> dict:
    key = jax.random.key(seed)
    ks = jax.random.split(key, 20)

    def nrm(k, shape, scale):
        return jax.random.normal(k, shape, jnp.float32) * scale

    def gain(k):
        return 1.0 + nrm(k, (DEPTH, D_MODEL), 0.05)

    return {
        "x": nrm(ks[0], (BATCH, SEQ, D_MODEL), 1.0),
        "mem": nrm(ks[1], (BATCH, MEM_LEN, D_MODEL), 1.0),
        "rel_bias": nrm(ks[2], (NUM_BUCKETS, ATT_HEADS), 0.5),
        "g_pre_mix": gain(ks[3]),
        "g_post_mix": gain(ks[4]),
        "g_pre_ffn": gain(ks[5]),
        "g_post_ffn": gain(ks[6]),
        "g_mem": gain(ks[7]),
        "w_in": nrm(ks[8], (DEPTH, D_MODEL, IN_COLS), D_MODEL ** -0.5),
        "b_gate": nrm(ks[9], (DEPTH, N_BRANCHES * D_MODEL), 0.01),
        "conv_mix_w": nrm(ks[10], (DEPTH, CONV_WIDTH, CONV_W), CONV_WIDTH ** -0.5),
        "w_conv_out": nrm(ks[11], (DEPTH, CONV_W, D_MODEL), CONV_W ** -0.5),
        "w_attn_out": nrm(ks[12], (DEPTH, ATT_W, D_MODEL), ATT_W ** -0.5),
        "w_mem_kv": nrm(ks[13], (DEPTH, D_MODEL, 2 * MEM_W), D_MODEL ** -0.5),
        "w_mem_out": nrm(ks[14], (DEPTH, MEM_W, D_MODEL), MEM_W ** -0.5),
        "w_out": nrm(ks[15], (DEPTH, D_MODEL, D_MODEL), D_MODEL ** -0.5),
        "w_up": nrm(ks[16], (DEPTH, D_MODEL, 2 * D_FF), D_MODEL ** -0.5),
        "ffn_conv_w": nrm(ks[17], (DEPTH, FFN_CONV_WIDTH, 2 * D_FF), FFN_CONV_WIDTH ** -0.5),
        "ffn_conv_b": nrm(ks[18], (DEPTH, 2 * D_FF), 0.01),
        "w_down": nrm(ks[19], (DEPTH, D_FF, D_MODEL), D_FF ** -0.5),
    }

def first_block(x, mem, rel_bias, g_pre_mix, g_post_mix, g_pre_ffn, g_post_ffn, g_mem,
              w_in, b_gate, conv_mix_w, w_conv_out, w_attn_out, w_mem_kv, w_mem_out,
              w_out, w_up, ffn_conv_w, ffn_conv_b, w_down):
    b_, s_, d_ = x.shape
    for l in range(DEPTH):
        h = rmsnorm(x, g_pre_mix[l])
        proj = h @ w_in[l]
        (cb, cc, cv, q, k, v, qm, ga, gb, gc) = jnp.split(proj, IN_OFFSETS, axis=-1)
        y_a = (cb * causal_dwconv(cc * cv, conv_mix_w[l])) @ w_conv_out[l]
        to_heads = lambda t: jnp.transpose(t.reshape(b_, s_, ATT_HEADS, ATT_DH), (0, 2, 1, 3))
        o = moba_attention(to_heads(q), to_heads(k), to_heads(v), rel_bias)
        y_b = jnp.transpose(o, (0, 2, 1, 3)).reshape(b_, s_, ATT_W) @ w_attn_out[l]
        y_c = memory_attention(qm, rmsnorm(mem, g_mem[l]), w_mem_kv[l]) @ w_mem_out[l]
        bg = b_gate[l].reshape(N_BRANCHES, d_)
        merged = (jax.nn.sigmoid(ga + bg[0]) * y_a + jax.nn.sigmoid(gb + bg[1]) * y_b
                  + jax.nn.sigmoid(gc + bg[2]) * y_c)
        x = x + rmsnorm(merged @ w_out[l], g_post_mix[l])
        h = rmsnorm(x, g_pre_ffn[l])
        u = causal_dwconv(h @ w_up[l], ffn_conv_w[l], ffn_conv_b[l])
        a, g = jnp.split(u, 2, axis=-1)
        f = (jax.nn.gelu(a) * g) @ w_down[l]
        x = x + rmsnorm(f, g_post_ffn[l])
    return x


SSD_EXPAND = 2
SSD_D_INNER = SSD_EXPAND * D_MODEL
SSD_HEAD_DIM = 64
SSD_N_HEADS = SSD_D_INNER // SSD_HEAD_DIM
SSD_N_GROUPS = 4
SSD_D_STATE = 128
SSD_CONV = 4
SSD_CHUNK = 128
SSD_CONV_DIM = SSD_D_INNER + 2 * SSD_N_GROUPS * SSD_D_STATE
ATT_HEAD_DIM = 64
ATT_N_HEADS = D_MODEL // ATT_HEAD_DIM
ATT_N_KV = 4
ATT_WINDOW = 128
ATT_BLOCK = 128
ATT_SCALE = ATT_HEAD_DIM ** -0.5
ROPE_THETA = 500000.0
ROPE_DIM = ATT_HEAD_DIM // 4
MOE_N_GROUPS = 8
MOE_EXPERTS_PER_GROUP = 8
MOE_N_EXPERTS = MOE_N_GROUPS * MOE_EXPERTS_PER_GROUP
MOE_TOP_K = 2
MOE_D_FF = 256
MOE_BLOCK = 128

COL_Z = SSD_D_INNER
COL_XBC = SSD_CONV_DIM
COL_DT = SSD_N_HEADS
COL_Q = ATT_N_HEADS * ATT_HEAD_DIM
COL_K = ATT_N_KV * ATT_HEAD_DIM
COL_V = ATT_N_KV * ATT_HEAD_DIM
COL_GATE = D_MODEL
IN_COLS_2 = COL_Z + COL_XBC + COL_DT + COL_Q + COL_K + COL_V + 2 * COL_GATE
IN_SPLITS_2 = (COL_Z,
             COL_Z + COL_XBC,
             COL_Z + COL_XBC + COL_DT,
             COL_Z + COL_XBC + COL_DT + COL_Q,
             COL_Z + COL_XBC + COL_DT + COL_Q + COL_K,
             COL_Z + COL_XBC + COL_DT + COL_Q + COL_K + COL_V,
             COL_Z + COL_XBC + COL_DT + COL_Q + COL_K + COL_V + COL_GATE)


def rms_norm(t, g):
    tf = t.astype(jnp.float32)
    tf = tf * lax.rsqrt(jnp.mean(tf * tf, axis=-1, keepdims=True) + RMS_EPS)
    return (tf * g.astype(jnp.float32)).astype(t.dtype)

def ssd_branch(z, xbc, dt_raw, conv_w, conv_b, dt_bias, a_log, d_skip, ssd_norm_g):
    b, s, _ = xbc.shape
    G, J, P, N, L = SSD_N_GROUPS, SSD_N_HEADS // SSD_N_GROUPS, SSD_HEAD_DIM, SSD_D_STATE, SSD_CHUNK
    nc = s // L
    xbc = lax.conv_general_dilated(xbc, conv_w[:, None, :].astype(xbc.dtype), window_strides=(1,),
                                   padding=[(SSD_CONV - 1, 0)], dimension_numbers=('NWC', 'WIO', 'NWC'),
                                   feature_group_count=SSD_CONV_DIM) + conv_b
    xbc = jax.nn.silu(xbc)
    xs, bm, cm = jnp.split(xbc, [SSD_D_INNER, SSD_D_INNER + G * N], axis=-1)
    xs = xs.reshape(b, nc, L, G, J, P)
    bm = bm.reshape(b, nc, L, G, N)
    cm = cm.reshape(b, nc, L, G, N)
    dt = jax.nn.softplus(dt_raw.astype(jnp.float32) + dt_bias.astype(jnp.float32))
    a = -jnp.exp(a_log.astype(jnp.float32))
    dt_c = dt.reshape(b, nc, L, G, J)
    a_cum = jnp.cumsum(dt_c * a.reshape(G, J), axis=2)
    xdt = xs * dt_c[..., None].astype(xs.dtype)
    causal = (jnp.arange(L)[:, None] >= jnp.arange(L)[None, :])[None, None, :, :, None, None]
    seg = a_cum[:, :, :, None] - a_cum[:, :, None, :]
    decay = jnp.exp(jnp.where(causal, seg, -jnp.inf)).astype(xs.dtype)
    cb = jnp.einsum('bclgn,bcsgn->bclsg', cm, bm)
    y_diag = jnp.einsum('bclsgj,bcsgjp->bclgjp', cb[..., None] * decay, xdt)
    decay_to_end = jnp.exp(a_cum[:, :, -1:] - a_cum).astype(xs.dtype)
    states = jnp.einsum('bclgn,bclgjp->bcgjpn', bm, xdt * decay_to_end[..., None])
    chunk_decay = jnp.exp(a_cum[:, :, -1]).astype(states.dtype)

    def step(carry, inp):
        st, dec = inp
        return carry * dec[..., None, None] + st, carry

    init = jnp.zeros((b, G, J, P, N), states.dtype)
    _, prev = lax.scan(step, init, (jnp.moveaxis(states, 1, 0), jnp.moveaxis(chunk_decay, 1, 0)))
    prev = jnp.moveaxis(prev, 0, 1)
    y_off = jnp.einsum('bclgn,bcgjpn->bclgjp', cm, prev) * jnp.exp(a_cum)[..., None].astype(xs.dtype)
    y = (y_diag + y_off + xs * d_skip.reshape(G, J)[:, :, None].astype(xs.dtype)).reshape(b, s, SSD_D_INNER)
    yz = (y * jax.nn.silu(z)).reshape(b, s, G, SSD_D_INNER // G)
    return rms_norm(yz, ssd_norm_g.reshape(G, -1)).reshape(b, s, SSD_D_INNER)

def partial_rope(t, cos, sin):
    half = ROPE_DIM // 2
    t1, t2, rest = t[..., :half], t[..., half:ROPE_DIM], t[..., ROPE_DIM:]
    cos = cos.astype(t.dtype)
    sin = sin.astype(t.dtype)
    return jnp.concatenate([t1 * cos - t2 * sin, t2 * cos + t1 * sin, rest], axis=-1)

def swa_sink_branch(q, k, v, positions, q_norm_g, k_norm_g, sinks):
    b, s, _ = q.shape
    HD, KV, QG, BLK = ATT_HEAD_DIM, ATT_N_KV, ATT_N_HEADS // ATT_N_KV, ATT_BLOCK
    nb = s // BLK
    q = rms_norm(q.reshape(b, s, ATT_N_HEADS, HD), q_norm_g)
    k = rms_norm(k.reshape(b, s, KV, HD), k_norm_g)
    v = v.reshape(b, s, KV, HD)
    inv_freq = ROPE_THETA ** (-jnp.arange(0, ROPE_DIM, 2, dtype=jnp.float32) / ROPE_DIM)
    ang = positions.astype(jnp.float32)[..., None] * inv_freq
    cos, sin = jnp.cos(ang)[:, :, None, :], jnp.sin(ang)[:, :, None, :]
    q = partial_rope(q, cos, sin)
    k = partial_rope(k, cos, sin)
    qb = q.reshape(b, nb, BLK, KV, QG, HD)
    kb = k.reshape(b, nb, BLK, KV, HD)
    vb = v.reshape(b, nb, BLK, KV, HD)
    pad = ((0, 0), (1, 0), (0, 0), (0, 0), (0, 0))
    kk = jnp.concatenate([jnp.pad(kb, pad)[:, :-1], kb], axis=2)
    vv = jnp.concatenate([jnp.pad(vb, pad)[:, :-1], vb], axis=2)
    scores = jnp.einsum('bnqhgd,bnkhd->bnhgqk', qb, kk).astype(jnp.float32) * ATT_SCALE
    qi = jnp.arange(nb)[:, None, None] * BLK + jnp.arange(BLK)[None, :, None]
    ki = (jnp.arange(nb)[:, None, None] - 1) * BLK + jnp.arange(2 * BLK)[None, None, :]
    diff = qi - ki
    mask = (diff >= 0) & (diff < ATT_WINDOW) & (ki >= 0)
    scores = jnp.where(mask[None, :, None, None], scores, -jnp.inf)
    sink = sinks.astype(jnp.float32).reshape(KV, QG)[None, None, :, :, None]
    m = jnp.maximum(jnp.max(scores, axis=-1), sink)
    p = jnp.exp(scores - m[..., None])
    denom = jnp.sum(p, axis=-1) + jnp.exp(sink - m)
    p = (p / denom[..., None]).astype(v.dtype)
    out = jnp.einsum('bnhgqk,bnkhd->bnqhgd', p, vv)
    return out.reshape(b, s, ATT_N_HEADS * HD)

def hier_moe(h2, w_rg, b_rg, w_re, b_re, w_gate_e, w_up_e, w_down_e):
    t = h2.shape[0]
    rows = jnp.arange(t)
    g_logits = jnp.dot(h2, w_rg).astype(jnp.float32) + b_rg.astype(jnp.float32)
    g_prob = jax.nn.softmax(g_logits, axis=-1)
    g_sel = jnp.argmax(g_logits, axis=-1).astype(jnp.int32)
    p_group = g_prob[rows, g_sel]
    e_logits_all = jnp.einsum('td,gde->tge', h2, w_re).astype(jnp.float32) + b_re.astype(jnp.float32)
    e_logits = e_logits_all[rows, g_sel]
    top_v, top_i = lax.top_k(e_logits, MOE_TOP_K)
    gate = p_group[:, None] * jax.nn.softmax(top_v, axis=-1)
    expert_id = g_sel[:, None] * MOE_EXPERTS_PER_GROUP + top_i.astype(jnp.int32)
    n_assign = t * MOE_TOP_K
    flat_e = expert_id.reshape(-1)
    flat_w = gate.reshape(-1)
    flat_t = jnp.arange(n_assign, dtype=jnp.int32) // MOE_TOP_K
    order = jnp.argsort(flat_e)
    sorted_e = flat_e[order]
    counts = jnp.bincount(flat_e, length=MOE_N_EXPERTS)
    starts = jnp.cumsum(counts) - counts
    padded = (counts + MOE_BLOCK - 1) // MOE_BLOCK * MOE_BLOCK
    padded_end = jnp.cumsum(padded)
    padded_start = padded_end - padded
    dest = padded_start[sorted_e] + jnp.arange(n_assign) - starts[sorted_e]
    n_rows = n_assign + MOE_N_EXPERTS * MOE_BLOCK
    n_blocks = n_rows // MOE_BLOCK
    tok = jnp.zeros((n_rows,), jnp.int32).at[dest].set(flat_t[order])
    wt = jnp.zeros((n_rows,), jnp.float32).at[dest].set(flat_w[order])
    block_e = jnp.minimum(jnp.searchsorted(padded_end, jnp.arange(n_blocks) * MOE_BLOCK, side='right'),
                          MOE_N_EXPERTS - 1)
    xs = h2[tok].reshape(n_blocks, MOE_BLOCK, -1)

    def expert_block(args):
        xb, e = args
        hid = jax.nn.silu(xb @ w_gate_e[e]) * (xb @ w_up_e[e])
        return hid @ w_down_e[e]

    ys = lax.map(expert_block, (xs, block_e)).reshape(n_rows, -1)
    return jnp.zeros_like(h2).at[tok].add(ys * wt[:, None].astype(ys.dtype))

def hybrid_layer(x, positions, norm1_g, w_in, conv_w, conv_b, dt_bias, a_log, d_skip, ssd_norm_g,
                 w_ssd_out, q_norm_g, k_norm_g, sinks, w_attn_out, w_out, norm2_g, w_router_group,
                 b_router_group, w_router_expert, b_router_expert, w_gate_e, w_up_e, w_down_e):
    b, s, d = x.shape
    h = rms_norm(x, norm1_g)
    proj = h @ w_in
    z, xbc, dt_raw, q, k, v, g_ssd, g_att = jnp.split(proj, IN_SPLITS_2, axis=-1)
    y_ssd = ssd_branch(z, xbc, dt_raw, conv_w, conv_b, dt_bias, a_log, d_skip, ssd_norm_g) @ w_ssd_out
    y_att = swa_sink_branch(q, k, v, positions, q_norm_g, k_norm_g, sinks) @ w_attn_out
    merged = jax.nn.sigmoid(g_ssd) * y_ssd + jax.nn.sigmoid(g_att) * y_att
    x = x + merged @ w_out
    h2 = rms_norm(x, norm2_g).reshape(b * s, d)
    y_moe = hier_moe(h2, w_router_group, b_router_group, w_router_expert, b_router_expert,
                     w_gate_e, w_up_e, w_down_e)
    return x + y_moe.reshape(b, s, d)

def second_inputs(seed: int = 0) -> dict:
    key = jax.random.key(seed)
    ks = jax.random.split(key, 24)
    L = DEPTH

    def nrm(k, shape, scale):
        return jax.random.normal(k, shape, jnp.float32) * scale

    x = nrm(ks[0], (BATCH, SEQ, D_MODEL), 1.0)
    positions = (jax.random.randint(ks[1], (BATCH, 1), 0, 1024, dtype=jnp.int32)
                 + jnp.arange(SEQ, dtype=jnp.int32)[None, :])
    dt0 = jnp.exp(jax.random.uniform(ks[6], (L, SSD_N_HEADS), jnp.float32,
                                     minval=math.log(1e-3), maxval=math.log(1e-1)))
    return {
        'x': x,
        'positions': positions,
        'norm1_g': 1.0 + nrm(ks[2], (L, D_MODEL), 0.02),
        'w_in': nrm(ks[3], (L, D_MODEL, IN_COLS_2), D_MODEL ** -0.5),
        'conv_w': nrm(ks[4], (L, SSD_CONV, SSD_CONV_DIM), SSD_CONV ** -0.5),
        'conv_b': nrm(ks[5], (L, SSD_CONV_DIM), 0.02),
        'dt_bias': dt0 + jnp.log(-jnp.expm1(-dt0)),
        'a_log': jnp.log(jax.random.uniform(ks[7], (L, SSD_N_HEADS), jnp.float32, minval=1.0, maxval=16.0)),
        'd_skip': 1.0 + nrm(ks[8], (L, SSD_N_HEADS), 0.1),
        'ssd_norm_g': 1.0 + nrm(ks[9], (L, SSD_D_INNER), 0.02),
        'w_ssd_out': nrm(ks[10], (L, SSD_D_INNER, D_MODEL), SSD_D_INNER ** -0.5),
        'q_norm_g': 1.0 + nrm(ks[11], (L, ATT_HEAD_DIM), 0.02),
        'k_norm_g': 1.0 + nrm(ks[12], (L, ATT_HEAD_DIM), 0.02),
        'sinks': nrm(ks[13], (L, ATT_N_HEADS), 0.5),
        'w_attn_out': nrm(ks[14], (L, ATT_N_HEADS * ATT_HEAD_DIM, D_MODEL), (ATT_N_HEADS * ATT_HEAD_DIM) ** -0.5),
        'w_out': nrm(ks[15], (L, D_MODEL, D_MODEL), D_MODEL ** -0.5),
        'norm2_g': 1.0 + nrm(ks[16], (L, D_MODEL), 0.02),
        'w_router_group': nrm(ks[17], (L, D_MODEL, MOE_N_GROUPS), D_MODEL ** -0.5),
        'b_router_group': nrm(ks[18], (L, MOE_N_GROUPS), 0.01),
        'w_router_expert': nrm(ks[19], (L, MOE_N_GROUPS, D_MODEL, MOE_EXPERTS_PER_GROUP), D_MODEL ** -0.5),
        'b_router_expert': nrm(ks[20], (L, MOE_N_GROUPS, MOE_EXPERTS_PER_GROUP), 0.01),
        'w_gate_e': nrm(ks[21], (L, MOE_N_EXPERTS, D_MODEL, MOE_D_FF), D_MODEL ** -0.5),
        'w_up_e': nrm(ks[22], (L, MOE_N_EXPERTS, D_MODEL, MOE_D_FF), D_MODEL ** -0.5),
        'w_down_e': nrm(ks[23], (L, MOE_N_EXPERTS, MOE_D_FF, D_MODEL), MOE_D_FF ** -0.5),
    }

def second_block(x, positions, norm1_g, w_in, conv_w, conv_b, dt_bias, a_log, d_skip, ssd_norm_g,
              w_ssd_out, q_norm_g, k_norm_g, sinks, w_attn_out, w_out, norm2_g, w_router_group,
              b_router_group, w_router_expert, b_router_expert, w_gate_e, w_up_e, w_down_e):
    for l in range(DEPTH):
        x = hybrid_layer(x, positions, norm1_g[l], w_in[l], conv_w[l], conv_b[l], dt_bias[l], a_log[l],
                         d_skip[l], ssd_norm_g[l], w_ssd_out[l], q_norm_g[l], k_norm_g[l], sinks[l],
                         w_attn_out[l], w_out[l], norm2_g[l], w_router_group[l], b_router_group[l],
                         w_router_expert[l], b_router_expert[l], w_gate_e[l], w_up_e[l], w_down_e[l])
    return x


def setup_inputs(seed=0):
    out = dict(first_inputs(seed))
    for name, value in second_inputs(seed + 1).items():
        if name != "x":
            out[name + "_2"] = value
    return out


def reference(
    x, mem, rel_bias, g_pre_mix, g_post_mix, g_pre_ffn, g_post_ffn, g_mem, w_in, b_gate,
    conv_mix_w, w_conv_out, w_attn_out, w_mem_kv, w_mem_out, w_out, w_up, ffn_conv_w,
    ffn_conv_b, w_down, positions_2, norm1_g_2, w_in_2, conv_w_2, conv_b_2, dt_bias_2, a_log_2,
    d_skip_2, ssd_norm_g_2, w_ssd_out_2, q_norm_g_2, k_norm_g_2, sinks_2, w_attn_out_2, w_out_2,
    norm2_g_2, w_router_group_2, b_router_group_2, w_router_expert_2, b_router_expert_2,
    w_gate_e_2, w_up_e_2, w_down_e_2,
):
    x = first_block(
        x, mem, rel_bias, g_pre_mix, g_post_mix, g_pre_ffn, g_post_ffn, g_mem, w_in, b_gate,
        conv_mix_w, w_conv_out, w_attn_out, w_mem_kv, w_mem_out, w_out, w_up, ffn_conv_w,
        ffn_conv_b, w_down,
    )
    return second_block(
        x, positions_2, norm1_g_2, w_in_2, conv_w_2, conv_b_2, dt_bias_2, a_log_2, d_skip_2,
        ssd_norm_g_2, w_ssd_out_2, q_norm_g_2, k_norm_g_2, sinks_2, w_attn_out_2, w_out_2,
        norm2_g_2, w_router_group_2, b_router_group_2, w_router_expert_2, b_router_expert_2,
        w_gate_e_2, w_up_e_2, w_down_e_2,
    )


_drawn_inputs = setup_inputs


def setup_inputs(seed=0):
    import zlib

    import numpy as np

    out = dict(_drawn_inputs(seed))
    spreads = {}
    factors = {'g_mem': 5.799,
     'b_gate': 8.0,
     'ffn_conv_b': 5.062,
     'norm1_g_2': 5.168,
     'conv_b_2': 4.745,
     'ssd_norm_g_2': 6.269,
     'q_norm_g_2': 8.0,
     'k_norm_g_2': 8.0,
     'sinks_2': 64.0,
     'norm2_g_2': 4.455,
     'b_router_group_2': 8.0,
     'b_router_expert_2': 8.0,
     'd_skip_2': 32.673}
    for name, (base, spread) in spreads.items():
        noise = np.random.default_rng([zlib.crc32(name.encode()), seed]).standard_normal(out[name].shape)
        drawn = base * np.exp(spread * noise) if base else spread * noise
        out[name] = __import__('jax').numpy.asarray(drawn.astype(out[name].dtype))
    for name, factor in factors.items():
        out[name] = (out[name] * factor).astype(out[name].dtype)
    return out
```

```python
import math
from contextlib import ExitStack

import numpy as np
import concourse.bass as bass
from concourse import mybir

F32 = mybir.dt.float32
I32 = mybir.dt.int32
ACT = mybir.ActivationFunctionType
ALU = mybir.AluOpType
AX = mybir.AxisListType.X

NEG = -1e30
EPS = 1e-6
CAP = 32
NOV = 31
NST = 64 * CAP
NSLOT = NST + NOV * 128
HEADS2 = [4 * (2 * kp + par) + i for kp in range(2) for i in range(4) for par in range(2)]

SLOTS = ["q", "k", "v", "qm", "mk", "mv", "cc", "cv", "cb", "yconv", "ga0", "ga1", "yattn", "gb0", "gb1",
         "ymem", "gc0", "gc1", "out0", "out1"]
SLOTS += [f"up{i}" for i in range(11)] + [f"down{i}" for i in range(6)]
SLOTS += ["bm", "cm"] + [f"{n}{g}" for g in range(4) for n in ("xs", "z")]
SLOTS += ["gs0", "so0", "so1", "gs1", "so2", "so3", "q0", "q1", "kv", "gt0", "ao0", "gt1", "ao1", "oo0", "oo1"]
SLOT = {n: i for i, n in enumerate(SLOTS)}

COLS = [("g_pre_mix", 8), ("g_mem", 8), ("b_gate", 24), ("conv_mix", 12), ("g_pre_ffn", 8), ("ffn_w", 132),
        ("ffn_b", 44), ("norm1_g", 8), ("conv_w", 96), ("conv_b", 24), ("norm2_g", 8)]
ROWS = [("dt_bias", 32), ("a_log", 32), ("d_skip", 32), ("q_g", 64), ("k_g", 64), ("sinks", 16),
        ("b_r", 72)]
CST = [("ident", 128), ("triu", 128), ("stri", 128), ("ones", 128), ("e32", 64), ("rev64", 64), ("rev8", 8),
       ("iob", 31), ("invf", 8), ("half", 64)]


def offsets(parts):
    at, out = 0, {}
    for n, w in parts:
        out[n] = (at, w)
        at += w
    return out, at


COL, NCOL = offsets(COLS)
ROW, NROW = offsets(ROWS)
CS, NCS = offsets(CST)


class Lane:

    def __init__(self, sem, dma_sems=()):
        self.sem, self.n, self.ops, self.seen = sem, 0, [], {}
        self.dma_sems, self.dma_n = list(dma_sems), 0

    def wait(self, *toks):
        for t in toks:
            if t is None:
                continue
            if isinstance(t, list):
                self.wait(*t)
                continue
            sem, value = t
            if self.seen.get(id(sem), 0) < value:
                self.seen[id(sem)] = value
                self.ops.append(lambda e, s=sem, v=value: e.wait_ge(s, v))

    def do(self, fn, *toks, inc=True):
        self.wait(*toks)
        if not inc:
            self.ops.append(fn)
            return None
        self.n += 1
        self.ops.append(lambda e: fn(e).then_inc(self.sem, 1))
        return (self.sem, self.n)

    def dma(self, out, in_, *toks, how=None):
        k, m = self.dma_n % len(self.dma_sems), self.dma_n // len(self.dma_sems)
        self.dma_n += 1
        sem = self.dma_sems[k]
        if m:
            self.wait((sem, 16 * m))
        self.wait(*toks)
        fn = how or (lambda e: e.dma_start(out, in_))
        self.ops.append(lambda e: fn(e).then_inc(sem, 16))
        return (sem, 16 * (m + 1))

    def pending(self):
        out = [(self.sem, self.n)] if self.n else []
        for k, s in enumerate(self.dma_sems):
            m = (self.dma_n - k + len(self.dma_sems) - 1) // len(self.dma_sems)
            if m > 0:
                out.append((s, 16 * m))
        return out

    def play(self, e):
        for op in self.ops:
            op(e)


class Body(Lane):

    def wait(self, *toks):
        for t in toks:
            if t is None:
                continue
            if isinstance(t, list):
                self.wait(*t)
                continue
            sem, value = t
            if self.seen.get(id(sem), 0) < value:
                self.seen[id(sem)] = value
                self.ops.append(lambda e, i, s=sem, v=value: self.until(e, s, i * self.gain[id(s)] + v))

    def until(self, e, sem, value):
        e.wait_ge(sem, value)
        if self.rest:
            e.sem_inc(self.rest, 1)

    def do(self, fn, *toks, inc=True):
        self.wait(*toks)
        if not inc:
            self.ops.append(lambda e, i: fn(e))
            return None
        self.n += 1
        self.ops.append(lambda e, i: fn(e).then_inc(self.sem, 1))
        return (self.sem, self.n)

    def dma(self, out, in_, *toks, how=None):
        sem = self.dma_sems[self.dma_n]
        self.dma_n += 1
        self.wait(*toks)
        fn = how or (lambda e, i: e.dma_start(out, in_))
        self.ops.append(lambda e, i: fn(e, i).then_inc(sem, 16))
        return (sem, 16)


class Ring:

    def __init__(self, n):
        self.free, self.i = [[] for _ in range(n)], 0

    def take(self):
        k = self.i % len(self.free)
        self.i += 1
        toks = self.free[k]
        assert toks is not None, "a place is taken before it was given back"
        self.free[k] = None
        return k, toks

    def give(self, k, *toks):
        self.free[k] = list(toks)


def zipped(a, b, na=1, nb=1):
    live = [(a, na), (b, nb)]
    while live:
        for g in list(live):
            for _ in range(g[1]):
                if next(g[0], StopIteration) is StopIteration:
                    live.remove(g)
                    break


def two_layers(nc, dram, out):
    ctx = ExitStack()
    with ctx:
        def sem(name):
            return ctx.enter_context(nc.semaphore(name))

        PE, DV, AC, PO, SP = (Lane(sem("s_" + n), [sem(f"d_{n}{i}") for i in range(k)])
                              for n, k in (("pe", 0), ("dve", 0), ("act", 6), ("pool", 12), ("sp", 16)))
        AR = ctx.enter_context(nc.sbuf_tensor("AR", [128, 52900], F32))
        IA = ctx.enter_context(nc.sbuf_tensor("IA", [128, 176], I32))
        PS = ctx.enter_context(nc.psum_tensor("PS", [128, 8, 512], F32))
        banks = Ring(8)

        def snap():
            return PE.pending() + DV.pending() + AC.pending() + PO.pending()

        def area(off, n):
            return AR[:, off:off + n]

        def cut(ap, a):
            return ap.rearrange("p (a b) -> p a b", a=a)

        top = [0]

        def alloc(n):
            top[0] += n
            return top[0] - n

        CPo, CCo, RRo, WSo, STo = (alloc(n) for n in (NCOL, NCS, NROW, 832, 560))
        CP, CC, RR, WS = area(CPo, NCOL), area(CCo, NCS), area(RRo, NROW), area(WSo, 832)
        Xo, HTo, MGo, GBo = alloc(4096), alloc(4096), alloc(4096), alloc(1024)
        WRo = alloc(12288)
        Fo = alloc(0)
        X, HT, MG, GB = cut(area(Xo, 4096), 4), cut(area(HTo, 4096), 8), cut(area(MGo, 4096), 8), area(GBo, 1024)
        XN = cut(area(MGo, 4096), 4)
        stat_at = [0]

        def col(n):
            stat_at[0] += n
            assert stat_at[0] <= 560
            return AR[:, STo + stat_at[0] - n:STo + stat_at[0]]

        def cp(name, j=0, n=1):
            o = COL[name][0] + j
            return CP[:, o:o + n]

        def cc(name):
            return CC[:, CS[name][0]:CS[name][0] + CS[name][1]]

        def rr(name):
            return RR[:, ROW[name][0]:ROW[name][0] + ROW[name][1]]

        ident = cc("ident")

        def bank():
            k, toks = banks.take()
            return PS[:, k, :], toks, k

        def mm(o, l, r, start, stop, *toks, inc=False):
            return PE.do(lambda e: e.matmul(o, l, r, start=start, stop=stop), *toks, inc=inc)

        def tr(o, i, *toks, inc=False):
            return PE.do(lambda e: e.transpose(o, i, ident), *toks, inc=inc)

        def act(o, i, f, *toks, **kw):
            return AC.do(lambda e: e.activation(o, i, f, **kw), *toks)

        def ts(o, i, s1, s2, op0, op1, *toks, lane=None):
            return (lane or DV).do(lambda e: e.tensor_scalar(o, i, s1, s2, op0, op1), *toks)

        def ts1(o, i, s1, op0, *toks, lane=None):
            return (lane or DV).do(lambda e: e.tensor_scalar(o, i, s1, None, op0), *toks)

        def tt(o, a, b, op, *toks, lane=None):
            return (lane or DV).do(lambda e: e.tensor_tensor(o, a, b, op), *toks)

        def stt(o, a, s, b, op0, op1, *toks):
            return DV.do(lambda e: e.scalar_tensor_tensor(out=o, in0=a, scalar=s, in1=b, op0=op0, op1=op1), *toks)

        def cpy(o, i, *toks, lane=None):
            return (lane or DV).do(lambda e: e.tensor_copy(o, i), *toks)

        def red(o, i, op, *toks, negate=False):
            return DV.do(lambda e: e.tensor_reduce(o, i, AX, op, negate=negate), *toks)

        wring = Ring(3)

        def wload(name):
            k, toks = wring.take()
            w = AR[:, WRo + 4096 * k:WRo + 4096 * (k + 1)]
            return w, SP.dma(w, dram["wpack"][SLOT[name]], *toks), k

        t_x = [SP.dma(X[:, i, :], dram["x"][128 * i:128 * i + 128, :]) for i in range(4)]
        t_cp = AC.dma(CP, dram["cols"])
        t_cc = AC.dma(CC, dram["consts"])
        t_rr = AC.dma(RR, dram["rows"].to_broadcast([128, NROW]))
        t_ws = AC.dma(WS, dram["wsmall"])
        half = cc("half")

        def rstd(ss, n, width, *toks):
            a = ts(ss, ss, 1.0 / width, EPS, ALU.mult, ALU.add, *toks, lane=PO)
            return tt(ss, ss, half[:, 0:n], ALU.pow, a, t_cc, lane=PO)

        def norm_t(src, n, g, dst, xn, toks):
            ss = col(n)
            a = [act(xn[:, i, :], src[:, i, :], ACT.Square, toks, accum_out=ss[:, i:i + 1]) for i in range(n)]
            r = rstd(ss, n, 1024, a)
            d = [ts1(xn[:, i, :], src[:, i, :], ss[:, i:i + 1], ALU.mult, r, toks) for i in range(n)]
            done = []
            for k in range(8):
                b, bt, bk = bank()
                for i in range(n):
                    p = tr(b[:, 128 * i:128 * i + 128], xn[:, i, 128 * k:128 * k + 128], d[i], bt, t_cc,
                           inc=(i == n - 1))
                o = dst[:, k, 0:128 * n]
                if k % 2:
                    e = ts1(o, b[:, 0:128 * n], cp(g, k), ALU.mult, p, t_cp)
                else:
                    e = act(o, b[:, 0:128 * n], ACT.Identity, p, t_cp, scale=cp(g, k))
                banks.give(bk, e)
                done.append(e)
            return done

        def tile_t(w, wt, kt, c, rhs, n, toks):
            b, bt, bk = bank()
            for k in range(kt):
                p = mm(b[:, 0:n], w[:, k, c:c + 128], rhs[:, k, 0:n], k == 0, k == kt - 1, bt, wt, toks,
                       inc=(k == kt - 1))
            return b, p, bk

        def tile_r(w, wt, kt, lhs, i, toks):
            b, bt, bk = bank()
            for k in range(kt):
                p = mm(b, lhs[:, k, 128 * i:128 * i + 128], w[:, k, :], k == 0, k == kt - 1, bt, wt, toks,
                       inc=(k == kt - 1))
            return b, p, bk

        def rows_norm_add(parts, gt, tmp, tmp_free):
            done = []
            for i, halves in enumerate(parts):
                ss = col(4)
                o = tmp[:, i % 2, :]
                a = [act(o[:, 512 * h:512 * h + 512], b, ACT.Square, p, tmp_free[i % 2], accum_out=ss[:, h:h + 1])
                     for h, (b, p, bk) in enumerate(halves)]
                s = tt(ss[:, 2:3], ss[:, 0:1], ss[:, 1:2], ALU.add, a)
                r = rstd(ss[:, 2:3], 1, 1024, s)
                adds = []
                for h, (b, p, bk) in enumerate(halves):
                    m = stt(o[:, 512 * h:512 * h + 512], b, ss[:, 2:3], GB[:, 512 * h:512 * h + 512],
                            ALU.mult, ALU.mult, r, gt)
                    banks.give(bk, m)
                    adds.append(tt(X[:, i, 512 * h:512 * h + 512], X[:, i, 512 * h:512 * h + 512],
                                   o[:, 512 * h:512 * h + 512], ALU.add, m))
                tmp_free[i % 2] = adds
                done += adds
            return done

        f = Fo
        AT, QT, KT, QM = (cut(area(f + 2048 * i, 2048), 4) for i in range(4))
        VV = cut(area(f + 8192, 2048), 4)
        MK = cut(area(f + 10240, 1024), 4)
        MV = cut(area(f + 11264, 1024), 2)
        SK = cut(area(f + 12288, 1024), 2)
        PB = cut(area(f + 13312, 2560), 2)
        PTo = f + 15872
        GT = cut(area(f + 17920, 1024), 2)
        BV = area(f + 17920, 640)
        PT = cut(area(PTo, 2048), 4)
        MEMR = cut(area(f + 13312, 2048), 2)
        MEMN = cut(area(PTo, 2048), 2)
        MEMT = cut(area(MGo, 2048), 8)
        CCB = cut(area(MGo + 2048, 2048), 4)

        t_mem = [PO.dma(MEMR[:, i, :], dram["mem"][128 * i:128 * i + 128, :]) for i in range(2)]
        t_oh = PO.dma(GB[0:32, 0:512], dram["onehot"])
        t_rb = PO.dma(GB[0:32, 512:520], dram["rel_bias"])

        b, bt, bk = bank()
        p = mm(b[0:8, :], GB[0:32, 512:520], GB[0:32, 0:512], True, True, bt, t_oh, t_rb, inc=True)
        e1 = DV.do(lambda e: e.memset(BV[0:8, 512:640], NEG))
        e2 = cpy(BV[0:8, 0:512], b[0:8, :], p)
        banks.give(bk, e2)
        t_bv = PO.dma(dram["bvec"], BV[0:8, 0:640].unsqueeze(1).to_broadcast([8, 128, 640]), e1, e2)
        t_gb = PO.dma(GB, dram["gains"][0:1, :].to_broadcast([128, 1024]), p)

        t_ht = norm_t(X, 4, "g_pre_mix", HT, XN, t_x)
        t_mt = norm_t(MEMR, 2, "g_mem", MEMT, MEMN, [t_mem, PE.pending()])

        def proj_t(name, dst, rhs, n, toks, lanes=(AC, DV)):
            w, wt, wk = wload(name)
            w = cut(w, 8)
            out_ = []
            for j in range(4):
                b, p, bk = tile_t(w, wt, 8, 128 * j, rhs, n, toks)
                if lanes[j % 2] is AC:
                    e = act(dst[:, j, 0:n], b[:, 0:n], ACT.Copy, p)
                else:
                    e = cpy(dst[:, j, 0:n], b[:, 0:n], p)
                banks.give(bk, e)
                out_.append(e)
            wring.give(wk, p)
            return out_

        t_q = proj_t("q", QT, HT, 512, t_ht)
        t_k = proj_t("k", KT, HT, 512, t_ht)
        w, wt, wk = wload("v")
        t_v = []
        for i in range(4):
            b, p, bk = tile_r(cut(w, 8), wt, 8, HT, i, t_ht)
            e = act(VV[:, i, :], b, ACT.Copy, p)
            banks.give(bk, e)
            t_v.append(e)
        wring.give(wk, p)
        t_qm = proj_t("qm", QM, HT, 512, t_ht)
        t_mk = proj_t("mk", MK, MEMT, 256, t_mt)
        w, wt, wk = wload("mv")
        t_mv = []
        for i in range(2):
            b, p, bk = tile_r(cut(w, 8), wt, 8, MEMT, i, t_mt)
            e = act(MV[:, i, :], b, ACT.Copy, p)
            banks.give(bk, e)
            t_mv.append(e)
        wring.give(wk, p)
        mem_read = p

        t_o1 = []
        t_om = []
        pt_free = [[t_mt, PE.pending()]]
        p_free = [[t_mt, PE.pending()], [t_mt, PE.pending()]]

        def attention_1():
            sk_free = [[], []]
            for h in range(8):
                lo, t, s = 64 * (h % 2), h // 2, h % 2
                skew = bass.AP(dram["bvec"].tensor, h * 81920 + 127, [[639, 128], [1, 512]])
                t_sk = PO.dma(SK[:, s, :], skew, t_bv, sk_free[s])
                P = PB[:, s, :]
                at = [0, 128, 384, 768]
                nm, rs = col(4), col(4)
                last = []
                for i in range(4):
                    n = 128 * (i + 1)
                    b, bt, bk = bank()
                    p = mm(b[:, 0:n], QT[lo:lo + 64, t, 128 * i:128 * i + 128], KT[lo:lo + 64, t, 0:n], True, True,
                           bt, t_q, t_k, inc=True)
                    Pi = P[:, at[i]:at[i] + n]
                    a = stt(Pi, b[:, 0:n], 0.125, SK[:, s, 384 - 128 * i:512], ALU.mult, ALU.add, p, t_sk,
                            p_free[s])
                    banks.give(bk, a)
                    m = red(nm[:, i:i + 1], Pi, ALU.max, a, negate=True)
                    x = act(Pi, Pi, ACT.Exp, m, bias=nm[:, i:i + 1], accum_out=rs[:, i:i + 1])
                    last.append(x)
                sk_free[s] = [a]
                r = DV.do(lambda e, rs=rs: e.reciprocal(rs, rs), last)
                last = [ts1(P[:, at[i]:at[i] + 128 * (i + 1)], P[:, at[i]:at[i] + 128 * (i + 1)], rs[:, i:i + 1],
                            ALU.mult, r) for i in range(4)]
                yield
                ev = []
                for k in range(4):
                    b, bt, bk = bank()
                    for i in range(k, 4):
                        p = tr(b[:, 128 * i:128 * i + 128], P[:, at[i] + 128 * k:at[i] + 128 * k + 128], bt, last,
                               inc=(i == 3))
                    if k % 2:
                        e = cpy(PT[:, k, 128 * k:512], b[:, 128 * k:512], p, pt_free[0])
                    else:
                        e = act(PT[:, k, 128 * k:512], b[:, 128 * k:512], ACT.Copy, p, pt_free[0])
                    banks.give(bk, e)
                    ev.append(e)
                p_free[s] = [p]
                yield
                b, bt, bk = bank()
                for k in range(4):
                    p = mm(b[lo:lo + 64, 128 * k:512], VV[:, k, 64 * h:64 * h + 64], PT[:, k, 128 * k:512], k == 0,
                           k == 3, bt, ev[k], t_v, inc=(k == 3))
                pt_free[0] = [p]
                e = cpy(QT[lo:lo + 64, t, :], b[lo:lo + 64, :], p)
                banks.give(bk, e)
                t_o1.append(e)
                yield
            scale = 128.0 ** -0.5
            for h in range(4):
                P = cut(PB[:, h % 2, 0:1024], 4)
                nm, rs = col(4), col(4)
                last = []
                for q in range(2):
                    b, bt, bk = bank()
                    for i in range(2):
                        p = mm(b[:, 256 * i:256 * i + 256], QM[:, h, 256 * q + 128 * i:256 * q + 128 * i + 128],
                               MK[:, h, :], True, True, bt, t_qm, t_mk, inc=(i == 1))
                    m = red(nm[:, 2 * q:2 * q + 2], cut(b, 2), ALU.max, p, negate=True)
                    m = ts1(nm[:, 2 * q:2 * q + 2], nm[:, 2 * q:2 * q + 2], scale, ALU.mult, m)
                    for i in range(2):
                        x = act(P[:, 2 * q + i, :], b[:, 256 * i:256 * i + 256], ACT.Exp, m, p_free[h % 2],
                                bias=nm[:, 2 * q + i:2 * q + i + 1], scale=scale,
                                accum_out=rs[:, 2 * q + i:2 * q + i + 1])
                        last.append(x)
                    banks.give(bk, x)
                r = DV.do(lambda e, rs=rs: e.reciprocal(rs, rs), last)
                last = [ts1(P[:, i, :], P[:, i, :], rs[:, i:i + 1], ALU.mult, r) for i in range(4)]
                yield
                ev = []
                for k in range(2):
                    b, bt, bk = bank()
                    for i in range(4):
                        p = tr(b[:, 128 * i:128 * i + 128], P[:, i, 128 * k:128 * k + 128], bt, last, inc=(i == 3))
                    e = cpy(PT[:, k, :], b, p, pt_free[0]) if k else act(PT[:, k, :], b, ACT.Copy, p, pt_free[0])
                    banks.give(bk, e)
                    ev.append(e)
                p_free[h % 2] = [p]
                yield
                b, bt, bk = bank()
                for k in range(2):
                    p = mm(b, MV[:, k, 128 * h:128 * h + 128], PT[:, k, :], k == 0, k == 1, bt, ev, t_mv,
                           inc=(k == 1))
                pt_free[0] = [p]
                e = cpy(QM[:, h, :], b, p)
                banks.give(bk, e)
                t_om.append(e)
                yield

        mg_done = [[] for _ in range(8)]
        gt_free = [[t_bv], [t_bv]]
        gt_i = [0]

        def gated(k, bias, w, wt, c, y, first):
            b, p, bk = tile_t(w, wt, 8, c, HT, 512, t_ht_now)
            g = gt_i[0] % 2
            gt_i[0] += 1
            kw = {} if bias is None else {"bias": bias}
            a = act(GT[:, g, :], b, ACT.Sigmoid, p, gt_free[g], **kw)
            banks.give(bk, a)
            yield
            yb, yp, yk = y()
            if first:
                m = tt(MG[:, k, :], GT[:, g, :], yb, ALU.mult, a, yp, mg_done[k])
                banks.give(yk, m)
                gt_free[g] = [m]
            else:
                m = tt(GT[:, g, :], GT[:, g, :], yb, ALU.mult, a, yp)
                banks.give(yk, m)
                m = tt(MG[:, k, :], MG[:, k, :], GT[:, g, :], ALU.add, m, mg_done[k])
                gt_free[g] = [m]
            mg_done[k] = [m]
            return p, yp

        def branch_1(yname, gname, bi, src, toks, first):
            wy, wyt, wyk = wload(yname)
            wy = cut(wy, 4)
            for s in range(2):
                w, wt, wk = wload(f"{gname}{s}")
                w = cut(w, 8)
                for j in range(4):
                    k = 4 * s + j
                    p, yp = yield from gated(k, cp("b_gate", 8 * bi + k), w, wt, 128 * j,
                                             lambda: tile_t(wy, wyt, 4, 128 * k, src, 512, toks), first)
                    yield
                wring.give(wk, p)
            wring.give(wyk, yp)

        t_ht_now = t_ht
        u_done = [None] * 4
        a_done = [None] * 4

        def dense_1():
            tc = proj_t("cc", CCB, HT, 512, t_ht + [mem_read])
            yield
            w, wt, wk = wload("cv")
            for j in range(4):
                b, p, bk = tile_t(cut(w, 8), wt, 8, 128 * j, HT, 512, t_ht)
                m = tt(CCB[:, j, :], CCB[:, j, :], b, ALU.mult, p, tc)
                banks.give(bk, m)
                u_done[j] = m
                c = [cp("conv_mix", 4 * q + j) for q in range(3)]
                m = ts1(AT[:, j, :], CCB[:, j, :], c[2], ALU.mult, m, t_cp)
                m = stt(AT[:, j, 1:512], CCB[:, j, 0:511], c[1], AT[:, j, 1:512], ALU.mult, ALU.add, m)
                m = stt(AT[:, j, 2:512], CCB[:, j, 0:510], c[0], AT[:, j, 2:512], ALU.mult, ALU.add, m)
                a_done[j] = m
                yield
            wring.give(wk, p)
            w, wt, wk = wload("cb")
            for j in range(4):
                b, p, bk = tile_t(cut(w, 8), wt, 8, 128 * j, HT, 512, t_ht)
                m = tt(AT[:, j, :], AT[:, j, :], b, ALU.mult, p, a_done[j])
                banks.give(bk, m)
                a_done[j] = m
                yield
            wring.give(wk, p)
            for k in range(8):
                mg_done[k] = [mem_read, a_done[3], t_mt]
            yield from branch_1("yconv", "ga", 0, AT, a_done, True)

        zipped(attention_1(), dense_1(), 1, 1)
        for _ in branch_1("yattn", "gb", 1, QT, t_o1, False):
            pass
        for _ in branch_1("ymem", "gc", 2, QM, t_om, False):
            pass

        def out_rows(names, toks):
            ws = [wload(n) for n in names]
            parts = []
            for i in range(4):
                halves = []
                for w, wt, wk in ws:
                    halves.append(tile_r(cut(w, 8), wt, 8, MG, i, toks))
                parts.append(halves)
                if i == 3:
                    for (w, wt, wk), (b, p, bk) in zip(ws, halves):
                        wring.give(wk, p)
            return parts

        TMP = cut(area(Fo, 2048), 2)
        free = snap()
        t_x1 = rows_norm_add(out_rows(["out0", "out1"], mg_done), t_gb, TMP, [free, free])
        t_gb = PO.dma(GB, dram["gains"][1:2, :].to_broadcast([128, 1024]), t_x1)

        mg_read = snap()
        t_ht = norm_t(X, 4, "g_pre_ffn", HT, XN, [t_x1, mg_read])
        FT = cut(area(Fo + 2048, 11264), 22)
        YB = cut(area(Fo + 13312, 4096), 8)
        start = snap()
        y_free = [start] * 8
        yi = 0
        ft_done = [None] * 22
        for s in range(11):
            w, wt, wk = wload(f"up{s}")
            w = cut(w, 8)
            half_y = {}
            for j in range(4):
                tix = 2 * s + j % 2 + (22 if j >= 2 else 0)
                b, p, bk = tile_t(w, wt, 8, 128 * j, HT, 512, t_ht)
                y, yk = YB[:, yi % 8, :], yi % 8
                yi += 1
                a = act(y, b, ACT.Identity, p, y_free[yk], t_cp, bias=cp("ffn_b", tix), scale=cp("ffn_w", 88 + tix))
                m = stt(y[:, 1:512], b[:, 0:511], cp("ffn_w", 44 + tix), y[:, 1:512], ALU.mult, ALU.add, a)
                m = stt(y[:, 2:512], b[:, 0:510], cp("ffn_w", tix), y[:, 2:512], ALU.mult, ALU.add, m)
                banks.give(bk, m)
                if j < 2:
                    half_y[j] = (y, act(y, y, ACT.Gelu_apprx_tanh, m), yk)
                else:
                    ya, ta, ka = half_y[j - 2]
                    m = tt(FT[:, 2 * s + j - 2, :], ya, y, ALU.mult, m, ta, start)
                    y_free[yk] = y_free[ka] = [m]
                    ft_done[2 * s + j - 2] = m
            wring.give(wk, p)
        parts = [[bank() for _ in range(2)] for _ in range(4)]
        done_p = [[None, None] for _ in range(4)]
        for k in range(22):
            if k % 4 == 0:
                w, wt, wk = wload(f"down{k // 4}")
                w = cut(w, 4)
            for i in range(4):
                for hf in range(2):
                    b, bt, bk = parts[i][hf]
                    done_p[i][hf] = mm(b, FT[:, k, 128 * i:128 * i + 128], w[:, k % 4, 512 * hf:512 * hf + 512],
                                       k == 0, k == 21, bt, wt, ft_done[k], inc=(k == 21 or k % 4 == 3))
            if k % 4 == 3 or k == 21:
                wring.give(wk, done_p[3][1])
        parts = [[(parts[i][h][0], done_p[i][h], parts[i][h][2]) for h in range(2)] for i in range(4)]
        t_x2 = rows_norm_add(parts, t_gb, TMP, [start, start])

        t_ht = norm_t(X, 4, "norm1_g", HT, XN, [t_x2, snap()])
        t_ht_now = t_ht
        f = Fo
        DT, DA, ACU, EXA, DTE, CDE = (area(f + 128 * i, 128) for i in range(6))
        f += 768
        CB = area(f, 512)
        PV = area(f + 512, 512)
        BR = cut(area(f + 1024, 512), 4)
        XS = cut(area(f + 1536, 2048), 4)
        XD = cut(area(f + 3584, 2048), 4)
        XE = cut(area(f + 5632, 1024), 2)
        EB = cut(area(f + 6656, 2048), 2)
        T1 = cut(area(f + 8704, 1024), 2)
        ZB = cut(area(f + 9728, 1024), 2)
        T2 = area(f + 10752, 512)
        YT = cut(area(Fo + 16281, 8192), 16)
        SNG = cut(GB, 2)
        BT, CT = cut(area(MGo, 2048), 4), cut(area(MGo + 2048, 2048), 4)
        start = snap()
        dtv = cut(DT, 4)
        h32 = lambda name: rr(name).unsqueeze(1).to_broadcast([128, 4, 32])

        wdt = cut(WS[:, 0:256], 8)
        b, bt, bk = bank()
        for i in range(4):
            for k in range(8):
                p = mm(b[:, 32 * i:32 * i + 32], HT[:, k, 128 * i:128 * i + 128], wdt[:, k, :], k == 0, k == 7,
                       bt, t_ws, t_ht, inc=(i == 3 and k == 7))
        e = tt(dtv, cut(b[:, 0:128], 4), h32("dt_bias"), ALU.add, p, t_rr, start)
        banks.give(bk, e)
        a = act(DA, DT, ACT.Abs, e, start)
        a = act(DA, DA, ACT.Exp, a, scale=-1.0)
        a = act(DA, DA, ACT.Ln, a, bias=1.0)
        m = ts1(DT, DT, 0.0, ALU.max, a)
        m = tt(DT, DT, DA, ALU.add, m)
        t_dt = m
        na = col(32)
        a = act(na, rr("a_log"), ACT.Exp, t_rr)
        m = ts1(na, na, -1.0, ALU.mult, a)
        m = tt(cut(DA, 4), dtv, na.unsqueeze(1).to_broadcast([128, 4, 32]), ALU.mult, m, t_dt)
        t_da = m
        b, bt, bk = bank()
        p = mm(b[:, 0:128], cc("triu"), DA, True, True, bt, t_da, t_cc)
        p = mm(b[:, 128:256], cc("ones"), DA, True, True, inc=True)
        c1 = cpy(ACU, b[:, 0:128], p, start)
        c2 = tt(DTE, b[:, 128:256], ACU, ALU.subtract, c1, start)
        c3 = act(CDE, b[:, 128:256], ACT.Exp, c2, start)
        c4 = act(EXA, ACU, ACT.Exp, c1, start)
        c5 = act(DTE, DTE, ACT.Exp, c2)
        banks.give(bk, c3)
        t_acu, t_dec = c1, [c3, c4, c5]

        def conv_silu(b, p, tix, y, toks):
            a = act(y, b, ACT.Identity, p, toks, t_cp, bias=cp("conv_b", tix), scale=cp("conv_w", 72 + tix))
            m = a
            for q in range(1, 4):
                m = stt(y[:, q:512], b[:, 0:512 - q], cp("conv_w", 24 * (3 - q) + tix), y[:, q:512], ALU.mult,
                        ALU.add, m)
            return m, act(y, y, ACT.Silu, m)

        t_bt, t_ct = [], []
        for name, dst, base, out_ in (("bm", BT, 16, t_bt), ("cm", CT, 20, t_ct)):
            w, wt, wk = wload(name)
            for j in range(4):
                b, p, bk = tile_t(cut(w, 8), wt, 8, 128 * j, HT, 512, t_ht)
                m, s = conv_silu(b, p, base + j, dst[:, j, :], start)
                banks.give(bk, m)
                out_.append(s)
            wring.give(wk, p)

        b4 = lambda ap, c, g: ap[:, 32 * c + 8 * g:32 * c + 8 * g + 8].unsqueeze(2).to_broadcast([128, 8, 64])
        h8 = lambda ap: ap.rearrange("p (h d) -> p h d", h=8)
        triu = cc("triu")
        t1_free, xe_free, eb_free = [start, start], [start, start], [start, start]
        zb_free, sng_free = [start, start], [start, start]
        yt_done = []
        grp_free = start

        def xs_rows(j, y, s, free, out_):
            b, bt, bk = bank()
            for c in range(4):
                q = tr(b[:, 128 * c:128 * c + 128], y[:, 128 * c:128 * c + 128], bt, s, inc=(c == 3))
            eb_free[j % 2] = [q]
            e = cpy(XS[:, :, 128 * j:128 * j + 128], cut(b, 4), q, free)
            banks.give(bk, e)
            out_.append(e)

        def finish(g, c, t1, o1, t_z, t_sn):
            o1 = tt(t1, t1, ZB[:, c % 2, :], ALU.mult, t_z, o1)
            ss = col(1)
            a = act(ZB[:, c % 2, :], t1, ACT.Square, o1, accum_out=ss)
            zb_free[c % 2] = [a]
            r = rstd(ss, 1, 512, a)
            o1 = stt(t1, t1, ss, SNG[:, g % 2, :], ALU.mult, ALU.mult, r, t_sn, a)
            sng_free[g % 2] = [o1]
            b, bt, bk = bank()
            for j in range(4):
                q = tr(b[:, 128 * j:128 * j + 128], t1[:, 128 * j:128 * j + 128], bt, o1, inc=(j == 3))
            t1_free[c % 2] = [q]
            e = act(YT[:, 4 * g:4 * g + 4, 128 * c:128 * c + 128], cut(b, 4), ACT.Copy, q, start)
            banks.give(bk, e)
            yt_done.append(e)

        todo = None
        for g in range(4):
            t_sn = PO.dma(SNG[:, g % 2, :], dram["sng"][0:1, 512 * g:512 * g + 512].to_broadcast([128, 512]),
                          sng_free[g % 2])
            w, wt, wk = wload(f"xs{g}")
            t_xs = []
            held = None
            for j in range(4):
                b, p, bk = tile_t(cut(w, 8), wt, 8, 128 * j, HT, 512, t_ht)
                y = EB[:, j % 2, 0:512]
                m, s = conv_silu(b, p, 4 * g + j, y, eb_free[j % 2])
                banks.give(bk, m)
                if held:
                    xs_rows(*held)
                held = (j, y, s, grp_free, t_xs)
                if j == 0 and todo:
                    finish(*todo)
                    todo = None
            wring.give(wk, p)
            b, bt, bk = bank()
            for c in range(4):
                q = tr(b[:, 128 * c:128 * c + 128], BT[:, g, 128 * c:128 * c + 128], bt, t_bt, inc=(c == 3))
            t_br = act(BR, cut(b, 4), ACT.Copy, q, grp_free)
            banks.give(bk, t_br)
            b, bt, bk = bank()
            for c in range(4):
                q = mm(b[:, 128 * c:128 * c + 128], BT[:, g, 128 * c:128 * c + 128],
                       CT[:, g, 128 * c:128 * c + 128], True, True, bt, t_bt, t_ct, inc=(c == 3))
            t_cb = tt(cut(CB, 4), cut(b, 4), triu.unsqueeze(1).to_broadcast([128, 4, 128]), ALU.mult, q, grp_free)
            banks.give(bk, t_cb)
            w, wt, wk = wload(f"z{g}")
            t_pv = None
            for c in range(4):
                eb = EB[:, c % 2, :]
                t_m = []
                rows = []
                for hh in range(2):
                    b, bt, bk = bank()
                    for h in range(4):
                        o = 32 * c + 8 * g + 4 * hh + h
                        q = mm(b[:, 128 * h:128 * h + 128], DA[:, o:o + 1].to_broadcast([128, 128]), triu, True,
                               True, bt, t_da, inc=(h == 3))
                    rows.append((b, q, bk))
                if held:
                    xs_rows(*held)
                    held = None
                    t_xd = [tt(h8(XD[:, n, :]), h8(XS[:, n, :]), b4(DT, n, g), ALU.mult, t_xs, t_dt, grp_free)
                            for n in range(4)]
                for hh, (b, q, bk) in enumerate(rows):
                    for h in range(4):
                        o = 32 * c + 8 * g + 4 * hh + h
                        m = ts(eb[:, 512 * hh + 128 * h:512 * hh + 128 * h + 128], b[:, 128 * h:128 * h + 128],
                               ACU[:, o:o + 1], 0.0, ALU.subtract, ALU.min, q, t_acu, eb_free[c % 2])
                    banks.give(bk, m)
                    eh = eb[:, 512 * hh:512 * hh + 512]
                    a = act(eh, eh, ACT.Exp, m)
                    t_m.append((eh, a))
                if c < 3:
                    t_xe = tt(h8(XE[:, c % 2, :]), h8(XD[:, c, :]), b4(DTE, c, g), ALU.mult, t_xd, t_dec,
                              xe_free[c % 2])
                t_m = [tt(cut(eh, 4), cut(eh, 4), CB[:, 128 * c:128 * c + 128].unsqueeze(1)
                          .to_broadcast([128, 4, 128]), ALU.mult, a, t_cb) for eh, a in t_m]
                zb, zp, zk = tile_r(cut(w, 8), wt, 8, HT, c, t_ht)
                t_z = act(ZB[:, c % 2, :], zb, ACT.Silu, zp, zb_free[c % 2])
                banks.give(zk, t_z)
                if todo:
                    finish(*todo)
                t1 = T1[:, c % 2, :]
                if c:
                    b, bt, bk = bank()
                    q = mm(b, CT[:, g, 128 * c:128 * c + 128], PV, True, True, bt, t_pv, t_ct, inc=True)
                    off_read = q
                    o1 = tt(h8(t1), h8(b), b4(EXA, c, g), ALU.mult, q, t_dec, t1_free[c % 2])
                    banks.give(bk, o1)
                t_cs = None
                if c < 3:
                    bs, bst, bsk = bank()
                    t_cs = mm(bs, BR[:, c, :], XE[:, c % 2, :], True, True, bst, t_br, t_xe, inc=True)
                    xe_free[c % 2] = [t_cs]
                b, bt, bk = bank()
                for h in range(8):
                    q = mm(b[:, 64 * h:64 * h + 64], eb[:, 128 * h:128 * h + 128], XD[:, c, 64 * h:64 * h + 64],
                           True, True, bt, t_m, t_xd, inc=(h == 7))
                eb_free[c % 2] = [q]
                if c < 3:
                    if c == 0:
                        t_pv = cpy(PV, bs, t_cs, grp_free)
                    else:
                        m = tt(h8(PV), h8(PV), b4(CDE, c, g), ALU.mult, t_pv, off_read, t_dec)
                        t_pv = tt(PV, PV, bs, ALU.add, m, t_cs)
                    banks.give(bsk, t_pv)
                if c:
                    o1 = tt(t1, t1, b, ALU.add, q, o1)
                else:
                    o1 = cpy(t1, b, q, t1_free[0])
                banks.give(bk, o1)
                d8 = rr("d_skip")[:, 8 * g:8 * g + 8].unsqueeze(2).to_broadcast([128, 8, 64])
                m = tt(h8(T2), h8(XS[:, c, :]), d8, ALU.mult, t_xs, t_rr, start, lane=DV)
                o1 = tt(t1, t1, T2, ALU.add, m, o1)
                todo = (g, c, t1, o1, t_z, t_sn)
            wring.give(wk, zp)
            grp_free = snap()
        finish(*todo)

        start = snap()
        f = Fo
        QKf = cut(area(f, 5120), 4)
        QK = area(f, 5120).rearrange("p (i h d) -> p i h d", i=4, h=20)
        OT = cut(area(f, 4096), 8)
        QT = cut(area(f + 5120, 4096), 8)
        KT = cut(area(f + 9216, 1024), 2)
        VV = cut(area(f + 10240, 1024), 4)
        LB = cut(area(f + 11264, 1792), 2)
        PTT = cut(area(f + 13056, 1792), 2)
        MKo = area(f + 14848, 896)
        COS, SIN, R1, R2 = (area(f + 15744 + 32 * i, 32) for i in range(4))
        TA, TB, TC = (area(f + 13056 + 160 * i, 160) for i in range(3))
        SQ = area(f + 11264, 1280)
        GT = SNG
        gt_free[0] = gt_free[1] = start
        mg_done = [[start] for _ in range(8)]
        t_mk2 = PO.dma(MKo, dram["mask2"], start)
        t_ps = PO.dma(IA[:, 0:4], dram["pos"])

        pf = col(4)
        m = cpy(pf, IA[:, 0:4], t_ps)
        v48 = lambda ap: ap.rearrange("p (i d) -> p i d", i=4)
        m = tt(v48(R1), pf.unsqueeze(2).to_broadcast([128, 4, 8]), cc("invf").unsqueeze(1).to_broadcast([128, 4, 8]),
               ALU.mult, m, start)
        m = ts(R2, R1, 1.0 / (2 * math.pi), 12582912.0, ALU.mult, ALU.add, m)
        m = ts1(R2, R2, 12582912.0, ALU.subtract, m)
        c1 = 6.28125
        c2 = 0.0019350051879882812
        c3 = 2 * math.pi - c1 - c2
        for c in (c1, c2, c3):
            m = stt(R1, R2, -c, R1, ALU.mult, ALU.add, m)
        m = ts(R1, R1, math.pi - 1e-6, -math.pi + 1e-6, ALU.min, ALU.max, m)
        a = act(SIN, R1, ACT.Sin, m)
        a = act(COS, R1, ACT.Sin, a, scale=0.5)
        m = tt(COS, COS, COS, ALU.mult, a)
        t_cs = ts(COS, COS, -2.0, 1.0, ALU.mult, ALU.add, m)

        t_qk = []
        t_v = []
        for s, name in enumerate(("q0", "q1", "kv")):
            w, wt, wk = wload(name)
            for i in range(4):
                b, p, bk = tile_r(cut(w, 8), wt, 8, HT, i, t_ht)
                if s < 2:
                    e = act(QKf[:, i, 512 * s:512 * s + 512], b, ACT.Copy, p, start)
                else:
                    e = cpy(QKf[:, i, 1024:1280], b[:, 0:256], p, start)
                    t_v.append(cpy(VV[:, i, :], b[:, 256:512], p, start))
                    e = t_v[-1]
                banks.give(bk, e)
                t_qk.append(e)
            wring.give(wk, p)

        def dense_2():
            for s in range(2):
                wg, wgt, wgk = wload(f"gs{s}")
                for u in range(2):
                    wy, wyt, wyk = wload(f"so{2 * s + u}")
                    wy = cut(wy, 16)
                    for j in range(2):
                        k = 4 * s + 2 * u + j
                        p, yp = yield from gated(k, None, cut(wg, 8), wgt, 128 * (2 * u + j),
                                                 lambda: tile_t(wy, wyt, 16, 128 * j, YT, 512, yt_done), True)
                        yield
                    wring.give(wyk, yp)
                wring.give(wgk, p)

        def attention_2():
            sq_done = start
            qn = []
            for i in range(4):
                a = act(SQ, QKf[:, i, :], ACT.Square, t_qk, sq_done)
                ss = col(20)
                m = red(ss, SQ.rearrange("p (h d) -> p h d", h=20), ALU.add, a)
                sq_done = [m]
                r = rstd(ss, 20, 64, m)
                m = tt(QK[:, i, :, :], QK[:, i, :, :], ss.unsqueeze(2).to_broadcast([128, 20, 64]), ALU.mult, r)
                m = tt(QK[:, i, 0:16, :], QK[:, i, 0:16, :], rr("q_g").unsqueeze(1).to_broadcast([128, 16, 64]),
                       ALU.mult, m)
                m = tt(QK[:, i, 16:20, :], QK[:, i, 16:20, :], rr("k_g").unsqueeze(1).to_broadcast([128, 4, 64]),
                       ALU.mult, m)
                va, vb, vc = (x.rearrange("p (h d) -> p h d", h=20) for x in (TA, TB, TC))
                ci = COS[:, 8 * i:8 * i + 8].unsqueeze(1).to_broadcast([128, 20, 8])
                si = SIN[:, 8 * i:8 * i + 8].unsqueeze(1).to_broadcast([128, 20, 8])
                q1, q2 = QK[:, i, :, 0:8], QK[:, i, :, 8:16]
                a1 = tt(va, q2, si, ALU.mult, m, t_cs, start)
                a2 = tt(vb, q1, si, ALU.mult, m, start)
                a3 = tt(vc, q2, ci, ALU.mult, m, start)
                a4 = tt(q1, q1, ci, ALU.mult, a2)
                a5 = tt(q1, q1, va, ALU.subtract, a4, a1)
                m = tt(q2, vb, vc, ALU.add, a3, a2)
                qn.append([a5, m])
                yield
            t_qt = []
            for t in (8, 0, 1, 2, 3, 9, 4, 5, 6, 7):
                b, bt, bk = bank()
                for i in range(4):
                    p = tr(b[:, 128 * i:128 * i + 128], QKf[:, i, 128 * t:128 * t + 128], bt, qn[i], inc=(i == 3))
                dst = QT[:, t, :] if t < 8 else KT[:, t - 8, :]
                e = cpy(dst, b, p, start) if t % 2 else act(dst, b, ACT.Copy, p, start)
                banks.give(bk, e)
                t_qt.append(e)
            qk_read = p
            l_free, pt_free2 = [qn, qn], [qn, qn]
            m3 = lambda ap: ap.rearrange("p (n k) -> p n k", k=256)

            def scores(pos):
                t, lo, kp, s = pos // 2, 64 * (pos % 2), pos // 8, pos % 2
                L = LB[:, s, :]
                nm, rs = col(4), col(4)
                scored = []
                for half_ in range(2):
                    b, bt, bk = bank()
                    o = 0
                    for n in ((0, 1), (2, 3))[half_]:
                        w_ = 128 if n == 0 else 256
                        k0 = 0 if n == 0 else 128 * (n - 1)
                        p = mm(b[:, o:o + w_], QT[lo:lo + 64, t, 128 * n:128 * n + 128],
                               KT[lo:lo + 64, kp, k0:k0 + w_], True, True, bt, t_qt, inc=(n % 2 == 1))
                        o += w_
                    lo_, hi_ = (0, 384) if half_ == 0 else (384, 896)
                    a = stt(L[:, lo_:hi_], b[:, 0:hi_ - lo_], 0.125, MKo[:, lo_:hi_], ALU.mult, ALU.add, p, t_mk2,
                            l_free[s])
                    banks.give(bk, a)
                    scored.append(a)
                m1 = red(nm[:, 0:1], L[:, 0:128], ALU.max, scored)
                m2 = red(nm[:, 1:4], m3(L[:, 128:896]), ALU.max, scored)
                m = ts(nm, nm, rr("sinks")[:, pos:pos + 1], -1.0, ALU.max, ALU.mult, m1, m2, t_rr)
                xs = []
                for n in range(4):
                    lo_, hi_ = (0, 128) if n == 0 else (128 + 256 * (n - 1), 128 + 256 * n)
                    xs.append(act(L[:, lo_:hi_], L[:, lo_:hi_], ACT.Exp, m, bias=nm[:, n:n + 1],
                                  accum_out=rs[:, n:n + 1]))
                xs.append(act(nm, nm, ACT.Exp, m, xs, bias=rr("sinks")[:, pos:pos + 1]))
                m = tt(rs, rs, nm, ALU.add, xs)
                m = DV.do(lambda e, rs=rs: e.reciprocal(rs, rs), m)
                d1 = ts1(L[:, 0:128], L[:, 0:128], rs[:, 0:1], ALU.mult, m)
                d2 = tt(m3(L[:, 128:896]), m3(L[:, 128:896]), rs[:, 1:4].unsqueeze(2).to_broadcast([128, 3, 256]),
                        ALU.mult, m, lane=PO)
                return [d1, d2]

            def values(pos, ready):
                t, lo, kp, s = pos // 2, 64 * (pos % 2), pos // 8, pos % 2
                kv = 2 * kp + pos % 2
                L = LB[:, s, :]
                ev = []
                for half_ in range(2):
                    b, bt, bk = bank()
                    lo_, n_ = (0, 3) if half_ == 0 else (384, 4)
                    for u in range(n_):
                        p = tr(b[:, 128 * u:128 * u + 128], L[:, lo_ + 128 * u:lo_ + 128 * u + 128], bt, ready,
                               inc=(u == n_ - 1))
                    e = act(PTT[:, s, lo_:lo_ + 128 * n_], b[:, 0:128 * n_], ACT.Copy, p, pt_free2[s])
                    banks.give(bk, e)
                    ev.append(e)
                l_free[s] = [p]
                yield
                b, bt, bk = bank()
                for n in range(4):
                    srcs = [(0, 0)] if n == 0 else [(n - 1, 128 + 256 * (n - 1)), (n, 256 + 256 * (n - 1))]
                    for u, (kb, o) in enumerate(srcs):
                        p = mm(b[lo:lo + 64, 128 * n:128 * n + 128], VV[:, kb, 64 * kv:64 * kv + 64],
                               PTT[:, s, o:o + 128], u == 0, u == len(srcs) - 1, bt, ev, t_v, inc=(n == 3))
                pt_free2[s] = [p]
                e = cpy(OT[lo:lo + 64, t, :], b[lo:lo + 64, :], p, qk_read)
                banks.give(bk, e)
                t_o2.append(e)

            ready = scores(0)
            yield
            for pos in range(16):
                nxt = scores(pos + 1) if pos < 15 else None
                yield from values(pos, ready)
                ready = nxt

        t_o2 = []
        zipped(dense_2(), attention_2(), 1, 2)
        for s in range(2):
            wg, wgt, wgk = wload(f"gt{s}")
            wy, wyt, wyk = wload(f"ao{s}")
            for j in range(4):
                step = gated(4 * s + j, None, cut(wg, 8), wgt, 128 * j,
                             lambda: tile_t(cut(wy, 8), wyt, 8, 128 * j, OT, 512, t_o2), False)
                while True:
                    try:
                        next(step)
                    except StopIteration as end:
                        p, yp = end.value
                        break
            wring.give(wgk, p)
            wring.give(wyk, yp)
        t_gb = PO.dma(GB, dram["gains"][2:3, :].to_broadcast([128, 1024]), snap())
        parts = out_rows(["oo0", "oo1"], mg_done)
        t_x3 = []
        for i, halves in enumerate(parts):
            for h, (b, p, bk) in enumerate(halves):
                m = tt(X[:, i, 512 * h:512 * h + 512], X[:, i, 512 * h:512 * h + 512], b, ALU.add, p)
                banks.give(bk, m)
                t_x3.append(m)

        start = snap()
        GUs = [WRo + 4096 * k for k in range(5)] + [HTo]
        DNs = [WRo + 20480 + 2048 * k for k in range(6)]
        XB = cut(area(MGo, 2048), 2)
        XT = cut(area(MGo + 2048, 2048), 2)
        f = WRo + 32768
        HS, HD, YE = cut(area(f, 512), 2), cut(area(f + 512, 512), 2), cut(area(f + 1024, 2048), 2)
        gur, dnr = Ring(6), Ring(6)
        gur.free = [[start] for _ in range(5)] + [None]
        dnr.free = [[start] for _ in range(6)]
        wexp = dram["wexp"]

        def eload(ring, places, width, lo, n):
            k, toks = ring.take()
            w = AR[:, places[k]:places[k] + width]
            return w, SP.dma(w, wexp[n, :, lo:lo + width], toks), k

        n_pre = 5
        pre = [(eload(gur, GUs, 4096, 0, n), eload(dnr, DNs, 2048, 4096, n)) for n in range(n_pre)]
        t_h2 = []
        ss = col(4)
        a = [act(XN[:, i, :], X[:, i, :], ACT.Square, t_x3, start, accum_out=ss[:, i:i + 1]) for i in range(4)]
        r = rstd(ss, 4, 1024, a)
        for i in range(4):
            m = stt(XN[:, i, :], X[:, i, :], ss[:, i:i + 1], GB, ALU.mult, ALU.mult, r, t_gb)
            t_h2.append(m)
        t_h2d = [PO.dma(dram["h2d"][128 * i:128 * i + 128, :], XN[:, i, :], t_h2[i]) for i in range(4)]
        t_ht = []
        for k in range(8):
            b, bt, bk = bank()
            for i in range(4):
                p = tr(b[:, 128 * i:128 * i + 128], XN[:, i, 128 * k:128 * k + 128], bt, t_h2[i], inc=(i == 3))
            e = act(HT[:, k, :], b, ACT.Copy, p, start) if k % 2 else cpy(HT[:, k, :], b, p, start)
            banks.give(bk, e)
            t_ht.append(e)
        wr = cut(WS[:, 256:832], 8)
        RL = cut(area(f, 288), 4)
        b, bt, bk = bank()
        for i in range(4):
            for k in range(8):
                p = mm(b[:, 72 * i:72 * i + 72], HT[:, k, 128 * i:128 * i + 128], wr[:, k, :], k == 0, k == 7, bt,
                       t_ht, t_ws, inc=(i == 3 and k == 7))
        m = tt(RL, cut(b[:, 0:288], 4), rr("b_r").unsqueeze(1).to_broadcast([128, 4, 72]), ALU.add, p, t_rr, start)
        banks.give(bk, m)
        f += 288
        GL = RL[:, :, 0:8]
        OG, VG = (area(f + 32 * i, 32).rearrange("p (i g) -> p i g", i=4) for i in range(2))
        f += 64
        EL, O1, O2, V1 = (area(f + 256 * i, 256).rearrange("p (i g) -> p i g", i=4) for i in range(4))
        f += 1024
        bc = lambda ap, n: ap.unsqueeze(2).to_broadcast([128, 4, n])
        row = lambda ap, n: ap.unsqueeze(1).to_broadcast([128, 4, n])
        gm, gs, v1, v2, ix = col(4), col(4), col(4), col(4), col(4)
        m = red(gm, GL, ALU.max, m)
        m2 = tt(VG, GL, bc(gm, 8), ALU.subtract, m, start)
        a = act(VG, VG, ACT.Exp, m2)
        m2 = red(gs, VG, ALU.add, a)
        m2 = DV.do(lambda e: e.reciprocal(gs, gs), m2)

        def first(oh, vals, mx, rev, n, *toks):
            m = tt(oh, vals, bc(mx, n), ALU.is_equal, *toks)
            m = tt(oh, oh, row(rev, n), ALU.mult, m, t_cc)
            m = red(ix, oh, ALU.max, m)
            return tt(oh, oh, bc(ix, n), ALU.is_equal, m)

        m = first(OG, GL, gm, cc("rev8"), 8, m, start)
        m = ts(VG, OG, -1.0, 1e30, ALU.add, ALU.mult, m, m2)
        el4 = lambda ap: ap.rearrange("p i (g e) -> p i g e", g=8)
        for i in range(4):
            mi = tt(el4(EL)[:, i], RL[:, i, 8:72].rearrange("p (g e) -> p g e", g=8),
                    VG[:, i, :].unsqueeze(2).to_broadcast([128, 8, 8]), ALU.add, m, start)
        m = red(v1, EL, ALU.max, mi)
        m = first(O1, EL, v1, cc("rev64"), 64, m, start)
        m = ts1(V1, O1, -2e30, ALU.mult, m, start)
        m = tt(V1, EL, V1, ALU.add, m)
        m = red(v2, V1, ALU.max, m)
        m = first(O2, V1, v2, cc("rev64"), 64, m, start)
        t_oh2 = m
        m = tt(v2, v2, v1, ALU.subtract, m)
        a = act(v2, v2, ACT.Exp, m)
        m = ts1(v1, v2, 1.0, ALU.add, a)
        m = DV.do(lambda e: e.reciprocal(v1, v1), m)
        m = tt(v1, v1, gs, ALU.mult, m, m2)
        t_gate = tt(v2, v2, v1, ALU.mult, m)
        m = tt(V1, O1, O2, ALU.add, t_oh2)
        b, bt, bk = bank()
        for i in range(4):
            for u in range(i + 1):
                p = mm(b[:, 64 * i:64 * i + 64], cc("stri") if u == i else cc("ones"), V1[:, u, :], u == 0, u == i,
                       bt, m, t_cc)
        for u in range(4):
            p = mm(b[:, 256:320], cc("ones"), V1[:, u, :], u == 0, u == 3, inc=(u == 3))
        PO_ = EL
        c1 = cpy(PO_, b[:, 0:256].rearrange("p (i e) -> p i e", i=4), p)
        CNT, NB, CA, CB2 = (area(f + 64 * i, 64) for i in range(4))
        f += 256
        m = ts(CNT, b[:, 256:320], -float(CAP), 0.0, ALU.add, ALU.max, p, start)
        banks.give(bk, m)
        m = ts1(NB, CNT, 0.5, ALU.is_gt, m)
        for q in range(1, 4):
            m = ts1(CA, CNT, 128.0 * q + 0.5, ALU.is_gt, m)
            m = tt(NB, NB, CA, ALU.add, m)
        m = cpy(CA, NB, m)
        a_, b_ = CA, CB2
        for q in range(6):
            st = 1 << q
            m1 = cpy(b_[:, 0:st], a_[:, 0:st], m)
            m = tt(b_[:, st:64], a_[:, st:64], a_[:, 0:64 - st], ALU.add, m1)
            a_, b_ = b_, a_
        incl = a_
        BEF = area(HTo, 31 * 64).rearrange("p (b e) -> p b e", b=31)
        bef = col(31)
        q1 = DV.do(lambda e: e.tensor_tensor(BEF, incl.unsqueeze(1).to_broadcast([128, 31, 64]),
                                             cc("iob").unsqueeze(2).to_broadcast([128, 31, 64]), ALU.is_le), m, start)
        q1 = red(bef, BEF, ALU.add, q1)
        q1 = ts1(bef, bef, 63.0, ALU.min, q1)
        t_be = cpy(IA[:, 64:95], bef, q1)
        t_be = cpy(IA[:, 95:96], incl[:, 63:64], t_be)
        m = tt(NB, incl, NB, ALU.subtract, m)
        m = ts(NB, NB, 128.0, float(NST - CAP), ALU.mult, ALU.add, m)
        S1, S2 = (area(f + 256 * i, 256).rearrange("p (i g) -> p i g", i=4) for i in range(2))
        f += 512
        m1 = tt(S1, PO_, row(cc("e32"), 64), ALU.add, c1, start)
        m2 = tt(S2, PO_, row(NB, 64), ALU.add, m, c1, start)
        m1 = tt(S1, S1, S2, ALU.subtract, m1, m2)
        m2 = ts1(PO_, PO_, CAP - 0.5, ALU.is_lt, m1)
        m1 = tt(S1, S1, PO_, ALU.mult, m2)
        m1 = tt(S1, S1, S2, ALU.add, m1)
        sl = col(8)
        for j, oh in enumerate((O1, O2)):
            m = tt(S2, S1, oh, ALU.mult, m1)
            m1 = red(sl[:, 4 * j:4 * j + 4], S2, ALU.add, m)
        t_sl = cpy(IA[:, 8:16], sl, m1)

        z = PO.do(lambda e: e.memset(IA[:, 16:63], 4096))
        t_z = PO.dma(dram["tab"].rearrange("(p c) o -> p (c o)", p=128), IA[:, 16:63], z)
        t_tk = PO.dma(IA[:, 96:104], dram["tokid"])
        t_sc = []
        for j in range(2):
            for i in range(4):
                idx, val = IA[:, 8 + 4 * j + i:9 + 4 * j + i], IA[:, 96 + 4 * j + i:97 + 4 * j + i]
                t_sc.append(PO.dma(None, None, t_z, t_tk, t_sl, how=lambda e, idx=idx, val=val: e.indirect_dma_start(
                    dram["tab"], bass.IndirectOffsetOnAxis(ap=idx, axis=0), val, None, bounds_check=NSLOT - 1,
                    oob_is_err=False)))
        t_tab = PO.dma(IA[:, 16:63], dram["tab"].rearrange("(b p) o -> p (b o)", p=128), t_sc)
        m = DV.do(lambda e: e.tensor_scalar(IA[:, 128:175], IA[:, 16:63], 1, None, ALU.logical_shift_right), t_tab)
        t_tok = ts1(IA[:, 128:175], IA[:, 128:175], 511.0, ALU.min, m)

        after = snap()
        gur.free[5] = [after]

        def expert(wid, gus, dns, xb, t_xb, fr, xt, hs, hd, ye):
            ne = len(gus)
            ev = []
            for hf in range(2):
                b, bt, bk = bank()
                for k in range(4):
                    p = tr(b[:, 128 * k:128 * k + 128], xb[:, 512 * hf + 128 * k:512 * hf + 128 * k + 128], bt, t_xb,
                           inc=(k == 3))
                o = xt[:, 4 * hf:4 * hf + 4, :]
                e = act(o, cut(b, 4), ACT.Copy, p, fr["xt"]) if hf else cpy(o, cut(b, 4), p, fr["xt"])
                banks.give(bk, e)
                ev.append(e)
            fr["xb"] = [p]
            b, bt, bk = bank()
            t_gu, t_dn = [], []
            pairs = [range(ne)[j:j + 2] for j in range(0, ne, 2)]
            for pair in pairs:
                for k in range(8):
                    for j in pair:
                        w = cut(gus[j][0], 8)
                        p = mm(b[wid * j:wid * j + wid, :], xt[:, k, wid * j:wid * j + wid], w[:, k, :], k == 0,
                               k == 7, bt, ev, gus[j][1], inc=(k == 7 and j == pair[-1]))
                t_gu += [p] * len(pair)
            fr["xt"] = [p]
            a = act(hs, b[:, 0:256], ACT.Silu, p, fr["hs"])
            m = tt(hs, hs, b[:, 256:512], ALU.mult, a)
            banks.give(bk, m)
            b, bt, bk = bank()
            for q in range(2):
                p = tr(b[:, 128 * q:128 * q + 128], hs[:, 128 * q:128 * q + 128], bt, m, inc=(q == 1))
            fr["hs"] = [p]
            e = cpy(hd, cut(b[:, 0:256], 2), p, fr["hd"])
            banks.give(bk, e)
            ys = []
            b2 = [bank() for _ in range(2)]
            for pair in pairs:
                for hf in range(2):
                    b, bt, bk = b2[hf]
                    for q in range(2):
                        for j in pair:
                            w = cut(dns[j][0], 2)
                            p = mm(b[wid * j:wid * j + wid, :], hd[:, q, wid * j:wid * j + wid],
                                   w[:, q, 512 * hf:512 * hf + 512], q == 0, q == 1, bt, e, dns[j][1],
                                   inc=(q == 1 and j == pair[-1]))
                t_dn += [p] * len(pair)
            for hf in range(2):
                b, bt, bk = b2[hf]
                o = ye[:, 512 * hf:512 * hf + 512]
                y = act(o, b, ACT.Copy, p, fr["ye"]) if hf else cpy(o, b, p, fr["ye"])
                banks.give(bk, y)
                ys.append(y)
            fr["hd"] = [p]
            return t_gu, t_dn, ys

        t_ya = []
        frs = [{n: after for n in ("xb", "xt", "hs", "hd", "ye")} for _ in range(2)]

        def gather(blk):
            xb, tok = XB[:, blk % 2, :], IA[:, 128 + blk:129 + blk]
            return PO.dma(None, None, t_h2d, t_tok, frs[blk % 2]["xb"], how=lambda e: e.indirect_dma_start(
                xb, None, dram["h2d"], bass.IndirectOffsetOnAxis(ap=tok, axis=0), bounds_check=511,
                oob_is_err=False))

        t_g = gather(0)
        for blk in range(16):
            s = blk % 2
            fr = frs[s]
            gu, dn = [], []
            for j in range(4):
                n = 4 * blk + j
                if n < n_pre:
                    gu.append(pre[n][0])
                    dn.append(pre[n][1])
                else:
                    gu.append(eload(gur, GUs, 4096, 0, n))
                    dn.append(eload(dnr, DNs, 2048, 4096, n))
            t_now, t_g = t_g, gather(blk + 1) if blk < 15 else None
            t_gu, t_dn, ys = expert(CAP, gu, dn, XB[:, s, :], t_now, fr, cut(XT[:, s, :], 8), HS[:, s, :],
                                    cut(HD[:, s, :], 2), YE[:, s, :])
            for j in range(4):
                gur.give(gu[j][2], t_gu[j])
                dnr.give(dn[j][2], t_dn[j])
            asg = IA[:, 16 + blk:17 + blk]
            t_y = PO.dma(None, None, ys, t_tab, how=lambda e, s=s, asg=asg: e.indirect_dma_start(
                dram["ya"], bass.IndirectOffsetOnAxis(ap=asg, axis=0), YE[:, s, :], None, bounds_check=1023,
                oob_is_err=False))
            fr["ye"] = [t_y]
            t_ya.append(t_y)

        outer = (PE, DV, AC, PO, SP)
        oend = [snap()]
        inner = tuple(Body(sem("l_" + n), [sem(f"l_{n}{i}") for i in range(k)])
                      for n, k in (("pe", 0), ("dve", 0), ("act", 0), ("pool", 2), ("sp", 2)))
        gain = {}
        for lane in inner:
            lane.gain, lane.rest = gain, None
        inner[3].rest, inner[4].rest = sem("rest_pool"), sem("rest_sp")
        PE, DV, AC, PO, SP = inner
        banks_outer, banks = banks, Ring(8)

        def dyn_idx(e, i):
            return e.tensor_copy(IA[:, 112:113], IA[:, bass.ds(i + 32, 1)])

        def dyn_tok(e, i):
            return e.tensor_copy(IA[:, 113:114], IA[:, bass.ds(i + 144, 1)])

        def load_w(e, i, w, lo, width):
            x = e.value_load(IA[0:1, bass.ds(i + 64, 1)], min_val=0, max_val=63)
            return e.dma_start(w, wexp[bass.ds(x, 1), :, lo:lo + width].rearrange("a p c -> (a p) c"))

        DV.n += 2
        DV.ops.append(lambda e, i: dyn_idx(e, i).then_inc(DVi.sem, 1))
        DV.ops.append(lambda e, i: dyn_tok(e, i).then_inc(DVi.sem, 1))
        DVi = DV
        t_ix = (DV.sem, 2)
        gw, dw = AR[:, GUs[0]:GUs[0] + 4096], AR[:, DNs[0]:DNs[0] + 2048]
        t_w1 = SP.dma(None, None, how=lambda e, i: load_w(e, i, gw, 0, 4096))
        t_w2 = SP.dma(None, None, how=lambda e, i: load_w(e, i, dw, 4096, 2048))
        t_g = PO.dma(None, None, t_ix, how=lambda e, i: e.indirect_dma_start(
            XB[:, 0, :], None, dram["h2d"], bass.IndirectOffsetOnAxis(ap=IA[:, 113:114], axis=0), bounds_check=511,
            oob_is_err=False))
        fr = {n: [] for n in ("xb", "xt", "hs", "hd", "ye")}
        t_gu, t_dn, ys = expert(128, [(gw, t_w1, 0)], [(dw, t_w2, 0)], XB[:, 0, :], t_g, fr,
                                cut(XT[:, 0, :], 8), HS[:, 0, :], cut(HD[:, 0, :], 2), YE[:, 0, :])
        t_last = PO.dma(None, None, ys, how=lambda e, i: e.indirect_dma_start(
            dram["ya"], bass.IndirectOffsetOnAxis(ap=IA[:, 112:113], axis=0), YE[:, 0, :], None, bounds_check=1023,
            oob_is_err=False))
        for lane in inner:
            if lane.n:
                gain[id(lane.sem)] = lane.n
            for q in lane.dma_sems:
                gain[id(q)] = 16
        ends = [(lane.sem, lane.n) for lane in inner if lane.n] + [(q, 16) for lane in inner for q in lane.dma_sems]
        PE, DV, AC, PO, SP = outer
        banks = banks_outer

        def loop_of(body):
            def run(e):
                n = e.value_load(IA[0:1, 95:96], min_val=0, max_val=NOV)
                with e.If(n > 0):
                    for t in oend[0]:
                        e.wait_ge(*t)
                    with e.Fori(0, n) as i:
                        for op in body.ops:
                            op(e, i)
                        for q, v in ends:
                            body.until(e, q, i * v + v)
            return run

        for lane, body in zip(outer, inner):
            lane.wait(t_be, t_tok)
            lane.ops.append(loop_of(body))

        YC = [AR[:, o:o + 2048].rearrange("p (j d) -> p j d", j=2) for o in GUs[0:4]]
        ya = dram["ya"].rearrange("(t j) d -> t j d", j=2)
        for i in range(4):
            t_c = PO.dma(YC[i], ya[128 * i:128 * i + 128], oend[0], t_ya)
            m = stt(X[:, i, :], YC[i][:, 0, :], v1[:, i:i + 1], X[:, i, :], ALU.mult, ALU.add, t_c, t_gate)
            m = stt(X[:, i, :], YC[i][:, 1, :], v2[:, i:i + 1], X[:, i, :], ALU.mult, ALU.add, m)
            SP.dma(out[128 * i:128 * i + 128, :], X[:, i, :], m)
        for lane in (SP, AC, PO):
            SP.wait(lane.pending())

        block = ctx.enter_context(nc.Block())

        @block.sync
        def _(e):
            SP.play(e)

        @block.gpsimd
        def _(e):
            PO.play(e)

        @block.scalar
        def _(e):
            AC.play(e)

        @block.tensor
        def _(e):
            PE.play(e)

        @block.vector
        def _(e):
            DV.play(e)


def constants():
    f = np.float32
    i = np.arange(128)
    c = np.zeros((128, NCS), f)

    def put(name, v):
        o, w = CS[name]
        c[:, o:o + w] = v

    put("ident", np.eye(128, dtype=f))
    put("triu", (i[:, None] <= i[None, :]).astype(f))
    put("stri", (i[:, None] < i[None, :]).astype(f))
    put("ones", 1.0)
    put("e32", (CAP * np.arange(64)).astype(f)[None])
    put("rev64", (64 - np.arange(64)).astype(f)[None])
    put("rev8", (8 - np.arange(8)).astype(f)[None])
    put("iob", np.arange(31).astype(f)[None])
    put("invf", (f(500000.0) ** (-np.arange(0, 16, 2, dtype=f) / f(16))).astype(f)[None])
    put("half", -0.5)
    n = 511 - np.arange(512)
    nf = np.maximum(n, 16).astype(f)
    large = 16 + (np.log(nf / f(16)) / f(math.log(1024 / 16)) * f(16)).astype(np.int32)
    bucket = np.where(n < 16, n, np.minimum(large, 31))
    onehot = (bucket[None, :] == np.arange(32)[:, None]).astype(f)
    diag = np.where(i[:, None] >= i[None, :], 0.0, NEG).astype(f)
    prev = np.where(i[None, :] > i[:, None], 0.0, NEG).astype(f)
    mask2 = np.concatenate([diag, prev, diag, prev, diag, prev, diag], axis=1)
    tokid = (np.arange(4)[None, :] * 128 + i[:, None]).astype(np.int32)
    tokid = np.concatenate([2 * tokid, 2 * tokid + 1], axis=1)
    return c, onehot, mask2, tokid


def kernel(**inputs):
    import numpy as _np
    import concourse.bacc as _bacc
    from concourse import mybir as _mybir
    from concourse.bass_utils import run_bass_kernel_spmd as _run

    g = {k: _np.asarray(v) for k, v in inputs.items()}

    def tiles(w, c0=0, c1=None):
        w = w[:, c0:c1]
        return w.reshape(-1, 128, w.shape[1]).transpose(1, 0, 2).reshape(128, -1)

    w_in, w2 = g["w_in"][0], g["w_in_2"][0]
    pack = _np.zeros((len(SLOTS), 128, 4096), _np.float32)

    def put(name, a):
        pack[SLOT[name], :, 0:a.shape[1]] = a

    for n, o in (("cb", 0), ("cc", 512), ("cv", 1024), ("q", 1536), ("k", 2048), ("v", 2560), ("qm", 3072),
                 ("ga0", 3584), ("ga1", 4096), ("gb0", 4608), ("gb1", 5120), ("gc0", 5632), ("gc1", 6144)):
        put(n, tiles(w_in, o, o + 512))
    put("mk", tiles(g["w_mem_kv"][0], 0, 512))
    put("mv", tiles(g["w_mem_kv"][0], 512, 1024))
    put("yconv", tiles(g["w_conv_out"][0]))
    put("yattn", tiles(g["w_attn_out"][0]))
    put("ymem", tiles(g["w_mem_out"][0]))
    for s in range(2):
        put(f"out{s}", tiles(g["w_out"][0], 512 * s, 512 * s + 512))
        put(f"oo{s}", tiles(g["w_out_2"][0], 512 * s, 512 * s + 512))
    up = g["w_up"][0]
    for s in range(11):
        a = _np.concatenate([up[:, 256 * s:256 * s + 256], up[:, 2816 + 256 * s:2816 + 256 * s + 256]], axis=1)
        put(f"up{s}", tiles(a))
    for s in range(6):
        put(f"down{s}", tiles(g["w_down"][0][512 * s:512 * s + 512]))
    xo = 2048
    for s in range(4):
        put(f"z{s}", tiles(w2, 512 * s, 512 * s + 512))
        put(f"xs{s}", tiles(w2, xo + 512 * s, xo + 512 * s + 512))
        put(f"so{s}", tiles(g["w_ssd_out_2"][0], 256 * s, 256 * s + 256))
    put("bm", tiles(w2, xo + 2048, xo + 2560))
    put("cm", tiles(w2, xo + 2560, xo + 3072))
    qo = xo + 3072 + 32
    wq = w2[:, qo:qo + 1024].reshape(1024, 16, 64)[:, HEADS2].reshape(1024, 1024)
    wa = g["w_attn_out_2"][0].reshape(16, 64, 1024)[HEADS2].reshape(1024, 1024)
    for s in range(2):
        put(f"q{s}", tiles(wq, 512 * s, 512 * s + 512))
        put(f"ao{s}", tiles(wa, 512 * s, 512 * s + 512))
        put(f"gs{s}", tiles(w2, qo + 1536 + 512 * s, qo + 2048 + 512 * s))
        put(f"gt{s}", tiles(w2, qo + 2560 + 512 * s, qo + 3072 + 512 * s))
    put("kv", tiles(w2, qo + 1024, qo + 1536))
    wsmall = _np.concatenate([tiles(w2, xo + 3072, xo + 3104), tiles(_np.concatenate(
        [g["w_router_group_2"][0], g["w_router_expert_2"][0].transpose(1, 0, 2).reshape(1024, 64)], axis=1))], axis=1)
    we = _np.concatenate([g["w_gate_e_2"][0], g["w_up_e_2"][0]], axis=2)
    we = we.reshape(64, 8, 128, 512).transpose(0, 2, 1, 3).reshape(64, 128, 4096)
    wd = g["w_down_e_2"][0].reshape(64, 2, 128, 1024).transpose(0, 2, 1, 3).reshape(64, 128, 2048)
    wexp = _np.concatenate([we, wd], axis=2)

    cols = _np.zeros((128, NCOL), _np.float32)
    for n, v in (("g_pre_mix", g["g_pre_mix"]), ("g_mem", g["g_mem"]), ("b_gate", g["b_gate"]),
                 ("conv_mix", g["conv_mix_w"]), ("g_pre_ffn", g["g_pre_ffn"]), ("ffn_w", g["ffn_conv_w"]),
                 ("ffn_b", g["ffn_conv_b"]), ("norm1_g", g["norm1_g_2"]), ("conv_w", g["conv_w_2"]),
                 ("conv_b", g["conv_b_2"]), ("norm2_g", g["norm2_g_2"])):
        o, w = COL[n]
        cols[:, o:o + w] = v.reshape(w, 128).T
    rows = _np.zeros((1, NROW), _np.float32)
    for n, v in (("dt_bias", g["dt_bias_2"]), ("a_log", g["a_log_2"]), ("d_skip", g["d_skip_2"]),
                 ("q_g", g["q_norm_g_2"]), ("k_g", g["k_norm_g_2"]), ("sinks", g["sinks_2"][0][HEADS2]),
                 ("b_r", _np.concatenate([g["b_router_group_2"].reshape(-1), g["b_router_expert_2"].reshape(-1)]))):
        o, w = ROW[n]
        rows[0, o:o + w] = v.reshape(-1)
    gains = _np.concatenate([g["g_post_mix"], g["g_post_ffn"], g["norm2_g_2"]], axis=0)
    consts, onehot, mask2, tokid = constants()
    arrays = {
        "x": g["x"][0], "mem": g["mem"][0], "rel_bias": g["rel_bias"], "wpack": pack, "wexp": wexp,
        "wsmall": wsmall, "cols": cols, "rows": rows, "gains": gains, "sng": g["ssd_norm_g_2"],
        "pos": g["positions_2"].reshape(4, 128).T, "consts": consts, "onehot": onehot, "mask2": mask2,
        "tokid": tokid,
    }
    nc = _bacc.Bacc("TRN2", target_bir_lowering=False, num_devices=1)
    ins, dram = {}, {}
    for name, a in arrays.items():
        a = _np.ascontiguousarray(a)
        ins[f"in_{name}"] = a
        dram[name] = nc.dram_tensor(f"in_{name}", a.shape, _mybir.dt.from_np(a.dtype), kind="ExternalInput").ap()
    for name, shape, dt in (("bvec", [8, 128, 640], F32), ("h2d", [512, 1024], F32), ("tab", [NSLOT, 1], I32),
                            ("ya", [1024, 1024], F32)):
        dram[name] = nc.dram_tensor(name, shape, dt, kind="Internal").ap()
    out = nc.dram_tensor("out_0", [512, 1024], F32, kind="ExternalOutput").ap()
    with nc.allow_non_contiguous_dma(reason="a column of four-byte entries"):
        two_layers(nc, dram, out)
    r = _run(nc, [ins], core_ids=[0])
    return r.results[0]["out_0"].reshape(1, 512, 1024)
```

```python
import math
from contextlib import ExitStack

import numpy as np
import concourse.bass as bass
from concourse import mybir

F32 = mybir.dt.float32
F32R = mybir.dt.float32r
I32 = mybir.dt.int32
ACT = mybir.ActivationFunctionType
ALU = mybir.AluOpType
AX = mybir.AxisListType.X

NEG = -1e30
EPS = 1e-6
CAP = 32
NOV = 31
NST = 64 * CAP
NSLOT = NST + NOV * 128
HEADS2 = [4 * (2 * kp + par) + i for kp in range(2) for i in range(4) for par in range(2)]

SLOTS = ["q", "k", "v", "qm", "mk", "mv", "cc", "cv", "cb", "yconv", "ga0", "ga1", "yattn", "gb0", "gb1",
         "ymem", "gc0", "gc1", "out0", "out1"]
SLOTS += [f"up{i}" for i in range(11)] + [f"down{i}" for i in range(6)]
SLOTS += ["bm", "cm"] + [f"{n}{g}" for g in range(4) for n in ("xs", "z")]
SLOTS += ["gs0", "so0", "so1", "gs1", "so2", "so3", "q0", "q1", "kv", "gt0", "ao0", "gt1", "ao1", "oo0", "oo1"]
SLOT = {n: i for i, n in enumerate(SLOTS)}

PLAN = []


def plan(kind, *names):
    PLAN.extend((n, h, kind) for n in names for h in range(2))


plan("q", "q", "k")
plan("h", "v")
plan("q", "qm", "mk")
plan("h", "mv")
plan("q", "cc", "cv", "cb", "ga0", "ga1", "gb0", "gb1", "gc0", "gc1")
plan("r", "out0", "out1")
plan("q", *(f"up{i}" for i in range(11)))
plan("r", *(f"down{i}" for i in range(5)))
PLAN.append(("down5", 0, "r"))
plan("q", "bm", "cm")
SWITCH = [len(PLAN)]
for g in range(4):
    for h in range(2):
        PLAN += [(f"xs{g}", h, "q"), (f"z{g}", h, "z")]
SWITCH.append(len(PLAN))
plan("h", "q0", "q1", "kv")
RAW = len(PLAN)
SWITCH.append(RAW)
for s in range(4):
    PLAN += [(f"gs{s // 2}", s % 2, "q"), (f"so{s}", 0, "r"), (f"so{s}", 1, "r")]
for s in range(4):
    PLAN += [(f"gt{s // 2}", s % 2, "q"), (f"ao{s // 2}", s % 2, "r")]
plan("r", "oo0", "oo1")
SWITCH.append(len(PLAN))

COLS = [("g_pre_mix", 8), ("g_mem", 8), ("b_gate", 24), ("conv_mix", 12), ("g_pre_ffn", 8), ("ffn_w", 132),
        ("ffn_b", 44), ("norm1_g", 8), ("conv_w", 96), ("conv_b", 24), ("norm2_g", 8)]
ROWS = [("dt_bias", 32), ("a_log", 32), ("d_skip", 32), ("q_g", 64), ("k_g", 64), ("sinks", 16),
        ("b_r", 72)]
CST = [("ident", 128), ("triu", 128), ("stri", 128), ("ones", 128), ("e32", 64), ("rev64", 64), ("rev8", 8),
       ("iob", 31), ("invf", 8), ("half", 64)]


def offsets(parts):
    at, out = 0, {}
    for n, w in parts:
        out[n] = (at, w)
        at += w
    return out, at


COL, NCOL = offsets(COLS)
ROW, NROW = offsets(ROWS)
CS, NCS = offsets(CST)


class Lane:

    def __init__(self, sem, dma_sems=()):
        self.sem, self.n, self.ops, self.seen = sem, 0, [], {}
        self.dma_sems, self.dma_n = list(dma_sems), 0

    def wait(self, *toks):
        for t in toks:
            if t is None:
                continue
            if isinstance(t, list):
                self.wait(*t)
                continue
            sem, value = t
            if self.seen.get(id(sem), 0) < value:
                self.seen[id(sem)] = value
                self.ops.append(lambda e, s=sem, v=value: e.wait_ge(s, v))

    def do(self, fn, *toks, inc=True):
        self.wait(*toks)
        if not inc:
            self.ops.append(fn)
            return None
        self.n += 1
        self.ops.append(lambda e: fn(e).then_inc(self.sem, 1))
        return (self.sem, self.n)

    def dma(self, out, in_, *toks, how=None):
        k, m = self.dma_n % len(self.dma_sems), self.dma_n // len(self.dma_sems)
        self.dma_n += 1
        sem = self.dma_sems[k]
        if m:
            self.wait((sem, 16 * m))
        self.wait(*toks)
        fn = how or (lambda e: e.dma_start(out, in_))
        self.ops.append(lambda e: fn(e).then_inc(sem, 16))
        return (sem, 16 * (m + 1))

    def mark(self):
        fn = self.ops.pop()
        self.n += 1
        self.ops.append(lambda e: fn(e).then_inc(self.sem, 1))
        return (self.sem, self.n)

    def pending(self):
        out = [(self.sem, self.n)] if self.n else []
        for k, s in enumerate(self.dma_sems):
            m = (self.dma_n - k + len(self.dma_sems) - 1) // len(self.dma_sems)
            if m > 0:
                out.append((s, 16 * m))
        return out

    def play(self, e):
        for op in self.ops:
            op(e)


class Body(Lane):

    def wait(self, *toks):
        for t in toks:
            if t is None:
                continue
            if isinstance(t, list):
                self.wait(*t)
                continue
            sem, value = t
            if self.seen.get(id(sem), 0) < value:
                self.seen[id(sem)] = value
                self.ops.append(lambda e, i, s=sem, v=value: self.until(e, s, i * self.gain[id(s)] + v))

    def until(self, e, sem, value):
        e.wait_ge(sem, value)
        if self.rest:
            e.sem_inc(self.rest, 1)

    def do(self, fn, *toks, inc=True):
        self.wait(*toks)
        if not inc:
            self.ops.append(lambda e, i: fn(e))
            return None
        self.n += 1
        self.ops.append(lambda e, i: fn(e).then_inc(self.sem, 1))
        return (self.sem, self.n)

    def dma(self, out, in_, *toks, how=None):
        sem = self.dma_sems[self.dma_n]
        self.dma_n += 1
        self.wait(*toks)
        fn = how or (lambda e, i: e.dma_start(out, in_))
        self.ops.append(lambda e, i: fn(e, i).then_inc(sem, 16))
        return (sem, 16)


class Ring:

    def __init__(self, n):
        self.free, self.i = [[] for _ in range(n)], 0

    def take(self):
        k = self.i % len(self.free)
        self.i += 1
        toks = self.free[k]
        assert toks is not None, "a place is taken before it was given back"
        self.free[k] = None
        return k, toks

    def give(self, k, *toks):
        self.free[k] = list(toks)


class Stream:

    def __init__(self, load, split):
        self.load, self.split = load, split
        self.li = self.ui = 0
        self.load_end = self.split_end = 0
        self.at, self.ready, self.sub = {}, {}, 0

    def places(self, raw=None, parts=None, own=None, free=()):
        if raw is not None:
            self.raw, self.raw_free, self.raw_i = raw, [list(free) for _ in raw], 0
        self.parts, self.parts_free, self.parts_i = parts, [list(free) for _ in parts], 0
        if own is not None:
            self.own, self.own_free, self.own_i = own, [list(free) for _ in own], 0

    def until(self, load_end, split_end):
        self.load_end, self.split_end = load_end, split_end
        self.pump()

    def give(self, frees, ks, *toks):
        for k in ks:
            frees[k] = list(toks)

    def pump(self):
        moved = True
        while moved:
            moved = False
            if self.li < self.load_end:
                k = self.raw_i % len(self.raw)
                if self.raw_free[k] is not None:
                    tok = self.load(self.raw[k], PLAN[self.li], self.raw_free[k])
                    self.raw_free[k] = None
                    self.at[self.li] = (k, tok)
                    self.raw_i += 1
                    self.li += 1
                    moved = True
            if self.ui < min(self.split_end, self.li):
                moved |= self.step()

    def step(self):
        name, _, kind = PLAN[self.ui]
        k, tok = self.at[self.ui]
        raw_free = self.raw_free
        if kind == "r":
            self.ready.setdefault(name, []).append(
                (self.raw[k], None, [tok], lambda *t, k=k, f=raw_free: self.give(f, [k], *t)))
            self.ui += 1
            return True
        if kind == "z":
            places, free, i, n, w = self.own, self.own_free, self.own_i, 1, 2048
        else:
            places, free, i, n, w = self.parts, self.parts_free, self.parts_i, 1, 1024
            if kind == "h":
                n, w = 2, 2048
        ks = [(i + j) % len(places) for j in range(n)]
        if any(free[j] is None for j in ks):
            return False
        toks = self.split(self.raw[k] + w * self.sub, places[ks[0]], w, tok, [free[j] for j in ks])
        for j in ks:
            free[j] = None
        if kind == "z":
            self.own_i += n
        else:
            self.parts_i += n
        self.ready.setdefault(name, []).append(
            (places[ks[0]], w, toks, lambda *t, ks=ks, f=free: self.give(f, ks, *t)))
        self.sub += 1
        if w * self.sub == 2048:
            raw_free[k] = list(toks)
            self.sub = 0
            self.ui += 1
        return True

    def get(self, name):
        self.pump()
        return self.ready[name].pop(0)


def zipped(a, b, na=1, nb=1):
    live = [(a, na), (b, nb)]
    while live:
        for g in list(live):
            for _ in range(g[1]):
                if next(g[0], StopIteration) is StopIteration:
                    live.remove(g)
                    break


def two_layers(nc, dram, out):
    ctx = ExitStack()
    with ctx:
        def sem(name):
            return ctx.enter_context(nc.semaphore(name))

        PE, DV, AC, PO, SP = (Lane(sem("s_" + n), [sem(f"d_{n}{i}") for i in range(k)])
                              for n, k in (("pe", 0), ("dve", 0), ("act", 6), ("pool", 12), ("sp", 16)))
        top = [0]

        def alloc(n):
            top[0] += n
            return top[0] - n

        CPo, CCo, RRo, WSo, STo = (alloc(n) for n in (NCOL, NCS, NROW, 832, 560))
        alloc(-top[0] % 8)
        Xo, HTo, MGo, GBo = alloc(4096), alloc(4096), alloc(4096), alloc(1024)
        WRo = alloc(16384)
        Fo = alloc(0)
        spots = [(HTo + 512 * k, 512) for k in range(8)] + [(Xo + 512 * k, 512) for k in range(8)]
        spots += [(MGo + 256 * k, 256) for k in range(16)]
        spots += [(WRo + 4096 + 1024 * k, 1024) for k in range(8)] + [(WRo + 4096 + 2048 * k, 2048) for k in range(6)]
        spots += [(Fo + 11520, 256), (Fo + 11776, 256)]
        RF = {}
        for off, n in spots:
            with nc.sbuf_tensor(f"pad_{off}_{n}", [128, off], F32):
                with nc.sbuf_tensor(f"rf_{off}_{n}", [128, n], F32R) as RF[off, n]:
                    pass
        AR = ctx.enter_context(nc.sbuf_tensor("AR", [128, 52900], F32))
        IA = ctx.enter_context(nc.sbuf_tensor("IA", [128, 176], I32))
        PS = ctx.enter_context(nc.psum_tensor("PS", [128, 8, 512], F32))
        banks = Ring(8)

        def snap():
            return PE.pending() + DV.pending() + AC.pending() + PO.pending()

        def area(off, n):
            return AR[:, off:off + n]

        def parts(off, n):
            return RF[off, n][:, :]

        def cut(ap, a):
            return ap.rearrange("p (a b) -> p a b", a=a)

        CP, CC, RR, WS = area(CPo, NCOL), area(CCo, NCS), area(RRo, NROW), area(WSo, 832)
        X, HT, MG, GB = cut(area(Xo, 4096), 4), cut(area(HTo, 4096), 8), cut(area(MGo, 4096), 8), area(GBo, 1024)
        XN = cut(area(MGo, 4096), 4)
        HH, HL = ([parts(o + 512 * k, 512) for k in range(8)] for o in (HTo, Xo))
        stat_at = [0]

        def col(n):
            stat_at[0] += n
            assert stat_at[0] <= 560
            return AR[:, STo + stat_at[0] - n:STo + stat_at[0]]

        def cp(name, j=0, n=1):
            o = COL[name][0] + j
            return CP[:, o:o + n]

        def cc(name):
            return CC[:, CS[name][0]:CS[name][0] + CS[name][1]]

        def rr(name):
            return RR[:, ROW[name][0]:ROW[name][0] + ROW[name][1]]

        ident = cc("ident")

        def bank():
            k, toks = banks.take()
            return PS[:, k, :], toks, k

        def mm(o, l, r, start, stop, *toks, inc=False):
            return PE.do(lambda e: e.matmul(o, l, r, start=start, stop=stop), *toks, inc=inc)

        def tr(o, i, *toks, inc=False):
            return PE.do(lambda e: e.transpose(o, i, ident), *toks, inc=inc)

        def act(o, i, f, *toks, **kw):
            return AC.do(lambda e: e.activation(o, i, f, **kw), *toks)

        def ts(o, i, s1, s2, op0, op1, *toks, lane=None):
            return (lane or DV).do(lambda e: e.tensor_scalar(o, i, s1, s2, op0, op1), *toks)

        def ts1(o, i, s1, op0, *toks, lane=None):
            return (lane or DV).do(lambda e: e.tensor_scalar(o, i, s1, None, op0), *toks)

        def tt(o, a, b, op, *toks, lane=None):
            return (lane or DV).do(lambda e: e.tensor_tensor(o, a, b, op), *toks)

        def stt(o, a, s, b, op0, op1, *toks):
            return DV.do(lambda e: e.scalar_tensor_tensor(out=o, in0=a, scalar=s, in1=b, op0=op0, op1=op1), *toks)

        def cpy(o, i, *toks, lane=None):
            return (lane or DV).do(lambda e: e.tensor_copy(o, i), *toks)

        def red(o, i, op, *toks, negate=False):
            return DV.do(lambda e: e.tensor_reduce(o, i, AX, op, negate=negate), *toks)

        def load(off, item, free):
            name, h, _ = item
            return SP.dma(AR[:, off:off + 2048], dram["wpack"][SLOT[name], :, 2048 * h:2048 * h + 2048], free)

        def split(src, dst, w, tok, free):
            a = act(parts(dst, w), AR[:, src:src + w], ACT.Copy, tok, free)
            d = tt(parts(dst + w, w), AR[:, src:src + w], parts(dst, w).bitcast(F32), ALU.subtract, a, tok)
            return [a, d]

        st = Stream(load, split)
        st.places([WRo, WRo + 2048], [WRo + 4096 + 2048 * i for i in range(4)])
        yfree = [[]]

        def yload(name):
            w = AR[:, WRo + 12288:WRo + 16384]
            return cut(w, 4), SP.dma(w, dram["wpack"][SLOT[name]], yfree[0])

        t_x = [SP.dma(X[:, i, :], dram["x"][128 * i:128 * i + 128, :]) for i in range(4)]
        t_cp = AC.dma(CP, dram["cols"])
        t_cc = AC.dma(CC, dram["consts"])
        t_rr = AC.dma(RR, dram["rows"].to_broadcast([128, NROW]))
        t_ws = AC.dma(WS, dram["wsmall"])
        half = cc("half")
        st.until(SWITCH[2], SWITCH[0])

        def rstd(ss, n, width, *toks):
            a = ts(ss, ss, 1.0 / width, EPS, ALU.mult, ALU.add, *toks, lane=PO)
            return tt(ss, ss, half[:, 0:n], ALU.pow, a, t_cc, lane=PO)

        def norm_t(src, n, g, hi, lo, xn, toks, lo_free=None):
            ss = col(n)
            a = [act(xn[:, i, :], src[:, i, :], ACT.Square, toks, accum_out=ss[:, i:i + 1]) for i in range(n)]
            r = rstd(ss, n, 1024, a)
            d = [ts1(xn[:, i, :], src[:, i, :], ss[:, i:i + 1], ALU.mult, r, toks) for i in range(n)]
            done = []
            for k in range(8):
                b, bt, bk = bank()
                for i in range(n):
                    p = tr(b[:, 128 * i:128 * i + 128], xn[:, i, 128 * k:128 * k + 128], d[i], bt, t_cc,
                           inc=(i == n - 1))
                o = hi[k]
                e = act(o, b[:, 0:128 * n], ACT.Identity, p, t_cp, scale=cp(g, k))
                l = stt(lo[k], b[:, 0:128 * n], cp(g, k), o.bitcast(F32), ALU.mult, ALU.subtract, e,
                        lo_free)
                banks.give(bk, l)
                done.append(l)
            return done

        def products(o, ws, xs, first, last, *toks):
            (wh, wl), (xh, xl) = ws, xs
            mm(o, wh, xh, first, False, *toks)
            mm(o, wh, xl, False, False)
            return mm(o, wl, xh, False, last, inc=last)

        def tile_q(name, hi, lo, n, toks):
            off, w, wt, done = st.get(name)
            wh, wl = cut(parts(off, w), 8), cut(parts(off + w, w), 8)
            b, bt, bk = bank()
            for k in range(8):
                p = products(b[:, 0:n], (wh[:, k, :], wl[:, k, :]), (hi[k], lo[k]), k == 0, k == 7,
                             bt, wt, toks)
            done(p)
            return b, p, bk

        def tiles_h(name, hi, lo, n, toks):
            bs = [bank() for _ in range(n)]
            out_ = []
            for u in range(2):
                off, w, wt, done = st.get(name)
                wh, wl = cut(parts(off, w), 4), cut(parts(off + w, w), 4)
                for i, (b, bt, bk) in enumerate(bs):
                    c = slice(128 * i, 128 * i + 128)
                    for k in range(4):
                        p = products(b, (hi[4 * u + k][:, c], lo[4 * u + k][:, c]), (wh[:, k, :], wl[:, k, :]),
                                     u + k == 0, u == 1 and k == 3, bt, wt, toks)
                    if u:
                        out_.append((b, p, bk))
                    elif i == n - 1:
                        p = PE.mark()
                done(p)
            return out_

        def tile_t(w, wt, kt, c, rhs, n, toks):
            b, bt, bk = bank()
            for k in range(kt):
                p = mm(b[:, 0:n], w[:, k, c:c + 128], rhs[:, k, 0:n], k == 0, k == kt - 1, bt, wt, toks,
                       inc=(k == kt - 1))
            return b, p, bk

        def rows_norm_add(rows, gt, tmp, tmp_free, t_x):
            done = []
            for i, halves in enumerate(rows):
                ss = col(4)
                o = tmp[:, i % 2, :]
                a = [act(o[:, 512 * h:512 * h + 512], b, ACT.Square, p, tmp_free[i % 2], accum_out=ss[:, h:h + 1])
                     for h, (b, p, bk) in enumerate(halves)]
                s = tt(ss[:, 2:3], ss[:, 0:1], ss[:, 1:2], ALU.add, a)
                r = rstd(ss[:, 2:3], 1, 1024, s)
                adds = []
                for h, (b, p, bk) in enumerate(halves):
                    m = stt(o[:, 512 * h:512 * h + 512], b, ss[:, 2:3], GB[:, 512 * h:512 * h + 512],
                            ALU.mult, ALU.mult, r, gt)
                    banks.give(bk, m)
                    adds.append(tt(X[:, i, 512 * h:512 * h + 512], X[:, i, 512 * h:512 * h + 512],
                                   o[:, 512 * h:512 * h + 512], ALU.add, m, t_x[i]))
                tmp_free[i % 2] = adds
                done += adds
            return done

        f = Fo
        AT, QT, KT, QM = (cut(area(f + 2048 * i, 2048), 4) for i in range(4))
        VV = cut(area(f + 8192, 2048), 4)
        MK = cut(area(f + 10240, 1024), 4)
        MV = cut(area(f + 11264, 1024), 2)
        SK = cut(area(f + 12288, 1024), 2)
        PB = cut(area(f + 13312, 2560), 2)
        PTo = f + 15872
        GT = cut(area(f + 17920, 1024), 2)
        BV = area(f + 17920, 640)
        PT = cut(area(PTo, 2048), 4)
        MEMR = cut(area(f + 13312, 2048), 2)
        MEMN = cut(area(PTo, 2048), 2)
        MH, ML = ([parts(o + 256 * k, 256) for k in range(8)] for o in (MGo, MGo + 2048))
        CCB = cut(area(MGo + 2048, 2048), 4)

        t_mem = [PO.dma(MEMR[:, i, :], dram["mem"][128 * i:128 * i + 128, :]) for i in range(2)]
        t_oh = PO.dma(GB[0:32, 0:512], dram["onehot"])
        t_rb = PO.dma(GB[0:32, 512:520], dram["rel_bias"])

        b, bt, bk = bank()
        p = mm(b[0:8, :], GB[0:32, 512:520], GB[0:32, 0:512], True, True, bt, t_oh, t_rb, inc=True)
        e1 = DV.do(lambda e: e.memset(BV[0:8, 512:640], NEG))
        e2 = cpy(BV[0:8, 0:512], b[0:8, :], p)
        banks.give(bk, e2)
        t_bv = PO.dma(dram["bvec"], BV[0:8, 0:640].unsqueeze(1).to_broadcast([8, 128, 640]), e1, e2)
        t_gb = PO.dma(GB, dram["gains"][0:1, :].to_broadcast([128, 1024]), p)

        t_ht = norm_t(X, 4, "g_pre_mix", HH, HL, XN, t_x)
        t_mt = norm_t(MEMR, 2, "g_mem", MH, ML, MEMN, [t_mem, PE.pending()])

        def proj_t(name, dst, hi, lo, n, toks):
            out_ = []
            for j in range(4):
                b, p, bk = tile_q(name, hi, lo, n, toks)
                if j % 2:
                    e = cpy(dst[:, j, 0:n], b[:, 0:n], p)
                else:
                    e = act(dst[:, j, 0:n], b[:, 0:n], ACT.Copy, p)
                banks.give(bk, e)
                out_.append(e)
            return out_

        t_q = proj_t("q", QT, HH, HL, 512, t_ht)
        t_k = proj_t("k", KT, HH, HL, 512, t_ht)
        t_v = []
        for i, (b, p, bk) in enumerate(tiles_h("v", HH, HL, 4, t_ht)):
            e = act(VV[:, i, :], b, ACT.Copy, p)
            banks.give(bk, e)
            t_v.append(e)
        t_qm = proj_t("qm", QM, HH, HL, 512, t_ht)
        t_mk = proj_t("mk", MK, MH, ML, 256, t_mt)
        t_mv = []
        for i, (b, p, bk) in enumerate(tiles_h("mv", MH, ML, 2, t_mt)):
            e = act(MV[:, i, :], b, ACT.Copy, p)
            banks.give(bk, e)
            t_mv.append(e)
        mem_read = p

        t_o1 = []
        t_om = []
        pt_free = [[t_mt, PE.pending()]]
        p_free = [[t_mt, PE.pending()], [t_mt, PE.pending()]]

        def attention_1():
            sk_free = [[], []]
            for h in range(8):
                lo, t, s = 64 * (h % 2), h // 2, h % 2
                skew = bass.AP(dram["bvec"].tensor, h * 81920 + 127, [[639, 128], [1, 512]])
                t_sk = PO.dma(SK[:, s, :], skew, t_bv, sk_free[s])
                P = PB[:, s, :]
                at = [0, 128, 384, 768]
                nm, rs = col(4), col(4)
                last = []
                for i in range(4):
                    n = 128 * (i + 1)
                    b, bt, bk = bank()
                    p = mm(b[:, 0:n], QT[lo:lo + 64, t, 128 * i:128 * i + 128], KT[lo:lo + 64, t, 0:n], True, True,
                           bt, t_q, t_k, inc=True)
                    Pi = P[:, at[i]:at[i] + n]
                    a = stt(Pi, b[:, 0:n], 0.125, SK[:, s, 384 - 128 * i:512], ALU.mult, ALU.add, p, t_sk,
                            p_free[s])
                    banks.give(bk, a)
                    m = red(nm[:, i:i + 1], Pi, ALU.max, a, negate=True)
                    x = act(Pi, Pi, ACT.Exp, m, bias=nm[:, i:i + 1], accum_out=rs[:, i:i + 1])
                    last.append(x)
                sk_free[s] = [a]
                r = DV.do(lambda e, rs=rs: e.reciprocal(rs, rs), last)
                last = [ts1(P[:, at[i]:at[i] + 128 * (i + 1)], P[:, at[i]:at[i] + 128 * (i + 1)], rs[:, i:i + 1],
                            ALU.mult, r) for i in range(4)]
                yield
                ev = []
                for k in range(4):
                    b, bt, bk = bank()
                    for i in range(k, 4):
                        p = tr(b[:, 128 * i:128 * i + 128], P[:, at[i] + 128 * k:at[i] + 128 * k + 128], bt, last,
                               inc=(i == 3))
                    if k % 2:
                        e = cpy(PT[:, k, 128 * k:512], b[:, 128 * k:512], p, pt_free[0])
                    else:
                        e = act(PT[:, k, 128 * k:512], b[:, 128 * k:512], ACT.Copy, p, pt_free[0])
                    banks.give(bk, e)
                    ev.append(e)
                p_free[s] = [p]
                yield
                b, bt, bk = bank()
                for k in range(4):
                    p = mm(b[lo:lo + 64, 128 * k:512], VV[:, k, 64 * h:64 * h + 64], PT[:, k, 128 * k:512], k == 0,
                           k == 3, bt, ev[k], t_v, inc=(k == 3))
                pt_free[0] = [p]
                e = cpy(QT[lo:lo + 64, t, :], b[lo:lo + 64, :], p)
                banks.give(bk, e)
                t_o1.append(e)
                yield
            scale = 128.0 ** -0.5
            for h in range(4):
                P = cut(PB[:, h % 2, 0:1024], 4)
                nm, rs = col(4), col(4)
                last = []
                for q in range(2):
                    b, bt, bk = bank()
                    for i in range(2):
                        p = mm(b[:, 256 * i:256 * i + 256], QM[:, h, 256 * q + 128 * i:256 * q + 128 * i + 128],
                               MK[:, h, :], True, True, bt, t_qm, t_mk, inc=(i == 1))
                    m = red(nm[:, 2 * q:2 * q + 2], cut(b, 2), ALU.max, p, negate=True)
                    m = ts1(nm[:, 2 * q:2 * q + 2], nm[:, 2 * q:2 * q + 2], scale, ALU.mult, m)
                    for i in range(2):
                        x = act(P[:, 2 * q + i, :], b[:, 256 * i:256 * i + 256], ACT.Exp, m, p_free[h % 2],
                                bias=nm[:, 2 * q + i:2 * q + i + 1], scale=scale,
                                accum_out=rs[:, 2 * q + i:2 * q + i + 1])
                        last.append(x)
                    banks.give(bk, x)
                r = DV.do(lambda e, rs=rs: e.reciprocal(rs, rs), last)
                last = [ts1(P[:, i, :], P[:, i, :], rs[:, i:i + 1], ALU.mult, r) for i in range(4)]
                yield
                ev = []
                for k in range(2):
                    b, bt, bk = bank()
                    for i in range(4):
                        p = tr(b[:, 128 * i:128 * i + 128], P[:, i, 128 * k:128 * k + 128], bt, last, inc=(i == 3))
                    e = cpy(PT[:, k, :], b, p, pt_free[0]) if k else act(PT[:, k, :], b, ACT.Copy, p, pt_free[0])
                    banks.give(bk, e)
                    ev.append(e)
                p_free[h % 2] = [p]
                yield
                b, bt, bk = bank()
                for k in range(2):
                    p = mm(b, MV[:, k, 128 * h:128 * h + 128], PT[:, k, :], k == 0, k == 1, bt, ev, t_mv,
                           inc=(k == 1))
                pt_free[0] = [p]
                e = cpy(QM[:, h, :], b, p)
                banks.give(bk, e)
                t_om.append(e)
                yield

        mg_done = [[] for _ in range(8)]
        gt_free = [[t_bv], [t_bv]]
        gt_i = [0]

        def gated(k, bias, name, y, first):
            b, p, bk = tile_q(name, HH, HL, 512, t_ht_now)
            g = gt_i[0] % 2
            gt_i[0] += 1
            kw = {} if bias is None else {"bias": bias}
            a = act(GT[:, g, :], b, ACT.Sigmoid, p, gt_free[g], **kw)
            banks.give(bk, a)
            yield
            yb, yp, yk = y()
            if first:
                m = tt(MG[:, k, :], GT[:, g, :], yb, ALU.mult, a, yp, mg_done[k])
                banks.give(yk, m)
                gt_free[g] = [m]
            else:
                m = tt(GT[:, g, :], GT[:, g, :], yb, ALU.mult, a, yp)
                banks.give(yk, m)
                m = tt(MG[:, k, :], MG[:, k, :], GT[:, g, :], ALU.add, m, mg_done[k])
                gt_free[g] = [m]
            mg_done[k] = [m]
            return p, yp

        def branch_1(yname, gname, bi, src, toks, first):
            wy, wyt = yload(yname)
            for k in range(8):
                p, yp = yield from gated(k, cp("b_gate", 8 * bi + k), f"{gname}{k // 4}",
                                         lambda: tile_t(wy, wyt, 4, 128 * k, src, 512, toks), first)
                yield
            yfree[0] = [yp]

        t_ht_now = t_ht
        u_done = [None] * 4
        a_done = [None] * 4

        def dense_1():
            tc = proj_t("cc", CCB, HH, HL, 512, t_ht + [mem_read])
            yield
            for j in range(4):
                b, p, bk = tile_q("cv", HH, HL, 512, t_ht)
                m = tt(CCB[:, j, :], CCB[:, j, :], b, ALU.mult, p, tc)
                banks.give(bk, m)
                u_done[j] = m
                c = [cp("conv_mix", 4 * q + j) for q in range(3)]
                m = ts1(AT[:, j, :], CCB[:, j, :], c[2], ALU.mult, m, t_cp)
                m = stt(AT[:, j, 1:512], CCB[:, j, 0:511], c[1], AT[:, j, 1:512], ALU.mult, ALU.add, m)
                m = stt(AT[:, j, 2:512], CCB[:, j, 0:510], c[0], AT[:, j, 2:512], ALU.mult, ALU.add, m)
                a_done[j] = m
                yield
            for j in range(4):
                b, p, bk = tile_q("cb", HH, HL, 512, t_ht)
                m = tt(AT[:, j, :], AT[:, j, :], b, ALU.mult, p, a_done[j])
                banks.give(bk, m)
                a_done[j] = m
                yield
            for k in range(8):
                mg_done[k] = [mem_read, a_done[3], t_mt]
            yield from branch_1("yconv", "ga", 0, AT, a_done, True)

        zipped(attention_1(), dense_1(), 1, 1)
        for _ in branch_1("yattn", "gb", 1, QT, t_o1, False):
            pass
        for _ in branch_1("ymem", "gc", 2, QM, t_om, False):
            pass

        def out_rows(names, toks):
            bs = [[bank() for _ in range(2)] for _ in range(4)]
            rows = [[None, None] for _ in range(4)]
            for h, name in enumerate(names):
                for q in range(2):
                    off, _, wt, done = st.get(name)
                    w = cut(area(off, 2048), 8)
                    for i in range(4):
                        b, bt, bk = bs[i][h]
                        for k in range(8):
                            p = mm(b[:, 256 * q:256 * q + 256], MG[:, k, 128 * i:128 * i + 128], w[:, k, :], k == 0,
                                   k == 7, bt, wt, toks, inc=(k == 7))
                        rows[i][h] = (b, p, bk)
                    done(p)
            return rows

        def reload(src, *toks):
            return [PO.dma(X[:, i, :], src[128 * i:128 * i + 128, :], *toks) for i in range(4)]

        t_xr = reload(dram["x"], snap())
        TMP = cut(area(Fo, 2048), 2)
        free = snap()
        t_x1 = rows_norm_add(out_rows(["out0", "out1"], mg_done), t_gb, TMP, [free, free], t_xr)
        t_gb = PO.dma(GB, dram["gains"][1:2, :].to_broadcast([128, 1024]), t_x1)

        mg_read = snap()
        t_st = [PO.dma(dram["x1d"][128 * i:128 * i + 128, :], X[:, i, :], t_x1) for i in range(4)]
        t_ht = norm_t(X, 4, "g_pre_ffn", HH, HL, XN, [t_x1, mg_read], t_st)
        FT = cut(area(Fo + 2048, 11264), 22)
        YB = cut(area(Fo + 13312, 4096), 8)
        start = snap()
        y_free = [start] * 8
        yi = 0
        ft_done = [None] * 22
        for s in range(11):
            half_y = {}
            for j in range(4):
                tix = 2 * s + j % 2 + (22 if j >= 2 else 0)
                b, p, bk = tile_q(f"up{s}", HH, HL, 512, t_ht)
                y, yk = YB[:, yi % 8, :], yi % 8
                yi += 1
                a = act(y, b, ACT.Identity, p, y_free[yk], t_cp, bias=cp("ffn_b", tix), scale=cp("ffn_w", 88 + tix))
                m = stt(y[:, 1:512], b[:, 0:511], cp("ffn_w", 44 + tix), y[:, 1:512], ALU.mult, ALU.add, a)
                m = stt(y[:, 2:512], b[:, 0:510], cp("ffn_w", tix), y[:, 2:512], ALU.mult, ALU.add, m)
                banks.give(bk, m)
                if j < 2:
                    half_y[j] = (y, act(y, y, ACT.Gelu_apprx_tanh, m), yk)
                else:
                    ya, ta, ka = half_y[j - 2]
                    m = tt(FT[:, 2 * s + j - 2, :], ya, y, ALU.mult, m, ta, start)
                    y_free[yk] = y_free[ka] = [m]
                    ft_done[2 * s + j - 2] = m
        t_xr = reload(dram["x1d"], snap(), t_st)
        rows = [[bank() for _ in range(2)] for _ in range(4)]
        done_p = [[None, None] for _ in range(4)]
        for k in range(22):
            if k % 2 == 0:
                off, _, wt, done = st.get(f"down{k // 4}")
                w = cut(area(off, 2048), 2)
            for i in range(4):
                for hf in range(2):
                    b, bt, bk = rows[i][hf]
                    done_p[i][hf] = mm(b, FT[:, k, 128 * i:128 * i + 128], w[:, k % 2, 512 * hf:512 * hf + 512],
                                       k == 0, k == 21, bt, wt, ft_done[k], inc=(k % 2 == 1))
            if k % 2:
                done(done_p[3][1])
        rows = [[(rows[i][h][0], done_p[i][h], rows[i][h][2]) for h in range(2)] for i in range(4)]
        t_x2 = rows_norm_add(rows, t_gb, TMP, [start, start], t_xr)

        t_st = [PO.dma(dram["x2d"][128 * i:128 * i + 128, :], X[:, i, :], t_x2) for i in range(4)]
        t_ht = norm_t(X, 4, "norm1_g", HH, HL, XN, [t_x2, snap()], t_st)
        t_ht_now = t_ht
        f = Fo
        DT, DA, ACU, EXA, DTE, CDE = (area(f + 128 * i, 128) for i in range(6))
        f += 768
        CB = area(f, 512)
        PV = area(f + 512, 512)
        BR = cut(area(f + 1024, 512), 4)
        XS = cut(area(f + 1536, 2048), 4)
        XD = cut(area(f + 3584, 2048), 4)
        XE = cut(area(f + 5632, 1024), 2)
        EB = cut(area(f + 6656, 2048), 2)
        T1 = cut(area(f + 8704, 1024), 2)
        ZB = cut(area(f + 9728, 1024), 2)
        T2 = area(f + 10752, 512)
        YT = cut(area(Fo + 12032, 8192), 16)
        SNG = cut(GB, 2)
        BT, CT = cut(area(MGo, 2048), 4), cut(area(MGo + 2048, 2048), 4)
        start = snap()
        dtv = cut(DT, 4)
        h32 = lambda name: rr(name).unsqueeze(1).to_broadcast([128, 4, 32])

        a = act(parts(f + 10752, 256), WS[:, 0:256], ACT.Copy, t_ws, start)
        m = tt(parts(f + 11008, 256), WS[:, 0:256], parts(f + 10752, 256).bitcast(F32), ALU.subtract, a)
        wdh, wdl = cut(parts(f + 10752, 256), 8), cut(parts(f + 11008, 256), 8)
        b, bt, bk = bank()
        for i in range(4):
            for k in range(8):
                c = slice(128 * i, 128 * i + 128)
                p = products(b[:, 32 * i:32 * i + 32], (HH[k][:, c], HL[k][:, c]), (wdh[:, k, :], wdl[:, k, :]),
                             k == 0, k == 7, bt, t_ht, m)
        e = tt(dtv, cut(b[:, 0:128], 4), h32("dt_bias"), ALU.add, p, t_rr, start)
        banks.give(bk, e)
        a = act(DA, DT, ACT.Abs, e, start)
        a = act(DA, DA, ACT.Exp, a, scale=-1.0)
        a = act(DA, DA, ACT.Ln, a, bias=1.0)
        m = ts1(DT, DT, 0.0, ALU.max, a)
        m = tt(DT, DT, DA, ALU.add, m)
        t_dt = m
        na = col(32)
        a = act(na, rr("a_log"), ACT.Exp, t_rr)
        m = ts1(na, na, -1.0, ALU.mult, a)
        m = tt(cut(DA, 4), dtv, na.unsqueeze(1).to_broadcast([128, 4, 32]), ALU.mult, m, t_dt)
        t_da = m
        b, bt, bk = bank()
        p = mm(b[:, 0:128], cc("triu"), DA, True, True, bt, t_da, t_cc)
        p = mm(b[:, 128:256], cc("ones"), DA, True, True, inc=True)
        c1 = cpy(ACU, b[:, 0:128], p, start)
        c2 = tt(DTE, b[:, 128:256], ACU, ALU.subtract, c1, start)
        c3 = act(CDE, b[:, 128:256], ACT.Exp, c2, start)
        c4 = act(EXA, ACU, ACT.Exp, c1, start)
        c5 = act(DTE, DTE, ACT.Exp, c2)
        banks.give(bk, c3)
        t_acu, t_dec = c1, [c3, c4, c5]

        def conv_silu(b, p, tix, y, toks):
            a = act(y, b, ACT.Identity, p, toks, t_cp, bias=cp("conv_b", tix), scale=cp("conv_w", 72 + tix))
            m = a
            for q in range(1, 4):
                m = stt(y[:, q:512], b[:, 0:512 - q], cp("conv_w", 24 * (3 - q) + tix), y[:, q:512], ALU.mult,
                        ALU.add, m)
            return m, act(y, y, ACT.Silu, m)

        t_bt, t_ct = [], []
        for name, dst, base, out_ in (("bm", BT, 16, t_bt), ("cm", CT, 20, t_ct)):
            for j in range(4):
                b, p, bk = tile_q(name, HH, HL, 512, t_ht)
                m, s = conv_silu(b, p, base + j, dst[:, j, :], start)
                banks.give(bk, m)
                out_.append(s)

        st.places(parts=[WRo + 4096, WRo + 6144], own=[WRo + 8192, WRo + 12288], free=snap())
        st.until(SWITCH[2], SWITCH[1])
        b4 = lambda ap, c, g: ap[:, 32 * c + 8 * g:32 * c + 8 * g + 8].unsqueeze(2).to_broadcast([128, 8, 64])
        h8 = lambda ap: ap.rearrange("p (h d) -> p h d", h=8)
        triu = cc("triu")
        t1_free, xe_free, eb_free = [start, start], [start, start], [start, start]
        zb_free, sng_free = [start, start], [start, start]
        yt_done = []
        grp_free = start

        def xs_rows(j, y, s, free, out_):
            b, bt, bk = bank()
            for c in range(4):
                q = tr(b[:, 128 * c:128 * c + 128], y[:, 128 * c:128 * c + 128], bt, s, inc=(c == 3))
            eb_free[j % 2] = [q]
            e = cpy(XS[:, :, 128 * j:128 * j + 128], cut(b, 4), q, free)
            banks.give(bk, e)
            out_.append(e)

        def finish(g, c, t1, o1, t_z, t_sn):
            o1 = tt(t1, t1, ZB[:, c % 2, :], ALU.mult, t_z, o1)
            ss = col(1)
            a = act(ZB[:, c % 2, :], t1, ACT.Square, o1, accum_out=ss)
            zb_free[c % 2] = [a]
            r = rstd(ss, 1, 512, a)
            o1 = stt(t1, t1, ss, SNG[:, g % 2, :], ALU.mult, ALU.mult, r, t_sn, a)
            sng_free[g % 2] = [o1]
            b, bt, bk = bank()
            for j in range(4):
                q = tr(b[:, 128 * j:128 * j + 128], t1[:, 128 * j:128 * j + 128], bt, o1, inc=(j == 3))
            t1_free[c % 2] = [q]
            e = act(YT[:, 4 * g:4 * g + 4, 128 * c:128 * c + 128], cut(b, 4), ACT.Copy, q, start)
            banks.give(bk, e)
            yt_done.append(e)

        todo = None
        for g in range(4):
            t_sn = PO.dma(SNG[:, g % 2, :], dram["sng"][0:1, 512 * g:512 * g + 512].to_broadcast([128, 512]),
                          sng_free[g % 2])
            t_xs = []
            held = None
            for j in range(4):
                b, p, bk = tile_q(f"xs{g}", HH, HL, 512, t_ht)
                y = EB[:, j % 2, 0:512]
                m, s = conv_silu(b, p, 4 * g + j, y, eb_free[j % 2])
                banks.give(bk, m)
                if held:
                    xs_rows(*held)
                held = (j, y, s, grp_free, t_xs)
                if j == 0 and todo:
                    finish(*todo)
                    todo = None
            b, bt, bk = bank()
            for c in range(4):
                q = tr(b[:, 128 * c:128 * c + 128], BT[:, g, 128 * c:128 * c + 128], bt, t_bt, inc=(c == 3))
            t_br = act(BR, cut(b, 4), ACT.Copy, q, grp_free)
            banks.give(bk, t_br)
            b, bt, bk = bank()
            for c in range(4):
                q = mm(b[:, 128 * c:128 * c + 128], BT[:, g, 128 * c:128 * c + 128],
                       CT[:, g, 128 * c:128 * c + 128], True, True, bt, t_bt, t_ct, inc=(c == 3))
            t_cb = tt(cut(CB, 4), cut(b, 4), triu.unsqueeze(1).to_broadcast([128, 4, 128]), ALU.mult, q, grp_free)
            banks.give(bk, t_cb)
            wz = [st.get(f"z{g}") for _ in range(2)]
            t_pv = None
            for c in range(4):
                eb = EB[:, c % 2, :]
                t_m = []
                rows = []
                for hh in range(2):
                    b, bt, bk = bank()
                    for h in range(4):
                        o = 32 * c + 8 * g + 4 * hh + h
                        q = mm(b[:, 128 * h:128 * h + 128], DA[:, o:o + 1].to_broadcast([128, 128]), triu, True,
                               True, bt, t_da, inc=(h == 3))
                    rows.append((b, q, bk))
                if held:
                    xs_rows(*held)
                    held = None
                    t_xd = [tt(h8(XD[:, n, :]), h8(XS[:, n, :]), b4(DT, n, g), ALU.mult, t_xs, t_dt, grp_free)
                            for n in range(4)]
                for hh, (b, q, bk) in enumerate(rows):
                    for h in range(4):
                        o = 32 * c + 8 * g + 4 * hh + h
                        m = ts(eb[:, 512 * hh + 128 * h:512 * hh + 128 * h + 128], b[:, 128 * h:128 * h + 128],
                               ACU[:, o:o + 1], 0.0, ALU.subtract, ALU.min, q, t_acu, eb_free[c % 2])
                    banks.give(bk, m)
                    eh = eb[:, 512 * hh:512 * hh + 512]
                    a = act(eh, eh, ACT.Exp, m)
                    t_m.append((eh, a))
                if c < 3:
                    t_xe = tt(h8(XE[:, c % 2, :]), h8(XD[:, c, :]), b4(DTE, c, g), ALU.mult, t_xd, t_dec,
                              xe_free[c % 2])
                t_m = [tt(cut(eh, 4), cut(eh, 4), CB[:, 128 * c:128 * c + 128].unsqueeze(1)
                          .to_broadcast([128, 4, 128]), ALU.mult, a, t_cb) for eh, a in t_m]
                zb, zbt, zk = bank()
                tc = slice(128 * c, 128 * c + 128)
                for k in range(8):
                    off, zw, wt, done = wz[k // 4]
                    zp = products(zb, (HH[k][:, tc], HL[k][:, tc]),
                                  (cut(parts(off, zw), 4)[:, k % 4, :], cut(parts(off + zw, zw), 4)[:, k % 4, :]),
                                  k == 0, k == 7, zbt, wt, t_ht)
                if c == 3:
                    for z_ in wz:
                        z_[3](zp)
                t_z = act(ZB[:, c % 2, :], zb, ACT.Silu, zp, zb_free[c % 2])
                banks.give(zk, t_z)
                if todo:
                    finish(*todo)
                t1 = T1[:, c % 2, :]
                if c:
                    b, bt, bk = bank()
                    q = mm(b, CT[:, g, 128 * c:128 * c + 128], PV, True, True, bt, t_pv, t_ct, inc=True)
                    off_read = q
                    o1 = tt(h8(t1), h8(b), b4(EXA, c, g), ALU.mult, q, t_dec, t1_free[c % 2])
                    banks.give(bk, o1)
                t_cs = None
                if c < 3:
                    bs, bst, bsk = bank()
                    t_cs = mm(bs, BR[:, c, :], XE[:, c % 2, :], True, True, bst, t_br, t_xe, inc=True)
                    xe_free[c % 2] = [t_cs]
                b, bt, bk = bank()
                for h in range(8):
                    q = mm(b[:, 64 * h:64 * h + 64], eb[:, 128 * h:128 * h + 128], XD[:, c, 64 * h:64 * h + 64],
                           True, True, bt, t_m, t_xd, inc=(h == 7))
                eb_free[c % 2] = [q]
                if c < 3:
                    if c == 0:
                        t_pv = cpy(PV, bs, t_cs, grp_free)
                    else:
                        m = tt(h8(PV), h8(PV), b4(CDE, c, g), ALU.mult, t_pv, off_read, t_dec)
                        t_pv = tt(PV, PV, bs, ALU.add, m, t_cs)
                    banks.give(bsk, t_pv)
                if c:
                    o1 = tt(t1, t1, b, ALU.add, q, o1)
                else:
                    o1 = cpy(t1, b, q, t1_free[0])
                banks.give(bk, o1)
                d8 = rr("d_skip")[:, 8 * g:8 * g + 8].unsqueeze(2).to_broadcast([128, 8, 64])
                m = tt(h8(T2), h8(XS[:, c, :]), d8, ALU.mult, t_xs, t_rr, start, lane=DV)
                o1 = tt(t1, t1, T2, ALU.add, m, o1)
                todo = (g, c, t1, o1, t_z, t_sn)
            grp_free = snap()
        finish(*todo)

        start = snap()
        st.places(parts=[WRo + 4096 + 2048 * i for i in range(4)], free=start)
        st.until(SWITCH[2], SWITCH[2])
        f = Fo - 4096
        QKf = cut(area(f, 5120), 4)
        QK = area(f, 5120).rearrange("p (i h d) -> p i h d", i=4, h=20)
        OT = cut(area(f, 4096), 8)
        QT = cut(area(f + 5120, 4096), 8)
        KT = cut(area(f + 9216, 1024), 2)
        VV = cut(area(f + 10240, 1024), 4)
        LB = cut(area(f + 11264, 1792), 2)
        PTT = cut(area(f + 13056, 1792), 2)
        MKo = area(f + 14848, 896)
        COS, SIN, R1, R2 = (area(f + 15744 + 32 * i, 32) for i in range(4))
        TA, TB, TC = (area(f + 13056 + 160 * i, 160) for i in range(3))
        SQ = area(f + 11264, 1280)
        GT = SNG
        gt_free[0] = gt_free[1] = start
        mg_done = [[start] for _ in range(8)]
        t_mk2 = PO.dma(MKo, dram["mask2"], start)
        t_ps = PO.dma(IA[:, 0:4], dram["pos"])

        pf = col(4)
        m = cpy(pf, IA[:, 0:4], t_ps)
        v48 = lambda ap: ap.rearrange("p (i d) -> p i d", i=4)
        m = tt(v48(R1), pf.unsqueeze(2).to_broadcast([128, 4, 8]), cc("invf").unsqueeze(1).to_broadcast([128, 4, 8]),
               ALU.mult, m, start)
        m = ts(R2, R1, 1.0 / (2 * math.pi), 12582912.0, ALU.mult, ALU.add, m)
        m = ts1(R2, R2, 12582912.0, ALU.subtract, m)
        c1 = 6.28125
        c2 = 0.0019350051879882812
        c3 = 2 * math.pi - c1 - c2
        for c in (c1, c2, c3):
            m = stt(R1, R2, -c, R1, ALU.mult, ALU.add, m)
        m = ts(R1, R1, math.pi - 1e-6, -math.pi + 1e-6, ALU.min, ALU.max, m)
        a = act(SIN, R1, ACT.Sin, m)
        a = act(COS, R1, ACT.Sin, a, scale=0.5)
        m = tt(COS, COS, COS, ALU.mult, a)
        t_cs = ts(COS, COS, -2.0, 1.0, ALU.mult, ALU.add, m)

        t_qk = []
        t_v = []
        for s, name in enumerate(("q0", "q1", "kv")):
            for i, (b, p, bk) in enumerate(tiles_h(name, HH, HL, 4, t_ht)):
                if s < 2:
                    e = act(QKf[:, i, 512 * s:512 * s + 512], b, ACT.Copy, p, start)
                else:
                    e = cpy(QKf[:, i, 1024:1280], b[:, 0:256], p, start)
                    t_v.append(cpy(VV[:, i, :], b[:, 256:512], p, start))
                    e = t_v[-1]
                banks.give(bk, e)
                t_qk.append(e)
        st.places(raw=[WRo + 2048 * i for i in range(3)], parts=[WRo + 6144 + 2048 * i for i in range(3)],
                  free=PE.pending())
        st.until(SWITCH[3], SWITCH[3])

        def dense_2():
            for k in range(8):
                def y():
                    off, _, wt, done = st.get(f"so{k // 2}")
                    b, p, bk = tile_t(cut(area(off, 2048), 16), wt, 16, 0, YT, 512, yt_done)
                    done(p)
                    return b, p, bk
                yield from gated(k, None, f"gs{k // 4}", y, True)
                yield

        def attention_2():
            sq_done = start
            qn = []
            for i in range(4):
                a = act(SQ, QKf[:, i, :], ACT.Square, t_qk, sq_done)
                ss = col(20)
                m = red(ss, SQ.rearrange("p (h d) -> p h d", h=20), ALU.add, a)
                sq_done = [m]
                r = rstd(ss, 20, 64, m)
                m = tt(QK[:, i, :, :], QK[:, i, :, :], ss.unsqueeze(2).to_broadcast([128, 20, 64]), ALU.mult, r)
                m = tt(QK[:, i, 0:16, :], QK[:, i, 0:16, :], rr("q_g").unsqueeze(1).to_broadcast([128, 16, 64]),
                       ALU.mult, m)
                m = tt(QK[:, i, 16:20, :], QK[:, i, 16:20, :], rr("k_g").unsqueeze(1).to_broadcast([128, 4, 64]),
                       ALU.mult, m)
                va, vb, vc = (x.rearrange("p (h d) -> p h d", h=20) for x in (TA, TB, TC))
                ci = COS[:, 8 * i:8 * i + 8].unsqueeze(1).to_broadcast([128, 20, 8])
                si = SIN[:, 8 * i:8 * i + 8].unsqueeze(1).to_broadcast([128, 20, 8])
                q1, q2 = QK[:, i, :, 0:8], QK[:, i, :, 8:16]
                a1 = tt(va, q2, si, ALU.mult, m, t_cs, start)
                a2 = tt(vb, q1, si, ALU.mult, m, start)
                a3 = tt(vc, q2, ci, ALU.mult, m, start)
                a4 = tt(q1, q1, ci, ALU.mult, a2)
                a5 = tt(q1, q1, va, ALU.subtract, a4, a1)
                m = tt(q2, vb, vc, ALU.add, a3, a2)
                qn.append([a5, m])
                yield
            t_qt = []
            for t in (8, 0, 1, 2, 3, 9, 4, 5, 6, 7):
                b, bt, bk = bank()
                for i in range(4):
                    p = tr(b[:, 128 * i:128 * i + 128], QKf[:, i, 128 * t:128 * t + 128], bt, qn[i], inc=(i == 3))
                dst = QT[:, t, :] if t < 8 else KT[:, t - 8, :]
                e = cpy(dst, b, p, start) if t % 2 else act(dst, b, ACT.Copy, p, start)
                banks.give(bk, e)
                t_qt.append(e)
            qk_read = p
            l_free, pt_free2 = [qn, qn], [qn, qn]
            m3 = lambda ap: ap.rearrange("p (n k) -> p n k", k=256)

            def scores(pos):
                t, lo, kp, s = pos // 2, 64 * (pos % 2), pos // 8, pos % 2
                L = LB[:, s, :]
                nm, rs = col(4), col(4)
                scored = []
                for half_ in range(2):
                    b, bt, bk = bank()
                    o = 0
                    for n in ((0, 1), (2, 3))[half_]:
                        w_ = 128 if n == 0 else 256
                        k0 = 0 if n == 0 else 128 * (n - 1)
                        p = mm(b[:, o:o + w_], QT[lo:lo + 64, t, 128 * n:128 * n + 128],
                               KT[lo:lo + 64, kp, k0:k0 + w_], True, True, bt, t_qt, inc=(n % 2 == 1))
                        o += w_
                    lo_, hi_ = (0, 384) if half_ == 0 else (384, 896)
                    a = stt(L[:, lo_:hi_], b[:, 0:hi_ - lo_], 0.125, MKo[:, lo_:hi_], ALU.mult, ALU.add, p, t_mk2,
                            l_free[s])
                    banks.give(bk, a)
                    scored.append(a)
                m1 = red(nm[:, 0:1], L[:, 0:128], ALU.max, scored)
                m2 = red(nm[:, 1:4], m3(L[:, 128:896]), ALU.max, scored)
                m = ts(nm, nm, rr("sinks")[:, pos:pos + 1], -1.0, ALU.max, ALU.mult, m1, m2, t_rr)
                xs = []
                for n in range(4):
                    lo_, hi_ = (0, 128) if n == 0 else (128 + 256 * (n - 1), 128 + 256 * n)
                    xs.append(act(L[:, lo_:hi_], L[:, lo_:hi_], ACT.Exp, m, bias=nm[:, n:n + 1],
                                  accum_out=rs[:, n:n + 1]))
                xs.append(act(nm, nm, ACT.Exp, m, xs, bias=rr("sinks")[:, pos:pos + 1]))
                m = tt(rs, rs, nm, ALU.add, xs)
                m = DV.do(lambda e, rs=rs: e.reciprocal(rs, rs), m)
                d1 = ts1(L[:, 0:128], L[:, 0:128], rs[:, 0:1], ALU.mult, m)
                d2 = tt(m3(L[:, 128:896]), m3(L[:, 128:896]), rs[:, 1:4].unsqueeze(2).to_broadcast([128, 3, 256]),
                        ALU.mult, m, lane=PO)
                return [d1, d2]

            def values(pos, ready):
                t, lo, kp, s = pos // 2, 64 * (pos % 2), pos // 8, pos % 2
                kv = 2 * kp + pos % 2
                L = LB[:, s, :]
                ev = []
                for half_ in range(2):
                    b, bt, bk = bank()
                    lo_, n_ = (0, 3) if half_ == 0 else (384, 4)
                    for u in range(n_):
                        p = tr(b[:, 128 * u:128 * u + 128], L[:, lo_ + 128 * u:lo_ + 128 * u + 128], bt, ready,
                               inc=(u == n_ - 1))
                    e = act(PTT[:, s, lo_:lo_ + 128 * n_], b[:, 0:128 * n_], ACT.Copy, p, pt_free2[s])
                    banks.give(bk, e)
                    ev.append(e)
                l_free[s] = [p]
                yield
                b, bt, bk = bank()
                for n in range(4):
                    srcs = [(0, 0)] if n == 0 else [(n - 1, 128 + 256 * (n - 1)), (n, 256 + 256 * (n - 1))]
                    for u, (kb, o) in enumerate(srcs):
                        p = mm(b[lo:lo + 64, 128 * n:128 * n + 128], VV[:, kb, 64 * kv:64 * kv + 64],
                               PTT[:, s, o:o + 128], u == 0, u == len(srcs) - 1, bt, ev, t_v, inc=(n == 3))
                pt_free2[s] = [p]
                e = cpy(OT[lo:lo + 64, t, :], b[lo:lo + 64, :], p, qk_read)
                banks.give(bk, e)
                t_o2.append(e)

            ready = scores(0)
            yield
            for pos in range(16):
                nxt = scores(pos + 1) if pos < 15 else None
                yield from values(pos, ready)
                ready = nxt

        t_o2, held_w = [], []
        zipped(dense_2(), attention_2(), 1, 2)
        for k in range(8):
            def y():
                if k % 2 == 0:
                    held_w[:] = st.get(f"ao{k // 4}")
                off, _, wt, done = held_w
                w = cut(area(off + 1024 * (k % 2), 1024), 8)
                b, p, bk = tile_t(w, wt, 8, 0, OT, 512, t_o2)
                if k % 2:
                    done(p)
                return b, p, bk
            for _ in gated(k, None, f"gt{k // 4}", y, False):
                pass
        t_xr = reload(dram["x2d"], snap())
        t_gb = PO.dma(GB, dram["gains"][2:3, :].to_broadcast([128, 1024]), snap())
        t_x3 = []
        for i, halves in enumerate(out_rows(["oo0", "oo1"], mg_done)):
            for h, (b, p, bk) in enumerate(halves):
                m = tt(X[:, i, 512 * h:512 * h + 512], X[:, i, 512 * h:512 * h + 512], b, ALU.add, p, t_xr)
                banks.give(bk, m)
                t_x3.append(m)

        start = snap()
        GUs = [WRo + 4096 * k for k in range(5)] + [HTo]
        DNs = [WRo + 20480 + 2048 * k for k in range(6)]
        XB = cut(area(MGo, 2048), 2)
        XT = cut(area(MGo + 2048, 2048), 2)
        f = WRo + 32768
        HS, HD, YE = cut(area(f, 512), 2), cut(area(f + 512, 512), 2), cut(area(f + 1024, 2048), 2)
        gur, dnr = Ring(6), Ring(6)
        gur.free = [[start] for _ in range(5)] + [None]
        dnr.free = [[start] for _ in range(6)]
        wexp = dram["wexp"]

        def eload(ring, places, width, lo, n):
            k, toks = ring.take()
            w = AR[:, places[k]:places[k] + width]
            return w, SP.dma(w, wexp[n, :, lo:lo + width], toks), k

        n_pre = 5
        pre = [(eload(gur, GUs, 4096, 0, n), eload(dnr, DNs, 2048, 4096, n)) for n in range(n_pre)]
        t_h2 = []
        ss = col(4)
        a = [act(XN[:, i, :], X[:, i, :], ACT.Square, t_x3, start, accum_out=ss[:, i:i + 1]) for i in range(4)]
        r = rstd(ss, 4, 1024, a)
        for i in range(4):
            m = stt(XN[:, i, :], X[:, i, :], ss[:, i:i + 1], GB, ALU.mult, ALU.mult, r, t_gb)
            t_h2.append(m)
        t_h2d = [PO.dma(dram["h2d"][128 * i:128 * i + 128, :], XN[:, i, :], t_h2[i]) for i in range(4)]
        t_ht = []
        for k in range(8):
            b, bt, bk = bank()
            for i in range(4):
                p = tr(b[:, 128 * i:128 * i + 128], XN[:, i, 128 * k:128 * k + 128], bt, t_h2[i], inc=(i == 3))
            e = act(HT[:, k, :], b, ACT.Copy, p, start) if k % 2 else cpy(HT[:, k, :], b, p, start)
            banks.give(bk, e)
            t_ht.append(e)
        wr = cut(WS[:, 256:832], 8)
        RL = cut(area(f, 288), 4)
        b, bt, bk = bank()
        for i in range(4):
            for k in range(8):
                p = mm(b[:, 72 * i:72 * i + 72], HT[:, k, 128 * i:128 * i + 128], wr[:, k, :], k == 0, k == 7, bt,
                       t_ht, t_ws, inc=(i == 3 and k == 7))
        m = tt(RL, cut(b[:, 0:288], 4), rr("b_r").unsqueeze(1).to_broadcast([128, 4, 72]), ALU.add, p, t_rr, start)
        banks.give(bk, m)
        f += 288
        GL = RL[:, :, 0:8]
        OG, VG = (area(f + 32 * i, 32).rearrange("p (i g) -> p i g", i=4) for i in range(2))
        f += 64
        EL, O1, O2, V1 = (area(f + 256 * i, 256).rearrange("p (i g) -> p i g", i=4) for i in range(4))
        f += 1024
        bc = lambda ap, n: ap.unsqueeze(2).to_broadcast([128, 4, n])
        row = lambda ap, n: ap.unsqueeze(1).to_broadcast([128, 4, n])
        gm, gs, v1, v2, ix = col(4), col(4), col(4), col(4), col(4)
        m = red(gm, GL, ALU.max, m)
        m2 = tt(VG, GL, bc(gm, 8), ALU.subtract, m, start)
        a = act(VG, VG, ACT.Exp, m2)
        m2 = red(gs, VG, ALU.add, a)
        m2 = DV.do(lambda e: e.reciprocal(gs, gs), m2)

        def first(oh, vals, mx, rev, n, *toks):
            m = tt(oh, vals, bc(mx, n), ALU.is_equal, *toks)
            m = tt(oh, oh, row(rev, n), ALU.mult, m, t_cc)
            m = red(ix, oh, ALU.max, m)
            return tt(oh, oh, bc(ix, n), ALU.is_equal, m)

        m = first(OG, GL, gm, cc("rev8"), 8, m, start)
        m = ts(VG, OG, -1.0, 1e30, ALU.add, ALU.mult, m, m2)
        el4 = lambda ap: ap.rearrange("p i (g e) -> p i g e", g=8)
        for i in range(4):
            mi = tt(el4(EL)[:, i], RL[:, i, 8:72].rearrange("p (g e) -> p g e", g=8),
                    VG[:, i, :].unsqueeze(2).to_broadcast([128, 8, 8]), ALU.add, m, start)
        m = red(v1, EL, ALU.max, mi)
        m = first(O1, EL, v1, cc("rev64"), 64, m, start)
        m = ts1(V1, O1, -2e30, ALU.mult, m, start)
        m = tt(V1, EL, V1, ALU.add, m)
        m = red(v2, V1, ALU.max, m)
        m = first(O2, V1, v2, cc("rev64"), 64, m, start)
        t_oh2 = m
        m = tt(v2, v2, v1, ALU.subtract, m)
        a = act(v2, v2, ACT.Exp, m)
        m = ts1(v1, v2, 1.0, ALU.add, a)
        m = DV.do(lambda e: e.reciprocal(v1, v1), m)
        m = tt(v1, v1, gs, ALU.mult, m, m2)
        t_gate = tt(v2, v2, v1, ALU.mult, m)
        m = tt(V1, O1, O2, ALU.add, t_oh2)
        b, bt, bk = bank()
        for i in range(4):
            for u in range(i + 1):
                p = mm(b[:, 64 * i:64 * i + 64], cc("stri") if u == i else cc("ones"), V1[:, u, :], u == 0, u == i,
                       bt, m, t_cc)
        for u in range(4):
            p = mm(b[:, 256:320], cc("ones"), V1[:, u, :], u == 0, u == 3, inc=(u == 3))
        PO_ = EL
        c1 = cpy(PO_, b[:, 0:256].rearrange("p (i e) -> p i e", i=4), p)
        CNT, NB, CA, CB2 = (area(f + 64 * i, 64) for i in range(4))
        f += 256
        m = ts(CNT, b[:, 256:320], -float(CAP), 0.0, ALU.add, ALU.max, p, start)
        banks.give(bk, m)
        m = ts1(NB, CNT, 0.5, ALU.is_gt, m)
        for q in range(1, 4):
            m = ts1(CA, CNT, 128.0 * q + 0.5, ALU.is_gt, m)
            m = tt(NB, NB, CA, ALU.add, m)
        m = cpy(CA, NB, m)
        a_, b_ = CA, CB2
        for q in range(6):
            st = 1 << q
            m1 = cpy(b_[:, 0:st], a_[:, 0:st], m)
            m = tt(b_[:, st:64], a_[:, st:64], a_[:, 0:64 - st], ALU.add, m1)
            a_, b_ = b_, a_
        incl = a_
        BEF = area(HTo, 31 * 64).rearrange("p (b e) -> p b e", b=31)
        bef = col(31)
        q1 = DV.do(lambda e: e.tensor_tensor(BEF, incl.unsqueeze(1).to_broadcast([128, 31, 64]),
                                             cc("iob").unsqueeze(2).to_broadcast([128, 31, 64]), ALU.is_le), m, start)
        q1 = red(bef, BEF, ALU.add, q1)
        q1 = ts1(bef, bef, 63.0, ALU.min, q1)
        t_be = cpy(IA[:, 64:95], bef, q1)
        t_be = cpy(IA[:, 95:96], incl[:, 63:64], t_be)
        m = tt(NB, incl, NB, ALU.subtract, m)
        m = ts(NB, NB, 128.0, float(NST - CAP), ALU.mult, ALU.add, m)
        S1, S2 = (area(f + 256 * i, 256).rearrange("p (i g) -> p i g", i=4) for i in range(2))
        f += 512
        m1 = tt(S1, PO_, row(cc("e32"), 64), ALU.add, c1, start)
        m2 = tt(S2, PO_, row(NB, 64), ALU.add, m, c1, start)
        m1 = tt(S1, S1, S2, ALU.subtract, m1, m2)
        m2 = ts1(PO_, PO_, CAP - 0.5, ALU.is_lt, m1)
        m1 = tt(S1, S1, PO_, ALU.mult, m2)
        m1 = tt(S1, S1, S2, ALU.add, m1)
        sl = col(8)
        for j, oh in enumerate((O1, O2)):
            m = tt(S2, S1, oh, ALU.mult, m1)
            m1 = red(sl[:, 4 * j:4 * j + 4], S2, ALU.add, m)
        t_sl = cpy(IA[:, 8:16], sl, m1)

        z = PO.do(lambda e: e.memset(IA[:, 16:63], 4096))
        t_z = PO.dma(dram["tab"].rearrange("(p c) o -> p (c o)", p=128), IA[:, 16:63], z)
        t_tk = PO.dma(IA[:, 96:104], dram["tokid"])
        t_sc = []
        for j in range(2):
            for i in range(4):
                idx, val = IA[:, 8 + 4 * j + i:9 + 4 * j + i], IA[:, 96 + 4 * j + i:97 + 4 * j + i]
                t_sc.append(PO.dma(None, None, t_z, t_tk, t_sl, how=lambda e, idx=idx, val=val: e.indirect_dma_start(
                    dram["tab"], bass.IndirectOffsetOnAxis(ap=idx, axis=0), val, None, bounds_check=NSLOT - 1,
                    oob_is_err=False)))
        t_tab = PO.dma(IA[:, 16:63], dram["tab"].rearrange("(b p) o -> p (b o)", p=128), t_sc)
        m = DV.do(lambda e: e.tensor_scalar(IA[:, 128:175], IA[:, 16:63], 1, None, ALU.logical_shift_right), t_tab)
        t_tok = ts1(IA[:, 128:175], IA[:, 128:175], 511.0, ALU.min, m)

        after = snap()
        gur.free[5] = [after]

        def expert(wid, gus, dns, xb, t_xb, fr, xt, hs, hd, ye):
            ne = len(gus)
            ev = []
            for hf in range(2):
                b, bt, bk = bank()
                for k in range(4):
                    p = tr(b[:, 128 * k:128 * k + 128], xb[:, 512 * hf + 128 * k:512 * hf + 128 * k + 128], bt, t_xb,
                           inc=(k == 3))
                o = xt[:, 4 * hf:4 * hf + 4, :]
                e = act(o, cut(b, 4), ACT.Copy, p, fr["xt"]) if hf else cpy(o, cut(b, 4), p, fr["xt"])
                banks.give(bk, e)
                ev.append(e)
            fr["xb"] = [p]
            b, bt, bk = bank()
            t_gu, t_dn = [], []
            pairs = [range(ne)[j:j + 2] for j in range(0, ne, 2)]
            for pair in pairs:
                for k in range(8):
                    for j in pair:
                        w = cut(gus[j][0], 8)
                        p = mm(b[wid * j:wid * j + wid, :], xt[:, k, wid * j:wid * j + wid], w[:, k, :], k == 0,
                               k == 7, bt, ev, gus[j][1], inc=(k == 7 and j == pair[-1]))
                t_gu += [p] * len(pair)
            fr["xt"] = [p]
            a = act(hs, b[:, 0:256], ACT.Silu, p, fr["hs"])
            m = tt(hs, hs, b[:, 256:512], ALU.mult, a)
            banks.give(bk, m)
            b, bt, bk = bank()
            for q in range(2):
                p = tr(b[:, 128 * q:128 * q + 128], hs[:, 128 * q:128 * q + 128], bt, m, inc=(q == 1))
            fr["hs"] = [p]
            e = cpy(hd, cut(b[:, 0:256], 2), p, fr["hd"])
            banks.give(bk, e)
            ys = []
            b2 = [bank() for _ in range(2)]
            for pair in pairs:
                for hf in range(2):
                    b, bt, bk = b2[hf]
                    for q in range(2):
                        for j in pair:
                            w = cut(dns[j][0], 2)
                            p = mm(b[wid * j:wid * j + wid, :], hd[:, q, wid * j:wid * j + wid],
                                   w[:, q, 512 * hf:512 * hf + 512], q == 0, q == 1, bt, e, dns[j][1],
                                   inc=(q == 1 and j == pair[-1]))
                t_dn += [p] * len(pair)
            for hf in range(2):
                b, bt, bk = b2[hf]
                o = ye[:, 512 * hf:512 * hf + 512]
                y = act(o, b, ACT.Copy, p, fr["ye"]) if hf else cpy(o, b, p, fr["ye"])
                banks.give(bk, y)
                ys.append(y)
            fr["hd"] = [p]
            return t_gu, t_dn, ys

        t_ya = []
        frs = [{n: after for n in ("xb", "xt", "hs", "hd", "ye")} for _ in range(2)]

        def gather(blk):
            xb, tok = XB[:, blk % 2, :], IA[:, 128 + blk:129 + blk]
            return PO.dma(None, None, t_h2d, t_tok, frs[blk % 2]["xb"], how=lambda e: e.indirect_dma_start(
                xb, None, dram["h2d"], bass.IndirectOffsetOnAxis(ap=tok, axis=0), bounds_check=511,
                oob_is_err=False))

        t_g = gather(0)
        for blk in range(16):
            s = blk % 2
            fr = frs[s]
            gu, dn = [], []
            for j in range(4):
                n = 4 * blk + j
                if n < n_pre:
                    gu.append(pre[n][0])
                    dn.append(pre[n][1])
                else:
                    gu.append(eload(gur, GUs, 4096, 0, n))
                    dn.append(eload(dnr, DNs, 2048, 4096, n))
            t_now, t_g = t_g, gather(blk + 1) if blk < 15 else None
            t_gu, t_dn, ys = expert(CAP, gu, dn, XB[:, s, :], t_now, fr, cut(XT[:, s, :], 8), HS[:, s, :],
                                    cut(HD[:, s, :], 2), YE[:, s, :])
            for j in range(4):
                gur.give(gu[j][2], t_gu[j])
                dnr.give(dn[j][2], t_dn[j])
            asg = IA[:, 16 + blk:17 + blk]
            t_y = PO.dma(None, None, ys, t_tab, how=lambda e, s=s, asg=asg: e.indirect_dma_start(
                dram["ya"], bass.IndirectOffsetOnAxis(ap=asg, axis=0), YE[:, s, :], None, bounds_check=1023,
                oob_is_err=False))
            fr["ye"] = [t_y]
            t_ya.append(t_y)

        outer = (PE, DV, AC, PO, SP)
        oend = [snap()]
        inner = tuple(Body(sem("l_" + n), [sem(f"l_{n}{i}") for i in range(k)])
                      for n, k in (("pe", 0), ("dve", 0), ("act", 0), ("pool", 2), ("sp", 2)))
        gain = {}
        for lane in inner:
            lane.gain, lane.rest = gain, None
        inner[3].rest, inner[4].rest = sem("rest_pool"), sem("rest_sp")
        PE, DV, AC, PO, SP = inner
        banks_outer, banks = banks, Ring(8)

        def dyn_idx(e, i):
            return e.tensor_copy(IA[:, 112:113], IA[:, bass.ds(i + 32, 1)])

        def dyn_tok(e, i):
            return e.tensor_copy(IA[:, 113:114], IA[:, bass.ds(i + 144, 1)])

        def load_w(e, i, w, lo, width):
            x = e.value_load(IA[0:1, bass.ds(i + 64, 1)], min_val=0, max_val=63)
            return e.dma_start(w, wexp[bass.ds(x, 1), :, lo:lo + width].rearrange("a p c -> (a p) c"))

        DV.n += 2
        DV.ops.append(lambda e, i: dyn_idx(e, i).then_inc(DVi.sem, 1))
        DV.ops.append(lambda e, i: dyn_tok(e, i).then_inc(DVi.sem, 1))
        DVi = DV
        t_ix = (DV.sem, 2)
        gw, dw = AR[:, GUs[0]:GUs[0] + 4096], AR[:, DNs[0]:DNs[0] + 2048]
        t_w1 = SP.dma(None, None, how=lambda e, i: load_w(e, i, gw, 0, 4096))
        t_w2 = SP.dma(None, None, how=lambda e, i: load_w(e, i, dw, 4096, 2048))
        t_g = PO.dma(None, None, t_ix, how=lambda e, i: e.indirect_dma_start(
            XB[:, 0, :], None, dram["h2d"], bass.IndirectOffsetOnAxis(ap=IA[:, 113:114], axis=0), bounds_check=511,
            oob_is_err=False))
        fr = {n: [] for n in ("xb", "xt", "hs", "hd", "ye")}
        t_gu, t_dn, ys = expert(128, [(gw, t_w1, 0)], [(dw, t_w2, 0)], XB[:, 0, :], t_g, fr,
                                cut(XT[:, 0, :], 8), HS[:, 0, :], cut(HD[:, 0, :], 2), YE[:, 0, :])
        t_last = PO.dma(None, None, ys, how=lambda e, i: e.indirect_dma_start(
            dram["ya"], bass.IndirectOffsetOnAxis(ap=IA[:, 112:113], axis=0), YE[:, 0, :], None, bounds_check=1023,
            oob_is_err=False))
        for lane in inner:
            if lane.n:
                gain[id(lane.sem)] = lane.n
            for q in lane.dma_sems:
                gain[id(q)] = 16
        ends = [(lane.sem, lane.n) for lane in inner if lane.n] + [(q, 16) for lane in inner for q in lane.dma_sems]
        PE, DV, AC, PO, SP = outer
        banks = banks_outer

        def loop_of(body):
            def run(e):
                n = e.value_load(IA[0:1, 95:96], min_val=0, max_val=NOV)
                with e.If(n > 0):
                    for t in oend[0]:
                        e.wait_ge(*t)
                    with e.Fori(0, n) as i:
                        for op in body.ops:
                            op(e, i)
                        for q, v in ends:
                            body.until(e, q, i * v + v)
            return run

        for lane, body in zip(outer, inner):
            lane.wait(t_be, t_tok)
            lane.ops.append(loop_of(body))

        YC = [AR[:, o:o + 2048].rearrange("p (j d) -> p j d", j=2) for o in GUs[0:4]]
        ya = dram["ya"].rearrange("(t j) d -> t j d", j=2)
        for i in range(4):
            t_c = PO.dma(YC[i], ya[128 * i:128 * i + 128], oend[0], t_ya)
            m = stt(X[:, i, :], YC[i][:, 0, :], v1[:, i:i + 1], X[:, i, :], ALU.mult, ALU.add, t_c, t_gate)
            m = stt(X[:, i, :], YC[i][:, 1, :], v2[:, i:i + 1], X[:, i, :], ALU.mult, ALU.add, m)
            SP.dma(out[128 * i:128 * i + 128, :], X[:, i, :], m)
        for lane in (SP, AC, PO):
            SP.wait(lane.pending())

        block = ctx.enter_context(nc.Block())

        @block.sync
        def _(e):
            SP.play(e)

        @block.gpsimd
        def _(e):
            PO.play(e)

        @block.scalar
        def _(e):
            AC.play(e)

        @block.tensor
        def _(e):
            PE.play(e)

        @block.vector
        def _(e):
            DV.play(e)


def constants():
    f = np.float32
    i = np.arange(128)
    c = np.zeros((128, NCS), f)

    def put(name, v):
        o, w = CS[name]
        c[:, o:o + w] = v

    put("ident", np.eye(128, dtype=f))
    put("triu", (i[:, None] <= i[None, :]).astype(f))
    put("stri", (i[:, None] < i[None, :]).astype(f))
    put("ones", 1.0)
    put("e32", (CAP * np.arange(64)).astype(f)[None])
    put("rev64", (64 - np.arange(64)).astype(f)[None])
    put("rev8", (8 - np.arange(8)).astype(f)[None])
    put("iob", np.arange(31).astype(f)[None])
    put("invf", (f(500000.0) ** (-np.arange(0, 16, 2, dtype=f) / f(16))).astype(f)[None])
    put("half", -0.5)
    n = 511 - np.arange(512)
    nf = np.maximum(n, 16).astype(f)
    large = 16 + (np.log(nf / f(16)) / f(math.log(1024 / 16)) * f(16)).astype(np.int32)
    bucket = np.where(n < 16, n, np.minimum(large, 31))
    onehot = (bucket[None, :] == np.arange(32)[:, None]).astype(f)
    diag = np.where(i[:, None] >= i[None, :], 0.0, NEG).astype(f)
    prev = np.where(i[None, :] > i[:, None], 0.0, NEG).astype(f)
    mask2 = np.concatenate([diag, prev, diag, prev, diag, prev, diag], axis=1)
    tokid = (np.arange(4)[None, :] * 128 + i[:, None]).astype(np.int32)
    tokid = np.concatenate([2 * tokid, 2 * tokid + 1], axis=1)
    return c, onehot, mask2, tokid


def kernel(**inputs):
    import numpy as _np
    import concourse.bacc as _bacc
    from concourse import mybir as _mybir
    from concourse.bass_utils import run_bass_kernel_spmd as _run

    g = {k: _np.asarray(v) for k, v in inputs.items()}

    def tiles(w, c0=0, c1=None):
        w = w[:, c0:c1]
        return w.reshape(-1, 128, w.shape[1]).transpose(1, 0, 2).reshape(128, -1)

    def quarters(w, c0=0, c1=None, n=128):
        w = w[:, c0:c1]
        return w.reshape(-1, 128, w.shape[1] // n, n).transpose(1, 2, 0, 3).reshape(128, -1)

    w_in, w2 = g["w_in"][0], g["w_in_2"][0]
    pack = _np.zeros((len(SLOTS), 128, 4096), _np.float32)

    def put(name, a):
        pack[SLOT[name], :, 0:a.shape[1]] = a

    for n, o in (("cb", 0), ("cc", 512), ("cv", 1024), ("q", 1536), ("k", 2048), ("v", 2560), ("qm", 3072),
                 ("ga0", 3584), ("ga1", 4096), ("gb0", 4608), ("gb1", 5120), ("gc0", 5632), ("gc1", 6144)):
        put(n, (tiles if n == "v" else quarters)(w_in, o, o + 512))
    put("mk", quarters(g["w_mem_kv"][0], 0, 512))
    put("mv", tiles(g["w_mem_kv"][0], 512, 1024))
    put("yconv", tiles(g["w_conv_out"][0]))
    put("yattn", tiles(g["w_attn_out"][0]))
    put("ymem", tiles(g["w_mem_out"][0]))
    for s in range(2):
        put(f"out{s}", quarters(g["w_out"][0], 512 * s, 512 * s + 512, 256))
        put(f"oo{s}", quarters(g["w_out_2"][0], 512 * s, 512 * s + 512, 256))
    up = g["w_up"][0]
    for s in range(11):
        a = _np.concatenate([up[:, 256 * s:256 * s + 256], up[:, 2816 + 256 * s:2816 + 256 * s + 256]], axis=1)
        put(f"up{s}", quarters(a))
    for s in range(6):
        put(f"down{s}", tiles(g["w_down"][0][512 * s:512 * s + 512]))
    xo = 2048
    for s in range(4):
        put(f"z{s}", tiles(w2, 512 * s, 512 * s + 512))
        put(f"xs{s}", quarters(w2, xo + 512 * s, xo + 512 * s + 512))
        put(f"so{s}", quarters(g["w_ssd_out_2"][0], 256 * s, 256 * s + 256))
    put("bm", quarters(w2, xo + 2048, xo + 2560))
    put("cm", quarters(w2, xo + 2560, xo + 3072))
    qo = xo + 3072 + 32
    wq = w2[:, qo:qo + 1024].reshape(1024, 16, 64)[:, HEADS2].reshape(1024, 1024)
    wa = g["w_attn_out_2"][0].reshape(16, 64, 1024)[HEADS2].reshape(1024, 1024)
    for s in range(2):
        put(f"q{s}", tiles(wq, 512 * s, 512 * s + 512))
        put(f"ao{s}", quarters(wa, 512 * s, 512 * s + 512))
        put(f"gs{s}", quarters(w2, qo + 1536 + 512 * s, qo + 2048 + 512 * s))
        put(f"gt{s}", quarters(w2, qo + 2560 + 512 * s, qo + 3072 + 512 * s))
    put("kv", tiles(w2, qo + 1024, qo + 1536))
    wsmall = _np.concatenate([tiles(w2, xo + 3072, xo + 3104), tiles(_np.concatenate(
        [g["w_router_group_2"][0], g["w_router_expert_2"][0].transpose(1, 0, 2).reshape(1024, 64)], axis=1))], axis=1)
    we = _np.concatenate([g["w_gate_e_2"][0], g["w_up_e_2"][0]], axis=2)
    we = we.reshape(64, 8, 128, 512).transpose(0, 2, 1, 3).reshape(64, 128, 4096)
    wd = g["w_down_e_2"][0].reshape(64, 2, 128, 1024).transpose(0, 2, 1, 3).reshape(64, 128, 2048)
    wexp = _np.concatenate([we, wd], axis=2)

    cols = _np.zeros((128, NCOL), _np.float32)
    for n, v in (("g_pre_mix", g["g_pre_mix"]), ("g_mem", g["g_mem"]), ("b_gate", g["b_gate"]),
                 ("conv_mix", g["conv_mix_w"]), ("g_pre_ffn", g["g_pre_ffn"]), ("ffn_w", g["ffn_conv_w"]),
                 ("ffn_b", g["ffn_conv_b"]), ("norm1_g", g["norm1_g_2"]), ("conv_w", g["conv_w_2"]),
                 ("conv_b", g["conv_b_2"]), ("norm2_g", g["norm2_g_2"])):
        o, w = COL[n]
        cols[:, o:o + w] = v.reshape(w, 128).T
    rows = _np.zeros((1, NROW), _np.float32)
    for n, v in (("dt_bias", g["dt_bias_2"]), ("a_log", g["a_log_2"]), ("d_skip", g["d_skip_2"]),
                 ("q_g", g["q_norm_g_2"]), ("k_g", g["k_norm_g_2"]), ("sinks", g["sinks_2"][0][HEADS2]),
                 ("b_r", _np.concatenate([g["b_router_group_2"].reshape(-1), g["b_router_expert_2"].reshape(-1)]))):
        o, w = ROW[n]
        rows[0, o:o + w] = v.reshape(-1)
    gains = _np.concatenate([g["g_post_mix"], g["g_post_ffn"], g["norm2_g_2"]], axis=0)
    consts, onehot, mask2, tokid = constants()
    arrays = {
        "x": g["x"][0], "mem": g["mem"][0], "rel_bias": g["rel_bias"], "wpack": pack, "wexp": wexp,
        "wsmall": wsmall, "cols": cols, "rows": rows, "gains": gains, "sng": g["ssd_norm_g_2"],
        "pos": g["positions_2"].reshape(4, 128).T, "consts": consts, "onehot": onehot, "mask2": mask2,
        "tokid": tokid,
    }
    nc = _bacc.Bacc("TRN2", target_bir_lowering=False, num_devices=1)
    ins, dram = {}, {}
    for name, a in arrays.items():
        a = _np.ascontiguousarray(a)
        ins[f"in_{name}"] = a
        dram[name] = nc.dram_tensor(f"in_{name}", a.shape, _mybir.dt.from_np(a.dtype), kind="ExternalInput").ap()
    for name, shape, dt in (("bvec", [8, 128, 640], F32), ("h2d", [512, 1024], F32),
                            ("x1d", [512, 1024], F32), ("x2d", [512, 1024], F32), ("tab", [NSLOT, 1], I32),
                            ("ya", [1024, 1024], F32)):
        dram[name] = nc.dram_tensor(name, shape, dt, kind="Internal").ap()
    out = nc.dram_tensor("out_0", [512, 1024], F32, kind="ExternalOutput").ap()
    with nc.allow_non_contiguous_dma(reason="a column of four-byte entries"):
        two_layers(nc, dram, out)
    r = _run(nc, [ins], core_ids=[0])
    return r.results[0]["out_0"].reshape(1, 512, 1024)
```

```python
import math
from contextlib import ExitStack

import numpy as np
import concourse.bass as bass
from concourse import mybir

F32 = mybir.dt.float32
F32R = mybir.dt.float32r
BF16 = mybir.dt.bfloat16
I32 = mybir.dt.int32
ACT = mybir.ActivationFunctionType
ALU = mybir.AluOpType
AX = mybir.AxisListType.X

NEG = -1e30
EPS = 1e-6
CAP = 32
NOV = 31
NST = 64 * CAP
NSLOT = NST + NOV * 128
HEADS2 = [4 * (2 * kp + par) + i for kp in range(2) for i in range(4) for par in range(2)]

SLOTS = ["q", "k", "v", "qm", "mk", "mv", "cc", "cv", "cb", "yconv", "ga0", "ga1", "yattn", "gb0", "gb1",
         "ymem", "gc0", "gc1", "out0", "out1"]
SLOTS += [f"up{i}" for i in range(11)] + [f"down{i}" for i in range(6)]
SLOTS += ["bm", "cm"] + [f"{n}{g}" for g in range(4) for n in ("xs", "z")]
SLOTS += ["gs0", "so0", "so1", "gs1", "so2", "so3", "q0", "q1", "kv", "gt0", "ao0", "gt1", "ao1", "oo0", "oo1"]
SLOT = {n: i for i, n in enumerate(SLOTS)}

PLAN = []


def plan(kind, *names):
    PLAN.extend((n, h, kind) for n in names for h in range(2))


plan("q", "q", "k")
plan("h", "v")
plan("q", "qm", "mk")
plan("h", "mv")
plan("q", "cc", "cv", "cb", "ga0", "ga1", "gb0", "gb1", "gc0", "gc1")
plan("h", "out0", "out1")
plan("q", *(f"up{i}" for i in range(11)))
plan("h", *(f"down{i}" for i in range(5)))
PLAN.append(("down5", 0, "h"))
plan("q", "bm", "cm")
SWITCH = [len(PLAN)]
for g in range(4):
    for h in range(2):
        PLAN += [(f"xs{g}", h, "q"), (f"z{g}", h, "z")]
SWITCH.append(len(PLAN))
plan("h", "q0", "q1", "kv")
RAW = len(PLAN)
SWITCH.append(RAW)
for s in range(4):
    PLAN += [(f"gs{s // 2}", s % 2, "q"), (f"so{s}", 0, "r"), (f"so{s}", 1, "r")]
for s in range(4):
    PLAN += [(f"gt{s // 2}", s % 2, "q"), (f"ao{s // 2}", s % 2, "r")]
plan("z", "oo0", "oo1")
SWITCH.append(len(PLAN))

COLS = [("g_pre_mix", 8), ("g_mem", 8), ("b_gate", 24), ("conv_mix", 12), ("g_pre_ffn", 8), ("ffn_w", 132),
        ("ffn_b", 44), ("norm1_g", 8), ("conv_w", 96), ("conv_b", 24), ("norm2_g", 8)]
ROWS = [("dt_bias", 32), ("a_log", 32), ("d_skip", 32), ("q_g", 64), ("k_g", 64), ("sinks", 16),
        ("b_r", 72)]
CST = [("ident", 128), ("triu", 128), ("stri", 128), ("ones", 128), ("e32", 64), ("rev64", 64), ("rev8", 8),
       ("iob", 31), ("invf", 8), ("half", 64)]


def offsets(parts):
    at, out = 0, {}
    for n, w in parts:
        out[n] = (at, w)
        at += w
    return out, at


COL, NCOL = offsets(COLS)
ROW, NROW = offsets(ROWS)
CS, NCS = offsets(CST)


class Lane:

    def __init__(self, sem, dma_sems=()):
        self.sem, self.n, self.ops, self.seen = sem, 0, [], {}
        self.dma_sems, self.dma_n = list(dma_sems), 0

    def wait(self, *toks):
        for t in toks:
            if t is None:
                continue
            if isinstance(t, list):
                self.wait(*t)
                continue
            sem, value = t
            if self.seen.get(id(sem), 0) < value:
                self.seen[id(sem)] = value
                self.ops.append(lambda e, s=sem, v=value: e.wait_ge(s, v))

    def do(self, fn, *toks, inc=True):
        self.wait(*toks)
        if not inc:
            self.ops.append(fn)
            return None
        self.n += 1
        self.ops.append(lambda e: fn(e).then_inc(self.sem, 1))
        return (self.sem, self.n)

    def dma(self, out, in_, *toks, how=None):
        k, m = self.dma_n % len(self.dma_sems), self.dma_n // len(self.dma_sems)
        self.dma_n += 1
        sem = self.dma_sems[k]
        if m:
            self.wait((sem, 16 * m))
        self.wait(*toks)
        fn = how or (lambda e: e.dma_start(out, in_))
        self.ops.append(lambda e: fn(e).then_inc(sem, 16))
        return (sem, 16 * (m + 1))

    def mark(self):
        fn = self.ops.pop()
        self.n += 1
        self.ops.append(lambda e: fn(e).then_inc(self.sem, 1))
        return (self.sem, self.n)

    def pending(self):
        out = [(self.sem, self.n)] if self.n else []
        for k, s in enumerate(self.dma_sems):
            m = (self.dma_n - k + len(self.dma_sems) - 1) // len(self.dma_sems)
            if m > 0:
                out.append((s, 16 * m))
        return out

    def play(self, e):
        for op in self.ops:
            op(e)


class Body(Lane):

    def wait(self, *toks):
        for t in toks:
            if t is None:
                continue
            if isinstance(t, list):
                self.wait(*t)
                continue
            sem, value = t
            if self.seen.get(id(sem), 0) < value:
                self.seen[id(sem)] = value
                self.ops.append(lambda e, i, s=sem, v=value: self.until(e, s, i * self.gain[id(s)] + v))

    def until(self, e, sem, value):
        e.wait_ge(sem, value)
        if self.rest:
            e.sem_inc(self.rest, 1)

    def do(self, fn, *toks, inc=True):
        self.wait(*toks)
        if not inc:
            self.ops.append(lambda e, i: fn(e))
            return None
        self.n += 1
        self.ops.append(lambda e, i: fn(e).then_inc(self.sem, 1))
        return (self.sem, self.n)

    def dma(self, out, in_, *toks, how=None):
        sem = self.dma_sems[self.dma_n]
        self.dma_n += 1
        self.wait(*toks)
        fn = how or (lambda e, i: e.dma_start(out, in_))
        self.ops.append(lambda e, i: fn(e, i).then_inc(sem, 16))
        return (sem, 16)


class Ring:

    def __init__(self, n):
        self.free, self.i = [[] for _ in range(n)], 0

    def take(self):
        for _ in self.free:
            k = self.i % len(self.free)
            self.i += 1
            toks = self.free[k]
            if toks is not None:
                break
        assert toks is not None, "a place is taken before it was given back"
        self.free[k] = None
        return k, toks

    def give(self, k, *toks):
        self.free[k] = list(toks)


class Stream:

    def __init__(self, load, split):
        self.load, self.split = load, split
        self.li = self.ui = 0
        self.load_end = self.split_end = 0
        self.at, self.ready, self.sub = {}, {}, 0

    def places(self, raw=None, parts=None, free=()):
        if raw is not None:
            self.raw, self.raw_free, self.raw_i = raw, [list(free) for _ in raw], 0
        self.parts, self.parts_free, self.parts_i = parts, [list(free) for _ in parts], 0

    def narrow(self, n, own, free):
        k = self.parts_i % len(self.parts)
        self.parts, self.parts_free, self.parts_i = self.parts[k:k + n], self.parts_free[k:k + n], 0
        self.own, self.own_free, self.own_i = own, [list(free) for _ in own], 0

    def shift(self):
        assert self.parts_i % len(self.parts) == 0
        k = self.raw_i % len(self.raw)
        self.raw, self.parts = self.raw[k:] + self.raw[:k] + self.parts[:1], self.parts[1:]
        self.raw_free = self.raw_free[k:] + self.raw_free[:k] + self.parts_free[:1]
        self.parts_free = self.parts_free[1:]
        self.raw_i = self.parts_i = 0

    def until(self, load_end, split_end):
        self.load_end, self.split_end = load_end, split_end
        self.pump()

    def give(self, frees, ks, *toks):
        for k in ks:
            frees[k] = list(toks)

    def pump(self):
        moved = True
        while moved:
            moved = False
            if self.li < self.load_end:
                k = self.raw_i % len(self.raw)
                if self.raw_free[k] is not None:
                    tok = self.load(self.raw[k], PLAN[self.li], self.raw_free[k])
                    self.raw_free[k] = None
                    self.at[self.li] = (k, tok)
                    self.raw_i += 1
                    self.li += 1
                    moved = True
            if self.ui < min(self.split_end, self.li):
                moved |= self.step()

    def step(self):
        name, _, kind = PLAN[self.ui]
        k, tok = self.at[self.ui]
        raw_free = self.raw_free
        if kind == "r":
            self.ready.setdefault(name, []).append(
                (self.raw[k], None, [tok], lambda *t, k=k, f=raw_free: self.give(f, [k], *t)))
            self.ui += 1
            return True
        if kind == "z":
            places, free, i, n, w = self.own, self.own_free, self.own_i, 1, 2048
        else:
            places, free, i, n, w = self.parts, self.parts_free, self.parts_i, 1, 1024
            if kind == "h":
                n, w = 2, 2048
        ks = [(i + j) % len(places) for j in range(n)]
        if any(free[j] is None for j in ks):
            return False
        toks = self.split(self.raw[k] + w * self.sub, places[ks[0]], w, tok, [free[j] for j in ks])
        for j in ks:
            free[j] = None
        if kind == "z":
            self.own_i += n
        else:
            self.parts_i += n
        self.ready.setdefault(name, []).append(
            (places[ks[0]], w, toks, lambda *t, ks=ks, f=free: self.give(f, ks, *t)))
        self.sub += 1
        if w * self.sub == 2048:
            raw_free[k] = list(toks)
            self.sub = 0
            self.ui += 1
        return True

    def get(self, name):
        self.pump()
        return self.ready[name].pop(0)


def zipped(a, b, na=1, nb=1):
    live = [(a, na), (b, nb)]
    while live:
        for g in list(live):
            for _ in range(g[1]):
                if next(g[0], StopIteration) is StopIteration:
                    live.remove(g)
                    break


def two_layers(nc, dram, out):
    ctx = ExitStack()
    with ctx:
        def sem(name):
            return ctx.enter_context(nc.semaphore(name))

        PE, DV, AC, PO, SP = (Lane(sem("s_" + n), [sem(f"d_{n}{i}") for i in range(k)])
                              for n, k in (("pe", 0), ("dve", 0), ("act", 6), ("pool", 12), ("sp", 16)))
        top = [0]

        def alloc(n):
            top[0] += n
            return top[0] - n

        CPo, CCo, RRo, WSo, STo = (alloc(n) for n in (NCOL, NCS, NROW, 832, 560))
        alloc(-top[0] % 8)
        Xo, HTo, MGo, GBo = alloc(4096), alloc(4096), alloc(4096), alloc(1024)
        WRo = alloc(16384)
        Fo = alloc(0)
        spots = [(HTo + 512 * k, 512) for k in range(8)] + [(Xo + 512 * k, 512) for k in range(8)]
        spots += [(MGo + 256 * k, 256) for k in range(16)]
        spots += [(WRo + 4096 + 1024 * k, 1024) for k in range(8)] + [(WRo + 4096 + 2048 * k, 2048) for k in range(6)]
        FHs = [Fo + 2048 + 512 * k for k in range(22)]
        FLs = [MGo + 512 * k for k in range(8)] + [WRo + 12288 + 512 * k for k in range(8)]
        FLs += [Fo + 512 * k for k in range(4)] + [Fo + 17408, Fo + 17920]
        spots += [(o, 512) for o in FHs + FLs]
        GHs = [Fo + 512 * k for k in range(8)]
        GLs = [Fo + 4096 + 512 * k for k in range(4)] + [Fo + 8192 + 512 * k for k in range(4)]
        G2s = [Fo + 1024 + 512 * k for k in range(16)]
        spots += [(o, 512) for o in GHs + GLs + G2s] + [(Fo + 12032 + 2048 * k, 2048) for k in range(4)]
        spots += [(Fo + 4352, 1024), (Fo + 5376, 1024)]
        RF = {}
        for off, n in dict.fromkeys(spots):
            with nc.sbuf_tensor(f"pad_{off}_{n}", [128, off], F32):
                with nc.sbuf_tensor(f"rf_{off}_{n}", [128, n], F32R) as RF[off, n]:
                    pass
        AR = ctx.enter_context(nc.sbuf_tensor("AR", [128, 52752], F32))
        BT16 = ctx.enter_context(nc.sbuf_tensor("BT16", [128, 512], BF16))
        IA = ctx.enter_context(nc.sbuf_tensor("IA", [128, 176], I32))
        PS = ctx.enter_context(nc.psum_tensor("PS", [128, 8, 512], F32))
        banks = Ring(8)

        def snap():
            return PE.pending() + DV.pending() + AC.pending() + PO.pending()

        def area(off, n):
            return AR[:, off:off + n]

        def parts(off, n):
            return RF[off, n][:, :]

        def cut(ap, a):
            return ap.rearrange("p (a b) -> p a b", a=a)

        CP, CC, RR, WS = area(CPo, NCOL), area(CCo, NCS), area(RRo, NROW), area(WSo, 832)
        X, HT, MG, GB = cut(area(Xo, 4096), 4), cut(area(HTo, 4096), 8), cut(area(MGo, 4096), 8), area(GBo, 1024)
        XN = cut(area(MGo, 4096), 4)
        HH, HL = ([parts(o + 512 * k, 512) for k in range(8)] for o in (HTo, Xo))
        stat_at = [0]

        def col(n):
            stat_at[0] += n
            assert stat_at[0] <= 560
            return AR[:, STo + stat_at[0] - n:STo + stat_at[0]]

        def cp(name, j=0, n=1):
            o = COL[name][0] + j
            return CP[:, o:o + n]

        def cc(name):
            return CC[:, CS[name][0]:CS[name][0] + CS[name][1]]

        def rr(name):
            return RR[:, ROW[name][0]:ROW[name][0] + ROW[name][1]]

        ident = cc("ident")

        def bank():
            k, toks = banks.take()
            return PS[:, k, :], toks, k

        def mm(o, l, r, start, stop, *toks, inc=False):
            return PE.do(lambda e: e.matmul(o, l, r, start=start, stop=stop), *toks, inc=inc)

        def tr(o, i, *toks, inc=False):
            return PE.do(lambda e: e.transpose(o, i, ident), *toks, inc=inc)

        def act(o, i, f, *toks, **kw):
            return AC.do(lambda e: e.activation(o, i, f, **kw), *toks)

        def ts(o, i, s1, s2, op0, op1, *toks, lane=None):
            return (lane or DV).do(lambda e: e.tensor_scalar(o, i, s1, s2, op0, op1), *toks)

        def ts1(o, i, s1, op0, *toks, lane=None):
            return (lane or DV).do(lambda e: e.tensor_scalar(o, i, s1, None, op0), *toks)

        def tt(o, a, b, op, *toks, lane=None):
            return (lane or DV).do(lambda e: e.tensor_tensor(o, a, b, op), *toks)

        def stt(o, a, s, b, op0, op1, *toks):
            return DV.do(lambda e: e.scalar_tensor_tensor(out=o, in0=a, scalar=s, in1=b, op0=op0, op1=op1), *toks)

        def cpy(o, i, *toks, lane=None):
            return (lane or DV).do(lambda e: e.tensor_copy(o, i), *toks)

        def red(o, i, op, *toks, negate=False):
            return DV.do(lambda e: e.tensor_reduce(o, i, AX, op, negate=negate), *toks)

        def load(off, item, free):
            name, h, _ = item
            return SP.dma(AR[:, off:off + 2048], dram["wpack"][SLOT[name], :, 2048 * h:2048 * h + 2048], free)

        def split(src, dst, w, tok, free):
            a = act(parts(dst, w), AR[:, src:src + w], ACT.Copy, tok, free)
            d = tt(parts(dst + w, w), AR[:, src:src + w], parts(dst, w).bitcast(F32), ALU.subtract, a, tok)
            return [a, d]

        st = Stream(load, split)
        st.places([WRo, WRo + 2048], [WRo + 4096 + 2048 * i for i in range(4)])
        yfree = [[]]

        def yload(name):
            w = AR[:, WRo + 12288:WRo + 16384]
            return cut(w, 4), SP.dma(w, dram["wpack"][SLOT[name]], yfree[0])

        t_x = [SP.dma(X[:, i, :], dram["x"][128 * i:128 * i + 128, :]) for i in range(4)]
        t_cp = AC.dma(CP, dram["cols"])
        t_cc = AC.dma(CC, dram["consts"])
        t_rr = AC.dma(RR, dram["rows"].to_broadcast([128, NROW]))
        t_ws = AC.dma(WS, dram["wsmall"])
        half = cc("half")
        st.until(SWITCH[2], 0)

        def rstd(ss, n, width, *toks):
            a = ts(ss, ss, 1.0 / width, EPS, ALU.mult, ALU.add, *toks, lane=PO)
            return tt(ss, ss, half[:, 0:n], ALU.pow, a, t_cc, lane=PO)

        class Norm:

            def __init__(self, src, n, g, hi, lo, xn, free=None, lo_free=None):
                self.src, self.n, self.g, self.hi, self.lo, self.xn = src, n, g, hi, lo, xn
                self.free, self.lo_free = free, lo_free
                self.ss, self.scaled, self.at = col(n), [None] * n, {}

            def square(self, i, *toks):
                toks = list(toks)
                s = self.ss[:, i:i + 1]
                self.at[i] = rstd(s, 1, 1024, act(self.xn[:, i, :], self.src[:, i, :], ACT.Square, toks, self.free,
                                                  accum_out=s)), toks

            def scale(self, i):
                r, toks = self.at[i]
                self.scaled[i] = ts1(self.xn[:, i, :], self.src[:, i, :], self.ss[:, i:i + 1], ALU.mult, r, toks)

            def turn(self):
                done = []
                for k in range(8):
                    b, bt, bk = bank()
                    for i in range(self.n):
                        p = tr(b[:, 128 * i:128 * i + 128], self.xn[:, i, 128 * k:128 * k + 128], self.scaled[i], bt,
                               t_cc, inc=(i == self.n - 1))
                    o, w = self.hi[k], 128 * self.n
                    e = act(o, b[:, 0:w], ACT.Identity, p, t_cp, scale=cp(self.g, k))
                    l = stt(self.lo[k], b[:, 0:w], cp(self.g, k), o.bitcast(F32), ALU.mult, ALU.subtract, e,
                            self.lo_free)
                    banks.give(bk, l)
                    done.append(l)
                return done

        def products(o, ws, xs, first, last, *toks):
            (wh, wl), (xh, xl) = ws, xs
            mm(o, wh, xh, first, False, *toks)
            mm(o, wh, xl, False, False)
            return mm(o, wl, xh, False, last, inc=last)

        def tile_q(name, hi, lo, n, toks):
            off, w, wt, done = st.get(name)
            wh, wl = cut(parts(off, w), 8), cut(parts(off + w, w), 8)
            b, bt, bk = bank()
            for k in range(8):
                p = products(b[:, 0:n], (wh[:, k, :], wl[:, k, :]), (hi[k], lo[k]), k == 0, k == 7,
                             bt, wt, toks)
            done(p)
            return b, p, bk

        def tiles_h(name, hi, lo, n, toks):
            bs = [bank() for _ in range(n)]
            out_ = []
            for u in range(2):
                off, w, wt, done = st.get(name)
                wh, wl = cut(parts(off, w), 4), cut(parts(off + w, w), 4)
                for i, (b, bt, bk) in enumerate(bs):
                    c = slice(128 * i, 128 * i + 128)
                    for k in range(4):
                        p = products(b, (hi[4 * u + k][:, c], lo[4 * u + k][:, c]), (wh[:, k, :], wl[:, k, :]),
                                     u + k == 0, u == 1 and k == 3, bt, wt, toks)
                    if u:
                        out_.append((b, p, bk))
                    elif i == n - 1:
                        p = PE.mark()
                done(p)
            return out_

        def tile_t(w, wt, kt, c, rhs, n, toks):
            b, bt, bk = bank()
            for k in range(kt):
                p = mm(b[:, 0:n], w[:, k, c:c + 128], rhs[:, k, 0:n], k == 0, k == kt - 1, bt, wt, toks,
                       inc=(k == kt - 1))
            return b, p, bk

        def rows_norm_add(rows, gt, free, t_x, norm, store):
            done, at = [], {}
            tmp = norm.xn

            def squares(i):
                ss = col(4)
                o = tmp[:, i, :]
                a = [act(o[:, 512 * h:512 * h + 512], b, ACT.Square, p, free, accum_out=ss[:, h:h + 1])
                     for h, (b, p, bk) in enumerate(rows[i])]
                s = tt(ss[:, 2:3], ss[:, 0:1], ss[:, 1:2], ALU.add, a, lane=PO)
                at[i] = ss[:, 2:3], rstd(ss[:, 2:3], 1, 1024, s)

            def add(i):
                s, r = at[i]
                o = tmp[:, i, :]
                adds = []
                ms = [stt(o[:, 512 * h:512 * h + 512], b, s, GB[:, 512 * h:512 * h + 512], ALU.mult, ALU.mult, r, gt)
                      for h, (b, p, bk) in enumerate(rows[i])]
                for m, (b, p, bk) in zip(ms, rows[i]):
                    banks.give(bk, m)
                done_i = tt(X[:, i, :], X[:, i, :], o, ALU.add, ms, t_x[i])
                done.append(done_i)
                norm.lo_free.append(PO.dma(store[128 * i:128 * i + 128, :], X[:, i, :], done_i))
                norm.square(i, done_i)

            squares(0)
            for i in range(4):
                if i == 0:
                    squares(1)
                add(i)
                if i < 2:
                    squares(i + 2)
                if i:
                    norm.scale(i - 1)
            norm.scale(3)
            return done

        f = Fo
        AT, QT, KT, QM = (cut(area(f + 2048 * i, 2048), 4) for i in range(4))
        VV = cut(area(f + 8192, 2048), 4)
        MK = cut(area(f + 10240, 1024), 4)
        MV = cut(area(f + 11264, 1024), 2)
        SK = cut(area(f + 12288, 1024), 2)
        PB = cut(area(f + 13312, 2560), 2)
        PTo = f + 15872
        GT = cut(area(f + 17920, 1024), 2)
        BV = area(f + 17920, 640)
        PT = cut(area(PTo, 2048), 4)
        MEMR = cut(area(f + 13312, 2048), 2)
        MEMN = cut(area(PTo, 2048), 2)
        MH, ML = ([parts(o + 256 * k, 256) for k in range(8)] for o in (MGo, MGo + 2048))
        CCB = cut(area(MGo + 2048, 2048), 4)

        t_mem = [PO.dma(MEMR[:, i, :], dram["mem"][128 * i:128 * i + 128, :]) for i in range(2)]
        t_oh = PO.dma(GB[0:32, 0:512], dram["onehot"])
        t_rb = PO.dma(GB[0:32, 512:520], dram["rel_bias"])

        pre = Norm(X, 4, "g_pre_mix", HH, HL, XN)
        for i in range(4):
            pre.square(i, t_x[i])
        for i in range(4):
            pre.scale(i)
        pre_m = Norm(MEMR, 2, "g_mem", MH, ML, MEMN)
        for i in range(2):
            pre_m.square(i, t_mem)
        for i in range(2):
            pre_m.scale(i)
        st.until(SWITCH[2], SWITCH[0])
        t_ht = pre.turn()

        b, bt, bk = bank()
        p = mm(b[0:8, :], GB[0:32, 512:520], GB[0:32, 0:512], True, True, bt, t_oh, t_rb, inc=True)
        e1 = DV.do(lambda e: e.memset(BV[0:8, 512:640], NEG))
        e2 = cpy(BV[0:8, 0:512], b[0:8, :], p)
        banks.give(bk, e2)
        t_bv = PO.dma(dram["bvec"], BV[0:8, 0:640].unsqueeze(1).to_broadcast([8, 128, 640]), e1, e2)
        t_gb = PO.dma(GB, dram["gains"][0:1, :].to_broadcast([128, 1024]), p)

        t_mt = pre_m.turn()

        def proj_t(name, dst, hi, lo, n, toks):
            out_ = []
            for j in range(4):
                b, p, bk = tile_q(name, hi, lo, n, toks)
                if j % 2:
                    e = cpy(dst[:, j, 0:n], b[:, 0:n], p)
                else:
                    e = act(dst[:, j, 0:n], b[:, 0:n], ACT.Copy, p)
                banks.give(bk, e)
                out_.append(e)
            return out_

        t_q = proj_t("q", QT, HH, HL, 512, t_ht)
        t_k = proj_t("k", KT, HH, HL, 512, t_ht)
        t_v = []
        for i, (b, p, bk) in enumerate(tiles_h("v", HH, HL, 4, t_ht)):
            e = act(VV[:, i, :], b, ACT.Copy, p)
            banks.give(bk, e)
            t_v.append(e)
        t_qm = proj_t("qm", QM, HH, HL, 512, t_ht)
        t_mk = proj_t("mk", MK, MH, ML, 256, t_mt)
        t_mv = []
        for i, (b, p, bk) in enumerate(tiles_h("mv", MH, ML, 2, t_mt)):
            e = act(MV[:, i, :], b, ACT.Copy, p)
            banks.give(bk, e)
            t_mv.append(e)
        mem_read = p

        t_o1 = []
        t_om = []
        pt_free = [[t_mt, PE.pending()]]
        p_free = [[t_mt, PE.pending()], [t_mt, PE.pending()]]

        def attention_1():
            sk_free = [[], []]
            for h in range(8):
                lo, t, s = 64 * (h % 2), h // 2, h % 2
                skew = bass.AP(dram["bvec"].tensor, h * 81920 + 127, [[639, 128], [1, 512]])
                t_sk = PO.dma(SK[:, s, :], skew, t_bv, sk_free[s])
                P = PB[:, s, :]
                at = [0, 128, 384, 768]
                nm, rs = col(4), col(4)
                last = []
                for i in range(4):
                    n = 128 * (i + 1)
                    b, bt, bk = bank()
                    p = mm(b[:, 0:n], QT[lo:lo + 64, t, 128 * i:128 * i + 128], KT[lo:lo + 64, t, 0:n], True, True,
                           bt, t_q, t_k, inc=True)
                    Pi = P[:, at[i]:at[i] + n]
                    a = stt(Pi, b[:, 0:n], 0.125, SK[:, s, 384 - 128 * i:512], ALU.mult, ALU.add, p, t_sk,
                            p_free[s])
                    banks.give(bk, a)
                    m = red(nm[:, i:i + 1], Pi, ALU.max, a, negate=True)
                    x = act(Pi, Pi, ACT.Exp, m, bias=nm[:, i:i + 1], accum_out=rs[:, i:i + 1])
                    last.append(x)
                sk_free[s] = [a]
                r = DV.do(lambda e, rs=rs: e.reciprocal(rs, rs), last)
                last = [ts1(P[:, at[i]:at[i] + 128 * (i + 1)], P[:, at[i]:at[i] + 128 * (i + 1)], rs[:, i:i + 1],
                            ALU.mult, r) for i in range(4)]
                yield
                ev = []
                for k in range(4):
                    b, bt, bk = bank()
                    for i in range(k, 4):
                        p = tr(b[:, 128 * i:128 * i + 128], P[:, at[i] + 128 * k:at[i] + 128 * k + 128], bt, last,
                               inc=(i == 3))
                    if k % 2:
                        e = cpy(PT[:, k, 128 * k:512], b[:, 128 * k:512], p, pt_free[0])
                    else:
                        e = act(PT[:, k, 128 * k:512], b[:, 128 * k:512], ACT.Copy, p, pt_free[0])
                    banks.give(bk, e)
                    ev.append(e)
                p_free[s] = [p]
                yield
                b, bt, bk = bank()
                for k in range(4):
                    p = mm(b[lo:lo + 64, 128 * k:512], VV[:, k, 64 * h:64 * h + 64], PT[:, k, 128 * k:512], k == 0,
                           k == 3, bt, ev[k], t_v, inc=(k == 3))
                pt_free[0] = [p]
                e = cpy(QT[lo:lo + 64, t, :], b[lo:lo + 64, :], p)
                banks.give(bk, e)
                t_o1.append(e)
                yield
            scale = 128.0 ** -0.5
            for h in range(4):
                P = cut(PB[:, h % 2, 0:1024], 4)
                nm, rs = col(4), col(4)
                last = []
                for q in range(2):
                    b, bt, bk = bank()
                    for i in range(2):
                        p = mm(b[:, 256 * i:256 * i + 256], QM[:, h, 256 * q + 128 * i:256 * q + 128 * i + 128],
                               MK[:, h, :], True, True, bt, t_qm, t_mk, inc=(i == 1))
                    m = red(nm[:, 2 * q:2 * q + 2], cut(b, 2), ALU.max, p, negate=True)
                    m = ts1(nm[:, 2 * q:2 * q + 2], nm[:, 2 * q:2 * q + 2], scale, ALU.mult, m)
                    for i in range(2):
                        x = act(P[:, 2 * q + i, :], b[:, 256 * i:256 * i + 256], ACT.Exp, m, p_free[h % 2],
                                bias=nm[:, 2 * q + i:2 * q + i + 1], scale=scale,
                                accum_out=rs[:, 2 * q + i:2 * q + i + 1])
                        last.append(x)
                    banks.give(bk, x)
                r = DV.do(lambda e, rs=rs: e.reciprocal(rs, rs), last)
                last = [ts1(P[:, i, :], P[:, i, :], rs[:, i:i + 1], ALU.mult, r) for i in range(4)]
                yield
                ev = []
                for k in range(2):
                    b, bt, bk = bank()
                    for i in range(4):
                        p = tr(b[:, 128 * i:128 * i + 128], P[:, i, 128 * k:128 * k + 128], bt, last, inc=(i == 3))
                    e = cpy(PT[:, k, :], b, p, pt_free[0]) if k else act(PT[:, k, :], b, ACT.Copy, p, pt_free[0])
                    banks.give(bk, e)
                    ev.append(e)
                p_free[h % 2] = [p]
                yield
                b, bt, bk = bank()
                for k in range(2):
                    p = mm(b, MV[:, k, 128 * h:128 * h + 128], PT[:, k, :], k == 0, k == 1, bt, ev, t_mv,
                           inc=(k == 1))
                pt_free[0] = [p]
                e = cpy(QM[:, h, :], b, p)
                banks.give(bk, e)
                t_om.append(e)
                yield

        mg_done = [[] for _ in range(8)]
        gt_free = [[t_bv], [t_bv]]
        gt_i = [0]

        def gated(k, bias, name, y, first, pair=None):
            b, p, bk = tile_q(name, HH, HL, 512, t_ht_now)
            g = gt_i[0] % 2
            gt_i[0] += 1
            kw = {} if bias is None else {"bias": bias}
            a = act(GT[:, g, :], b, ACT.Sigmoid, p, gt_free[g], **kw)
            banks.give(bk, a)
            yield
            for part in y[:-1]:
                part()
                yield
            yb, yp, yk = y[-1]()
            if first:
                m = tt(MG[:, k, :], GT[:, g, :], yb, ALU.mult, a, yp, mg_done[k])
                banks.give(yk, m)
                gt_free[g] = [m]
            else:
                m = tt(GT[:, g, :], GT[:, g, :], yb, ALU.mult, a, yp)
                banks.give(yk, m)
                m = tt(MG[:, k, :], MG[:, k, :], GT[:, g, :], ALU.add, m, mg_done[k])
                gt_free[g] = [m]
            if pair:
                hi, lo = pair[0][k], pair[1][k]
                h = act(hi, MG[:, k, :], ACT.Copy, m, pair[2])
                m = tt(lo, MG[:, k, :], hi.bitcast(F32), ALU.subtract, h, pair[2])
            mg_done[k] = [m]
            return p, yp

        def branch_1(yname, gname, bi, src, toks, first, pair=None):
            wy, wyt = yload(yname)
            for k in range(8):
                p, yp = yield from gated(k, cp("b_gate", 8 * bi + k), f"{gname}{k // 4}",
                                         [lambda: tile_t(wy, wyt, 4, 128 * k, src, 512, toks)], first, pair)
                yield
            yfree[0] = [yp]

        t_ht_now = t_ht
        u_done = [None] * 4
        a_done = [None] * 4

        def dense_1():
            tc = proj_t("cc", CCB, HH, HL, 512, t_ht + [mem_read])
            yield
            for j in range(4):
                b, p, bk = tile_q("cv", HH, HL, 512, t_ht)
                m = tt(CCB[:, j, :], CCB[:, j, :], b, ALU.mult, p, tc)
                banks.give(bk, m)
                u_done[j] = m
                c = [cp("conv_mix", 4 * q + j) for q in range(3)]
                m = ts1(AT[:, j, :], CCB[:, j, :], c[2], ALU.mult, m, t_cp)
                m = stt(AT[:, j, 1:512], CCB[:, j, 0:511], c[1], AT[:, j, 1:512], ALU.mult, ALU.add, m)
                m = stt(AT[:, j, 2:512], CCB[:, j, 0:510], c[0], AT[:, j, 2:512], ALU.mult, ALU.add, m)
                a_done[j] = m
                yield
            for j in range(4):
                b, p, bk = tile_q("cb", HH, HL, 512, t_ht)
                m = tt(AT[:, j, :], AT[:, j, :], b, ALU.mult, p, a_done[j])
                banks.give(bk, m)
                a_done[j] = m
                yield
            for k in range(8):
                mg_done[k] = [mem_read, a_done[3], t_mt]
            yield from branch_1("yconv", "ga", 0, AT, a_done, True)

        zipped(attention_1(), dense_1(), 1, 1)
        for _ in branch_1("yattn", "gb", 1, QT, t_o1, False):
            pass
        GP = [[parts(o, 512) for o in os] for os in (GHs, GLs)] + [snap()]
        for _ in branch_1("ymem", "gc", 2, QM, t_om, False, GP):
            pass

        def out_rows(names, pair, toks):
            bs = [[bank() for _ in range(2)] for _ in range(4)]
            rows = [[None, None] for _ in range(4)]
            for h, name in enumerate(names):
                for q in range(2):
                    off, w, wt, done = st.get(name)
                    wh, wl = cut(parts(off, w), 8), cut(parts(off + w, w), 8)
                    for i in range(4):
                        b, bt, bk = bs[i][h]
                        c = slice(128 * i, 128 * i + 128)
                        for k in range(8):
                            p = products(b[:, 256 * q:256 * q + 256], (pair[0][k][:, c], pair[1][k][:, c]),
                                         (wh[:, k, :], wl[:, k, :]), k == 0, k == 7, bt, wt, toks)
                        rows[i][h] = (b, p, bk)
                    done(p)
            return rows

        def reload(src, *toks):
            return [PO.dma(X[:, i, :], src[128 * i:128 * i + 128, :], *toks) for i in range(4)]

        t_xr = reload(dram["x"], snap())
        free = snap()
        norm = Norm(X, 4, "g_pre_ffn", HH, HL, cut(area(Fo + 13312, 4096), 4), free, [])
        t_x1 = rows_norm_add(out_rows(["out0", "out1"], GP, mg_done), t_gb, free, t_xr, norm, dram["x1d"])
        t_gb = PO.dma(GB, dram["gains"][1:2, :].to_broadcast([128, 1024]), t_x1)

        t_ht = norm.turn()
        FH, FL = ([parts(o, 512) for o in os] for os in (FHs, FLs))
        YB = cut(area(Fo + 13312, 4096), 8)
        start = snap()
        y_free = [start] * 8
        yi = 0
        ft_done = [None] * 22
        for s in range(11):
            half_y = {}
            for j in range(4):
                tix = 2 * s + j % 2 + (22 if j >= 2 else 0)
                b, p, bk = tile_q(f"up{s}", HH, HL, 512, t_ht)
                y, yk = YB[:, yi % 8, :], yi % 8
                yi += 1
                a = act(y, b, ACT.Identity, p, y_free[yk], t_cp, bias=cp("ffn_b", tix), scale=cp("ffn_w", 88 + tix))
                m = stt(y[:, 1:512], b[:, 0:511], cp("ffn_w", 44 + tix), y[:, 1:512], ALU.mult, ALU.add, a)
                m = stt(y[:, 2:512], b[:, 0:510], cp("ffn_w", tix), y[:, 2:512], ALU.mult, ALU.add, m)
                banks.give(bk, m)
                if j < 2:
                    half_y[j] = (y, act(y, y, ACT.Gelu_apprx_tanh, m), yk)
                else:
                    ya, ta, ka = half_y[j - 2]
                    m = tt(y, ya, y, ALU.mult, m, ta)
                    k = 2 * s + j - 2
                    h_ = act(FH[k], y, ACT.Copy, m, start)
                    l_ = tt(FL[k], y, FH[k].bitcast(F32), ALU.subtract, h_, start)
                    y_free[yk] = y_free[ka] = [h_, l_]
                    ft_done[k] = l_
        t_xr = reload(dram["x1d"], snap(), norm.lo_free)
        rows = [[bank() for _ in range(2)] for _ in range(4)]
        done_p = [[None, None] for _ in range(4)]
        units = []

        def down_row(i, k0):
            c = slice(128 * i, 128 * i + 128)
            for u, (off, w, wt, done) in enumerate(units):
                wh, wl = cut(parts(off, w), 2), cut(parts(off + w, w), 2)
                for k in range(k0 + 2 * u, k0 + 2 * u + 2):
                    for hf in range(2):
                        b, bt, bk = rows[i][hf]
                        d = slice(512 * hf, 512 * hf + 512)
                        p = products(b, (FH[k][:, c], FL[k][:, c]), (wh[:, k % 2, d], wl[:, k % 2, d]), k == 0,
                                     k == 21, bt, wt, ft_done[k])
                        done_p[i][hf] = p

        for u in range(9):
            units.append(st.get(f"down{u // 2}"))
            for i in range(4):
                down_row(i, 2 * u)
            units.pop()[3](PE.mark())
        units += [st.get("down4"), st.get("down5")]
        for i in range(4):
            down_row(i, 18)
        for unit in units:
            unit[3](done_p[3][1])
        rows = [[(rows[i][h][0], done_p[i][h], rows[i][h][2]) for h in range(2)] for i in range(4)]
        norm = Norm(X, 4, "norm1_g", HH, HL, YB.rearrange("p (i a) c -> p i (a c)", a=2), y_free, [])
        t_x2 = rows_norm_add(rows, t_gb, norm.free, t_xr, norm, dram["x2d"])

        t_ht = norm.turn()
        t_ht_now = t_ht
        f = Fo
        DT, DA, ACU, EXA, DTE, CDE = (area(f + 128 * i, 128) for i in range(6))
        f += 768
        CB = area(f, 512)
        PV = area(f + 512, 512)
        BR = cut(area(f + 1024, 512), 4)
        XS = cut(area(f + 1536, 2048), 4)
        XD = cut(area(f + 3584, 2048), 4)
        XE = cut(area(f + 5632, 1024), 2)
        EB = cut(area(f + 6656, 2048), 2)
        T1 = cut(area(f + 8704, 1024), 2)
        ZB = cut(area(f + 9728, 1024), 2)
        T2 = area(f + 10752, 512)
        YT = cut(area(Fo + 12032, 8192), 16)
        SNG = cut(GB, 2)
        BT, CT = cut(area(MGo, 2048), 4), cut(area(MGo + 2048, 2048), 4)
        start = snap()
        dtv = cut(DT, 4)
        h32 = lambda name: rr(name).unsqueeze(1).to_broadcast([128, 4, 32])

        WD, D0 = area(f + 1536, 1024), area(f + 6656, 512)
        t_wd = SP.dma(WD, dram["wdt"], start)
        t_bt, t_ct = [], []

        def xbc(name, dst, base, out_, at, then):
            for j in range(4):
                b, p, bk = tile_q(name, HH, HL, 512, t_ht)
                if j == at:
                    then()
                m, s = conv_silu(b, p, base + j, dst[:, j, :], start)
                banks.give(bk, m)
                out_.append(s)

        def conv_silu(b, p, tix, y, toks):
            a = act(y, b, ACT.Identity, p, toks, t_cp, bias=cp("conv_b", tix), scale=cp("conv_w", 72 + tix))
            m = a
            for q in range(1, 4):
                m = stt(y[:, q:512], b[:, 0:512 - q], cp("conv_w", 24 * (3 - q) + tix), y[:, q:512], ALU.mult,
                        ALU.add, m)
            return m, act(y, y, ACT.Silu, m)

        wdh, wdl = parts(f + 3584, 1024), parts(f + 4608, 1024)
        t_wds = []

        def split_wd():
            a = act(wdh, WD, ACT.Copy, t_wd, start)
            t_wds.append(tt(wdl, WD, wdh.bitcast(F32), ALU.subtract, a))

        xbc("bm", BT, 16, t_bt, 1, split_wd)
        b, bt, bk = bank()
        for k in range(8):
            p = products(b, (cut(wdh, 8)[:, k, :], cut(wdl, 8)[:, k, :]), (HH[k], HL[k]), k == 0, k == 7, bt, t_ht,
                         t_wds)
        e = cpy(D0, b, p, start)
        banks.give(bk, e)
        b, bt, bk = bank()
        for i in range(4):
            p = tr(b[:, 128 * i:128 * i + 128], D0[:, 128 * i:128 * i + 128], bt, e, inc=(i == 3))
        e = tt(dtv, cut(b, 4)[:, :, 0:32], h32("dt_bias"), ALU.add, p, t_rr, start)
        banks.give(bk, e)
        a = act(DA, DT, ACT.Abs, e, start)
        a = act(DA, DA, ACT.Exp, a, scale=-1.0)
        a = act(DA, DA, ACT.Ln, a, bias=1.0)
        m = ts1(DT, DT, 0.0, ALU.max, a)
        m = tt(DT, DT, DA, ALU.add, m)
        t_dt = m
        na = col(32)
        a = act(na, rr("a_log"), ACT.Exp, t_rr)
        m = ts1(na, na, -1.0, ALU.mult, a)
        m = tt(cut(DA, 4), dtv, na.unsqueeze(1).to_broadcast([128, 4, 32]), ALU.mult, m, t_dt)
        t_da = m

        def narrow():
            st.narrow(2, [WRo + 4096, WRo + 12288], PE.pending())
            st.until(SWITCH[2], SWITCH[1])

        xbc("cm", CT, 20, t_ct, 3, narrow)
        b, bt, bk = bank()
        p = mm(b[:, 0:128], cc("triu"), DA, True, True, bt, t_da, t_cc)
        p = mm(b[:, 128:256], cc("ones"), DA, True, True, inc=True)
        c1 = cpy(ACU, b[:, 0:128], p, start)
        c2 = tt(DTE, b[:, 128:256], ACU, ALU.subtract, c1, start)
        c3 = act(CDE, b[:, 128:256], ACT.Exp, c2, start)
        c4 = act(EXA, ACU, ACT.Exp, c1, start)
        c5 = act(DTE, DTE, ACT.Exp, c2)
        banks.give(bk, c3)
        t_acu, t_dec = c1, [c3, c4, c5]

        b4 = lambda ap, c, g: ap[:, 32 * c + 8 * g:32 * c + 8 * g + 8].unsqueeze(2).to_broadcast([128, 8, 64])
        h8 = lambda ap: ap.rearrange("p (h d) -> p h d", h=8)
        triu = cc("triu")
        t1_free, xe_free, eb_free = [start, start], [start, start], [start, start]
        zb_free, sng_free = [start, start], [start, start]
        yt_done = []
        t2_free = [start]
        grp_free = start

        def xs_rows(j, y, s, free, out_):
            b, bt, bk = bank()
            for c in range(4):
                q = tr(b[:, 128 * c:128 * c + 128], y[:, 128 * c:128 * c + 128], bt, s, inc=(c == 3))
            eb_free[j % 2] = [q]
            e = cpy(XS[:, :, 128 * j:128 * j + 128], cut(b, 4), q, free)
            banks.give(bk, e)
            out_.append(e)

        def finish(g, c, t1, o1, t_z, t_sn):
            o1 = tt(t1, t1, ZB[:, c % 2, :], ALU.mult, t_z, o1)
            ss = col(1)
            a = act(ZB[:, c % 2, :], t1, ACT.Square, o1, accum_out=ss)
            zb_free[c % 2] = [a]
            r = rstd(ss, 1, 512, a)
            o1 = stt(t1, t1, ss, SNG[:, g % 2, :], ALU.mult, ALU.mult, r, t_sn, a)
            sng_free[g % 2] = [o1]
            return g, c, t1, o1

        def turn(g, c, t1, o1):
            b, bt, bk = bank()
            for j in range(4):
                q = tr(b[:, 128 * j:128 * j + 128], t1[:, 128 * j:128 * j + 128], bt, o1, inc=(j == 3))
            t1_free[c % 2] = [q]
            e = act(YT[:, 4 * g:4 * g + 4, 128 * c:128 * c + 128], cut(b, 4), ACT.Copy, q, start)
            banks.give(bk, e)
            yt_done.append(e)

        todo = None
        for g in range(4):
            t_sn = PO.dma(SNG[:, g % 2, :], dram["sng"][0:1, 512 * g:512 * g + 512].to_broadcast([128, 512]),
                          sng_free[g % 2])
            t_xs = []
            held = None
            for j in range(4):
                b, p, bk = tile_q(f"xs{g}", HH, HL, 512, t_ht)
                y = EB[:, j % 2, 0:512]
                m, s = conv_silu(b, p, 4 * g + j, y, eb_free[j % 2])
                banks.give(bk, m)
                if held:
                    xs_rows(*held)
                held = (j, y, s, grp_free, t_xs)
                if j == 0 and todo:
                    todo = finish(*todo)
                if j == 1 and todo:
                    turn(*todo)
                    todo = None
            b, bt, bk = bank()
            for c in range(4):
                q = tr(b[:, 128 * c:128 * c + 128], BT[:, g, 128 * c:128 * c + 128], bt, t_bt, inc=(c == 3))
            t_br = act(BR, cut(b, 4), ACT.Copy, q, grp_free)
            banks.give(bk, t_br)
            b, bt, bk = bank()
            for c in range(4):
                q = mm(b[:, 128 * c:128 * c + 128], BT[:, g, 128 * c:128 * c + 128],
                       CT[:, g, 128 * c:128 * c + 128], True, True, bt, t_bt, t_ct, inc=(c == 3))
            t_cb = tt(cut(CB, 4), cut(b, 4), triu.unsqueeze(1).to_broadcast([128, 4, 128]), ALU.mult, q, grp_free)
            banks.give(bk, t_cb)
            wz = [st.get(f"z{g}") for _ in range(2)]
            t_pv = None
            def prepare(c):
                eb = EB[:, c % 2, :]
                rows = []
                for hh in range(2):
                    b, bt, bk = bank()
                    for h in range(4):
                        o = 32 * c + 8 * g + 4 * hh + h
                        q = mm(b[:, 128 * h:128 * h + 128], DA[:, o:o + 1].to_broadcast([128, 128]), triu, True,
                               True, bt, t_da, inc=(h == 3))
                    rows.append((b, q, bk))
                return eb, rows

            def exponents(c, eb, rows):
                out_ = []
                for hh, (b, q, bk) in enumerate(rows):
                    for h in range(4):
                        o = 32 * c + 8 * g + 4 * hh + h
                        m = ts(eb[:, 512 * hh + 128 * h:512 * hh + 128 * h + 128], b[:, 128 * h:128 * h + 128],
                               ACU[:, o:o + 1], 0.0, ALU.subtract, ALU.min, q, t_acu, eb_free[c % 2])
                    banks.give(bk, m)
                    eh = eb[:, 512 * hh:512 * hh + 512]
                    out_.append((eh, act(eh, eh, ACT.Exp, m)))
                return out_

            def weigh(c, halves):
                t_e = None
                if c < 3:
                    t_e = tt(h8(XE[:, c % 2, :]), h8(XD[:, c, :]), b4(DTE, c, g), ALU.mult, t_xd, t_dec,
                             xe_free[c % 2])
                return t_e, [tt(cut(eh, 4), cut(eh, 4), CB[:, 128 * c:128 * c + 128].unsqueeze(1)
                                .to_broadcast([128, 4, 128]), ALU.mult, a, t_cb) for eh, a in halves]

            eb, rows = prepare(0)
            xs_rows(*held)
            held = None
            ex = exponents(0, eb, rows)
            t_xd = [tt(h8(XD[:, n, :]), h8(XS[:, n, :]), b4(DT, n, g), ALU.mult, t_xs, t_dt, grp_free)
                    for n in range(4)]
            t_xe, t_m = weigh(0, ex)
            for c in range(4):
                eb = EB[:, c % 2, :]
                zb, zbt, zk = bank()
                tc = slice(128 * c, 128 * c + 128)
                for k in range(8):
                    off, zw, wt, done = wz[k // 4]
                    zp = products(zb, (HH[k][:, tc], HL[k][:, tc]),
                                  (cut(parts(off, zw), 4)[:, k % 4, :], cut(parts(off + zw, zw), 4)[:, k % 4, :]),
                                  k == 0, k == 7, zbt, wt, t_ht)
                if c == 3:
                    for z_ in wz:
                        z_[3](zp)
                if c < 3:
                    ebn, rows = prepare(c + 1)
                t_z = act(ZB[:, c % 2, :], zb, ACT.Silu, zp, zb_free[c % 2])
                banks.give(zk, t_z)
                if c < 3:
                    ex = exponents(c + 1, ebn, rows)
                if todo:
                    todo = finish(*todo)
                t1 = T1[:, c % 2, :]
                if c:
                    b, bt, bk = bank()
                    q = mm(b, CT[:, g, 128 * c:128 * c + 128], PV, True, True, bt, t_pv, t_ct, inc=True)
                    off_read = q
                    o1 = tt(h8(t1), h8(b), b4(EXA, c, g), ALU.mult, q, t_dec, t1_free[c % 2])
                    banks.give(bk, o1)
                t_cs = None
                if c < 3:
                    bs, bst, bsk = bank()
                    t_cs = mm(bs, BR[:, c, :], XE[:, c % 2, :], True, True, bst, t_br, t_xe, inc=True)
                    xe_free[c % 2] = [t_cs]
                b, bt, bk = bank()
                for h in range(8):
                    q = mm(b[:, 64 * h:64 * h + 64], eb[:, 128 * h:128 * h + 128], XD[:, c, 64 * h:64 * h + 64],
                           True, True, bt, t_m, t_xd, inc=(h == 7))
                eb_free[c % 2] = [q]
                if todo:
                    turn(*todo)
                if c < 3:
                    if c == 0:
                        t_pv = cpy(PV, bs, t_cs, grp_free)
                    else:
                        m = tt(h8(PV), h8(PV), b4(CDE, c, g), ALU.mult, t_pv, off_read, t_dec)
                        t_pv = tt(PV, PV, bs, ALU.add, m, t_cs)
                    banks.give(bsk, t_pv)
                if c:
                    o1 = tt(t1, t1, b, ALU.add, q, o1)
                else:
                    o1 = cpy(t1, b, q, t1_free[0])
                banks.give(bk, o1)
                d8 = rr("d_skip")[:, 8 * g:8 * g + 8].unsqueeze(2).to_broadcast([128, 8, 64])
                m = tt(h8(T2), h8(XS[:, c, :]), d8, ALU.mult, t_xs, t_rr, t2_free[0], lane=PO)
                o1 = tt(t1, t1, T2, ALU.add, m, o1)
                t2_free[0] = [o1]
                todo = (g, c, t1, o1, t_z, t_sn)
                if c < 3:
                    t_xe, t_m = weigh(c + 1, ex)
                st.pump()
            grp_free = snap()
        st.places(parts=[WRo + 4096 + 2048 * i for i in range(4)], free=PE.pending())
        st.until(SWITCH[2], SWITCH[2])
        todo = finish(*todo)
        t_q0 = tiles_h("q0", HH, HL, 4, t_ht)
        turn(*todo)

        start = snap()
        f = Fo - 4096
        QKf = cut(area(f, 5120), 4)
        QK = area(f, 5120).rearrange("p (i h d) -> p i h d", i=4, h=20)
        OT = cut(area(f, 4096), 8)
        QT = cut(area(f + 5120, 4096), 8)
        KT = cut(area(f + 9216, 1024), 2)
        VV = cut(area(f + 10240, 1024), 4)
        LB = cut(area(f + 11264, 1792), 2)
        PTT = cut(area(f + 13056, 1792), 2)
        MKo = area(f + 14848, 896)
        COS, SIN, R1, R2 = (area(f + 15744 + 32 * i, 32) for i in range(4))
        TA, TB, TC = (area(f + 13056 + 160 * i, 160) for i in range(3))
        SQ = area(f + 11264, 1280)
        GT = SNG
        gt_free[0] = gt_free[1] = start
        mg_done = [[start] for _ in range(8)]
        t_mk2 = PO.dma(MKo, dram["mask2"], start)
        t_ps = PO.dma(IA[:, 0:4], dram["pos"])

        pf = col(4)
        m = cpy(pf, IA[:, 0:4], t_ps)
        v48 = lambda ap: ap.rearrange("p (i d) -> p i d", i=4)
        m = tt(v48(R1), pf.unsqueeze(2).to_broadcast([128, 4, 8]), cc("invf").unsqueeze(1).to_broadcast([128, 4, 8]),
               ALU.mult, m, start)
        m = ts(R2, R1, 1.0 / (2 * math.pi), 12582912.0, ALU.mult, ALU.add, m)
        m = ts1(R2, R2, 12582912.0, ALU.subtract, m)
        c1 = 6.28125
        c2 = 0.0019350051879882812
        c3 = 2 * math.pi - c1 - c2
        for c in (c1, c2, c3):
            m = stt(R1, R2, -c, R1, ALU.mult, ALU.add, m)
        m = ts(R1, R1, math.pi - 1e-6, -math.pi + 1e-6, ALU.min, ALU.max, m)
        a = act(SIN, R1, ACT.Sin, m)
        a = act(COS, R1, ACT.Sin, a, scale=0.5)
        m = tt(COS, COS, COS, ALU.mult, a)
        t_cs = ts(COS, COS, -2.0, 1.0, ALU.mult, ALU.add, m)

        t_qk = []
        t_v = []
        for s, name in enumerate(("q0", "q1", "kv")):
            for i, (b, p, bk) in enumerate(tiles_h(name, HH, HL, 4, t_ht) if s else t_q0):
                if s < 2:
                    e = act(QKf[:, i, 512 * s:512 * s + 512], b, ACT.Copy, p, start)
                else:
                    e = cpy(QKf[:, i, 1024:1280], b[:, 0:256], p, start)
                    t_v.append(cpy(VV[:, i, :], b[:, 256:512], p, start))
                    e = t_v[-1]
                banks.give(bk, e)
                t_qk.append(e)
        st.shift()
        st.until(SWITCH[3], SWITCH[3])

        def dense_2():
            for k in range(8):
                at = {}

                def half_so(u):
                    if u == 0:
                        at["w"], at["b"] = st.get(f"so{k // 2}"), bank()
                    off, _, wt, done = at["w"]
                    b, bt, bk = at["b"]
                    w = cut(area(off, 2048), 16)
                    for d in range(8 * u, 8 * u + 8):
                        p = mm(b, w[:, d, :], YT[:, d, :], d == 0, d == 15, bt, wt, yt_done, inc=(d == 15))
                    if u:
                        done(p)
                    return b, p, bk
                yield from gated(k, None, f"gs{k // 4}", [lambda: half_so(0), lambda: half_so(1)], True)
                yield

        def attention_2():
            sq_done = start
            qn = []
            for i in range(4):
                a = act(SQ, QKf[:, i, :], ACT.Square, t_qk, sq_done)
                ss = col(20)
                m = red(ss, SQ.rearrange("p (h d) -> p h d", h=20), ALU.add, a)
                sq_done = [m]
                r = rstd(ss, 20, 64, m)
                m = tt(QK[:, i, :, :], QK[:, i, :, :], ss.unsqueeze(2).to_broadcast([128, 20, 64]), ALU.mult, r)
                m = tt(QK[:, i, 0:16, :], QK[:, i, 0:16, :], rr("q_g").unsqueeze(1).to_broadcast([128, 16, 64]),
                       ALU.mult, m)
                m = tt(QK[:, i, 16:20, :], QK[:, i, 16:20, :], rr("k_g").unsqueeze(1).to_broadcast([128, 4, 64]),
                       ALU.mult, m)
                va, vb, vc = (x.rearrange("p (h d) -> p h d", h=20) for x in (TA, TB, TC))
                ci = COS[:, 8 * i:8 * i + 8].unsqueeze(1).to_broadcast([128, 20, 8])
                si = SIN[:, 8 * i:8 * i + 8].unsqueeze(1).to_broadcast([128, 20, 8])
                q1, q2 = QK[:, i, :, 0:8], QK[:, i, :, 8:16]
                a1 = tt(va, q2, si, ALU.mult, m, t_cs, start)
                a2 = tt(vb, q1, si, ALU.mult, m, start)
                a3 = tt(vc, q2, ci, ALU.mult, m, start)
                a4 = tt(q1, q1, ci, ALU.mult, a2)
                a5 = tt(q1, q1, va, ALU.subtract, a4, a1)
                m = tt(q2, vb, vc, ALU.add, a3, a2)
                qn.append([a5, m])
                yield
                yield
            t_qt = []
            for t in (8, 0, 1, 2, 3, 9, 4, 5, 6, 7):
                b, bt, bk = bank()
                for i in range(4):
                    p = tr(b[:, 128 * i:128 * i + 128], QKf[:, i, 128 * t:128 * t + 128], bt, qn[i], inc=(i == 3))
                dst = QT[:, t, :] if t < 8 else KT[:, t - 8, :]
                e = cpy(dst, b, p, start) if t % 2 else act(dst, b, ACT.Copy, p, start)
                banks.give(bk, e)
                t_qt.append(e)
            qk_read = p
            l_free, pt_free2 = [qn, qn], [qn, qn]
            m3 = lambda ap: ap.rearrange("p (n k) -> p n k", k=256)

            def scores(pos):
                t, lo, kp, s = pos // 2, 64 * (pos % 2), pos // 8, pos % 2
                L = LB[:, s, :]
                nm, rs = col(4), col(4)
                scored = []
                for half_ in range(2):
                    b, bt, bk = bank()
                    o = 0
                    for n in ((0, 1), (2, 3))[half_]:
                        w_ = 128 if n == 0 else 256
                        k0 = 0 if n == 0 else 128 * (n - 1)
                        p = mm(b[:, o:o + w_], QT[lo:lo + 64, t, 128 * n:128 * n + 128],
                               KT[lo:lo + 64, kp, k0:k0 + w_], True, True, bt, t_qt, inc=(n % 2 == 1))
                        o += w_
                    lo_, hi_ = (0, 384) if half_ == 0 else (384, 896)
                    a = stt(L[:, lo_:hi_], b[:, 0:hi_ - lo_], 0.125, MKo[:, lo_:hi_], ALU.mult, ALU.add, p, t_mk2,
                            l_free[s])
                    banks.give(bk, a)
                    scored.append(a)
                m1 = red(nm[:, 0:1], L[:, 0:128], ALU.max, scored)
                m2 = red(nm[:, 1:4], m3(L[:, 128:896]), ALU.max, scored)
                m = ts(nm, nm, rr("sinks")[:, pos:pos + 1], -1.0, ALU.max, ALU.mult, m1, m2, t_rr)
                xs = []
                for n in range(4):
                    lo_, hi_ = (0, 128) if n == 0 else (128 + 256 * (n - 1), 128 + 256 * n)
                    xs.append(act(L[:, lo_:hi_], L[:, lo_:hi_], ACT.Exp, m, bias=nm[:, n:n + 1],
                                  accum_out=rs[:, n:n + 1]))
                xs.append(act(nm, nm, ACT.Exp, m, xs, bias=rr("sinks")[:, pos:pos + 1]))
                m = tt(rs, rs, nm, ALU.add, xs)
                m = DV.do(lambda e, rs=rs: e.reciprocal(rs, rs), m)
                d1 = ts1(L[:, 0:128], L[:, 0:128], rs[:, 0:1], ALU.mult, m)
                d2 = tt(m3(L[:, 128:896]), m3(L[:, 128:896]), rs[:, 1:4].unsqueeze(2).to_broadcast([128, 3, 256]),
                        ALU.mult, m, lane=PO)
                return [d1, d2]

            def values(pos, ready):
                t, lo, kp, s = pos // 2, 64 * (pos % 2), pos // 8, pos % 2
                kv = 2 * kp + pos % 2
                L = LB[:, s, :]
                ev = []
                for half_ in range(2):
                    b, bt, bk = bank()
                    lo_, n_ = (0, 3) if half_ == 0 else (384, 4)
                    for u in range(n_):
                        p = tr(b[:, 128 * u:128 * u + 128], L[:, lo_ + 128 * u:lo_ + 128 * u + 128], bt, ready,
                               inc=(u == n_ - 1))
                    e = act(PTT[:, s, lo_:lo_ + 128 * n_], b[:, 0:128 * n_], ACT.Copy, p, pt_free2[s])
                    banks.give(bk, e)
                    ev.append(e)
                l_free[s] = [p]
                yield
                b, bt, bk = bank()
                for n in range(4):
                    srcs = [(0, 0)] if n == 0 else [(n - 1, 128 + 256 * (n - 1)), (n, 256 + 256 * (n - 1))]
                    for u, (kb, o) in enumerate(srcs):
                        p = mm(b[lo:lo + 64, 128 * n:128 * n + 128], VV[:, kb, 64 * kv:64 * kv + 64],
                               PTT[:, s, o:o + 128], u == 0, u == len(srcs) - 1, bt, ev, t_v, inc=(n == 3))
                pt_free2[s] = [p]
                e = cpy(OT[lo:lo + 64, t, :], b[lo:lo + 64, :], p, qk_read)
                banks.give(bk, e)
                t_o2.append(e)

            ready = scores(0)
            yield
            for pos in range(16):
                nxt = scores(pos + 1) if pos < 15 else None
                yield from values(pos, ready)
                ready = nxt

        t_o2, held_w = [], []
        zipped(dense_2(), attention_2(), 1, 1)
        GP = [[parts(o, 512) for o in os] for os in (G2s[:8], G2s[8:])] + [snap()]
        st.own, st.own_i = [Fo + 12032, Fo + 16128], 0
        st.own_free = [GP[2], GP[2]]
        for k in range(8):
            def y():
                if k % 2 == 0:
                    held_w[:] = st.get(f"ao{k // 4}")
                off, _, wt, done = held_w
                w = cut(area(off + 1024 * (k % 2), 1024), 8)
                b, p, bk = tile_t(w, wt, 8, 0, OT, 512, t_o2)
                if k % 2:
                    done(p)
                return b, p, bk
            for _ in gated(k, None, f"gt{k // 4}", [y], False, GP):
                pass
        ht_free = snap()
        t_xr = reload(dram["x2d"], ht_free)
        t_gb = PO.dma(GB, dram["gains"][2:3, :].to_broadcast([128, 1024]), snap())
        XR, HR = cut(area(HTo, 4096), 4), MG
        ss = col(4)
        t_x3, t_h2, t_h2d = [], [], []

        def row_3(i):
            s = ss[:, i:i + 1]
            a = act(XR[:, i, :], X[:, i, :], ACT.Square, t_x3[2 * i:2 * i + 2], ht_free, accum_out=s)
            r = rstd(s, 1, 1024, a)
            m = stt(XR[:, i, :], X[:, i, :], s, GB, ALU.mult, ALU.mult, r, t_gb)
            t_h2.append(m)
            t_h2d.append(PO.dma(dram["h2d"][128 * i:128 * i + 128, :], XR[:, i, :], m))

        for i, halves in enumerate(out_rows(["oo0", "oo1"], GP, mg_done)):
            for h, (b, p, bk) in enumerate(halves):
                m = tt(X[:, i, 512 * h:512 * h + 512], X[:, i, 512 * h:512 * h + 512], b, ALU.add, p, t_xr)
                banks.give(bk, m)
                t_x3.append(m)
            if i:
                row_3(i - 1)
        row_3(3)

        t_16 = [cpy(BT16[:, 0:128], cc("stri"), t_cc), cpy(BT16[:, 128:256], cc("ones"), t_cc)]

        start = snap()
        GUs = [WRo + 4096 * k for k in range(5)] + [HTo]
        DNs = [WRo + 20480 + 2048 * k for k in range(6)]
        XB = cut(area(MGo, 2048), 2)
        XT = cut(area(MGo + 2048, 2048), 2)
        f = WRo + 32768
        HS, HD, YE = cut(area(f, 512), 2), cut(area(f + 512, 512), 2), cut(area(f + 1024, 2048), 2)
        gur, dnr = Ring(6), Ring(6)
        gur.free = [[start] for _ in range(5)] + [None]
        dnr.free = [[start] for _ in range(6)]
        wexp = dram["wexp"]

        def eload(ring, places, width, lo, n):
            k, toks = ring.take()
            w = AR[:, places[k]:places[k] + width]
            return w, SP.dma(w, wexp[n, :, lo:lo + width], toks), k

        n_pre = 5
        pre = [(eload(gur, GUs, 4096, 0, n), eload(dnr, DNs, 2048, 4096, n)) for n in range(n_pre)]
        t_ht = []
        for k in range(8):
            b, bt, bk = bank()
            for i in range(4):
                p = tr(b[:, 128 * i:128 * i + 128], XR[:, i, 128 * k:128 * k + 128], bt, t_h2[i], inc=(i == 3))
            e = act(HR[:, k, :], b, ACT.Copy, p) if k % 2 else cpy(HR[:, k, :], b, p)
            banks.give(bk, e)
            t_ht.append(e)
        wr = cut(WS[:, 256:832], 8)
        RL = cut(area(f, 288), 4)
        b, bt, bk = bank()
        for i in range(4):
            for k in range(8):
                p = mm(b[:, 72 * i:72 * i + 72], HR[:, k, 128 * i:128 * i + 128], wr[:, k, :], k == 0, k == 7, bt,
                       t_ht, t_ws, inc=(i == 3 and k == 7))
        m = tt(RL, cut(b[:, 0:288], 4), rr("b_r").unsqueeze(1).to_broadcast([128, 4, 72]), ALU.add, p, t_rr, start)
        banks.give(bk, m)
        f += 288
        GL = RL[:, :, 0:8]
        OG, VG = (area(f + 32 * i, 32).rearrange("p (i g) -> p i g", i=4) for i in range(2))
        f += 64
        EL, O1, O2, V1 = (area(f + 256 * i, 256).rearrange("p (i g) -> p i g", i=4) for i in range(4))
        f += 1024
        bc = lambda ap, n: ap.unsqueeze(2).to_broadcast([128, 4, n])
        row = lambda ap, n: ap.unsqueeze(1).to_broadcast([128, 4, n])
        gm, gs, v1, v2, ix = col(4), col(4), col(4), col(4), col(4)
        m = red(gm, GL, ALU.max, m)
        m2 = tt(VG, GL, bc(gm, 8), ALU.subtract, m, start)
        a = act(VG, VG, ACT.Exp, m2)
        m2 = red(gs, VG, ALU.add, a)
        m2 = DV.do(lambda e: e.reciprocal(gs, gs), m2)

        def first(oh, vals, mx, rev, n, *toks):
            m = tt(oh, vals, bc(mx, n), ALU.is_equal, *toks)
            m = tt(oh, oh, row(rev, n), ALU.mult, m, t_cc)
            m = red(ix, oh, ALU.max, m)
            return tt(oh, oh, bc(ix, n), ALU.is_equal, m)

        m = first(OG, GL, gm, cc("rev8"), 8, m, start)
        m = ts(VG, OG, -1.0, 1e30, ALU.add, ALU.mult, m, m2)
        el4 = lambda ap: ap.rearrange("p i (g e) -> p i g e", g=8)
        for i in range(4):
            mi = tt(el4(EL)[:, i], RL[:, i, 8:72].rearrange("p (g e) -> p g e", g=8),
                    VG[:, i, :].unsqueeze(2).to_broadcast([128, 8, 8]), ALU.add, m, start)
        m = red(v1, EL, ALU.max, mi)
        m = first(O1, EL, v1, cc("rev64"), 64, m, start)
        m = ts1(V1, O1, -2e30, ALU.mult, m, start)
        m = tt(V1, EL, V1, ALU.add, m)
        m = red(v2, V1, ALU.max, m)
        m = first(O2, V1, v2, cc("rev64"), 64, m, start)
        t_oh2 = m
        m = tt(v2, v2, v1, ALU.subtract, m)
        a = act(v2, v2, ACT.Exp, m)
        m = ts1(v1, v2, 1.0, ALU.add, a)
        m = DV.do(lambda e: e.reciprocal(v1, v1), m)
        m = tt(v1, v1, gs, ALU.mult, m, m2)
        t_gate = tt(v2, v2, v1, ALU.mult, m)
        V16 = BT16[:, 256:512].rearrange("p (i g) -> p i g", i=4)
        m = tt(V16, O1, O2, ALU.add, t_oh2)
        b, bt, bk = bank()
        for i in range(4):
            for u in range(i + 1):
                p = mm(b[:, 64 * i:64 * i + 64], BT16[:, 0:128] if u == i else BT16[:, 128:256], V16[:, u, :], u == 0,
                       u == i, bt, m, t_16)
        for u in range(4):
            p = mm(b[:, 256:320], BT16[:, 128:256], V16[:, u, :], u == 0, u == 3, inc=(u == 3))
        PO_ = EL
        c1 = cpy(PO_, b[:, 0:256].rearrange("p (i e) -> p i e", i=4), p)
        CNT, NB, CA, CB2 = (area(f + 64 * i, 64) for i in range(4))
        f += 256
        m = ts(CNT, b[:, 256:320], -float(CAP), 0.0, ALU.add, ALU.max, p, start)
        banks.give(bk, m)
        m = ts1(NB, CNT, 0.5, ALU.is_gt, m)
        for q in range(1, 4):
            m = ts1(CA, CNT, 128.0 * q + 0.5, ALU.is_gt, m)
            m = tt(NB, NB, CA, ALU.add, m)
        m = cpy(CA, NB, m)
        a_, b_ = CA, CB2
        for q in range(6):
            st = 1 << q
            m1 = cpy(b_[:, 0:st], a_[:, 0:st], m)
            m = tt(b_[:, st:64], a_[:, st:64], a_[:, 0:64 - st], ALU.add, m1)
            a_, b_ = b_, a_
        incl = a_
        m = tt(NB, incl, NB, ALU.subtract, m)
        m = ts(NB, NB, 128.0, float(NST - CAP), ALU.mult, ALU.add, m)
        S1, S2 = (area(f + 256 * i, 256).rearrange("p (i g) -> p i g", i=4) for i in range(2))
        f += 512
        m1 = tt(S1, PO_, row(cc("e32"), 64), ALU.add, c1, start)
        m2 = tt(S2, PO_, row(NB, 64), ALU.add, m, c1, start)
        m1 = tt(S1, S1, S2, ALU.subtract, m1, m2)
        m2 = ts1(PO_, PO_, CAP - 0.5, ALU.is_lt, m1)
        m1 = tt(S1, S1, PO_, ALU.mult, m2)
        m1 = tt(S1, S1, S2, ALU.add, m1)
        sl = col(8)
        for j, oh in enumerate((O1, O2)):
            m = tt(S2, S1, oh, ALU.mult, m1)
            m1 = red(sl[:, 4 * j:4 * j + 4], S2, ALU.add, m)
        t_sl = cpy(IA[:, 8:16], sl, m1)
        BEF = area(HTo, 31 * 64).rearrange("p (b e) -> p b e", b=31)
        bef = col(31)
        q1 = DV.do(lambda e: e.tensor_tensor(BEF, incl.unsqueeze(1).to_broadcast([128, 31, 64]),
                                             cc("iob").unsqueeze(2).to_broadcast([128, 31, 64]), ALU.is_le), t_h2d, p, m)
        q1 = red(bef, BEF, ALU.add, q1)
        q1 = ts1(bef, bef, 63.0, ALU.min, q1)
        t_be = cpy(IA[:, 64:95], bef, q1)
        t_be = cpy(IA[:, 95:96], incl[:, 63:64], t_be)

        z = PO.do(lambda e: e.memset(IA[:, 16:63], 4096))
        t_z = PO.dma(dram["tab"].rearrange("(p c) o -> p (c o)", p=128), IA[:, 16:63], z)
        t_tk = PO.dma(IA[:, 96:104], dram["tokid"])
        t_sc = []
        for j in range(2):
            for i in range(4):
                idx, val = IA[:, 8 + 4 * j + i:9 + 4 * j + i], IA[:, 96 + 4 * j + i:97 + 4 * j + i]
                t_sc.append(PO.dma(None, None, t_z, t_tk, t_sl, how=lambda e, idx=idx, val=val: e.indirect_dma_start(
                    dram["tab"], bass.IndirectOffsetOnAxis(ap=idx, axis=0), val, None, bounds_check=NSLOT - 1,
                    oob_is_err=False)))
        t_tab = PO.dma(IA[:, 16:63], dram["tab"].rearrange("(b p) o -> p (b o)", p=128), t_sc)
        m = DV.do(lambda e: e.tensor_scalar(IA[:, 128:175], IA[:, 16:63], 1, None, ALU.logical_shift_right), t_tab)
        t_tok = ts1(IA[:, 128:175], IA[:, 128:175], 511.0, ALU.min, m)

        after = snap()

        def expert(wid, gus, dns, xb, t_xb, fr, xt, hs, hd, ye):
            ne = len(gus)
            ev = []
            for hf in range(2):
                b, bt, bk = bank()
                for k in range(4):
                    p = tr(b[:, 128 * k:128 * k + 128], xb[:, 512 * hf + 128 * k:512 * hf + 128 * k + 128], bt, t_xb,
                           inc=(k == 3))
                o = xt[:, 4 * hf:4 * hf + 4, :]
                e = act(o, cut(b, 4), ACT.Copy, p, fr["xt"]) if hf else cpy(o, cut(b, 4), p, fr["xt"])
                banks.give(bk, e)
                ev.append(e)
            fr["xb"] = [p]
            b, bt, bk = bank()
            t_gu, t_dn = [], []
            pairs = [range(ne)[j:j + 2] for j in range(0, ne, 2)]
            for pair in pairs:
                for k in range(8):
                    for j in pair:
                        w = cut(gus[j][0], 8)
                        p = mm(b[wid * j:wid * j + wid, :], xt[:, k, wid * j:wid * j + wid], w[:, k, :], k == 0,
                               k == 7, bt, ev, gus[j][1], inc=(k == 7 and j == pair[-1]))
                t_gu += [p] * len(pair)
            fr["xt"] = [p]
            a = act(hs, b[:, 0:256], ACT.Silu, p, fr["hs"])
            m = tt(hs, hs, b[:, 256:512], ALU.mult, a)
            banks.give(bk, m)
            b, bt, bk = bank()
            for q in range(2):
                p = tr(b[:, 128 * q:128 * q + 128], hs[:, 128 * q:128 * q + 128], bt, m, inc=(q == 1))
            fr["hs"] = [p]
            e = cpy(hd, cut(b[:, 0:256], 2), p, fr["hd"])
            banks.give(bk, e)
            ys = []
            b2 = [bank() for _ in range(2)]
            for pair in pairs:
                for hf in range(2):
                    b, bt, bk = b2[hf]
                    for q in range(2):
                        for j in pair:
                            w = cut(dns[j][0], 2)
                            p = mm(b[wid * j:wid * j + wid, :], hd[:, q, wid * j:wid * j + wid],
                                   w[:, q, 512 * hf:512 * hf + 512], q == 0, q == 1, bt, e, dns[j][1],
                                   inc=(q == 1 and j == pair[-1]))
                t_dn += [p] * len(pair)
            for hf in range(2):
                b, bt, bk = b2[hf]
                o = ye[:, 512 * hf:512 * hf + 512]
                y = act(o, b, ACT.Copy, p, fr["ye"]) if hf else cpy(o, b, p, fr["ye"])
                banks.give(bk, y)
                ys.append(y)
            fr["hd"] = [p]
            return t_gu, t_dn, ys

        t_ya = []
        frs = [{n: after for n in ("xb", "xt", "hs", "hd", "ye")} for _ in range(2)]

        def gather(blk):
            xb, tok = XB[:, blk % 2, :], IA[:, 128 + blk:129 + blk]
            return PO.dma(None, None, t_h2d, t_tok, frs[blk % 2]["xb"], how=lambda e: e.indirect_dma_start(
                xb, None, dram["h2d"], bass.IndirectOffsetOnAxis(ap=tok, axis=0), bounds_check=511,
                oob_is_err=False))

        t_g = gather(0)
        gur.free[5] = [after, t_g]
        for blk in range(16):
            s = blk % 2
            fr = frs[s]
            gu, dn = [], []
            for j in range(4):
                n = 4 * blk + j
                if n < n_pre:
                    gu.append(pre[n][0])
                    dn.append(pre[n][1])
                else:
                    gu.append(eload(gur, GUs, 4096, 0, n))
                    dn.append(eload(dnr, DNs, 2048, 4096, n))
            t_now, t_g = t_g, gather(blk + 1) if blk < 15 else None
            t_gu, t_dn, ys = expert(CAP, gu, dn, XB[:, s, :], t_now, fr, cut(XT[:, s, :], 8), HS[:, s, :],
                                    cut(HD[:, s, :], 2), YE[:, s, :])
            for j in range(4):
                gur.give(gu[j][2], t_gu[j])
                dnr.give(dn[j][2], t_dn[j])
            asg = IA[:, 16 + blk:17 + blk]
            t_y = PO.dma(None, None, ys, t_tab, how=lambda e, s=s, asg=asg: e.indirect_dma_start(
                dram["ya"], bass.IndirectOffsetOnAxis(ap=asg, axis=0), YE[:, s, :], None, bounds_check=1023,
                oob_is_err=False))
            fr["ye"] = [t_y]
            t_ya.append(t_y)

        outer = (PE, DV, AC, PO, SP)
        oend = [snap()]
        inner = tuple(Body(sem("l_" + n), [sem(f"l_{n}{i}") for i in range(k)])
                      for n, k in (("pe", 0), ("dve", 0), ("act", 0), ("pool", 2), ("sp", 2)))
        gain = {}
        for lane in inner:
            lane.gain, lane.rest = gain, None
        inner[3].rest, inner[4].rest = sem("rest_pool"), sem("rest_sp")
        PE, DV, AC, PO, SP = inner
        banks_outer, banks = banks, Ring(8)

        def dyn_idx(e, i):
            return e.tensor_copy(IA[:, 112:113], IA[:, bass.ds(i + 32, 1)])

        def dyn_tok(e, i):
            return e.tensor_copy(IA[:, 113:114], IA[:, bass.ds(i + 144, 1)])

        def load_w(e, i, w, lo, width):
            x = e.value_load(IA[0:1, bass.ds(i + 64, 1)], min_val=0, max_val=63)
            return e.dma_start(w, wexp[bass.ds(x, 1), :, lo:lo + width].rearrange("a p c -> (a p) c"))

        DV.n += 2
        DV.ops.append(lambda e, i: dyn_idx(e, i).then_inc(DVi.sem, 1))
        DV.ops.append(lambda e, i: dyn_tok(e, i).then_inc(DVi.sem, 1))
        DVi = DV
        t_ix = (DV.sem, 2)
        gw, dw = AR[:, GUs[0]:GUs[0] + 4096], AR[:, DNs[0]:DNs[0] + 2048]
        t_w1 = SP.dma(None, None, how=lambda e, i: load_w(e, i, gw, 0, 4096))
        t_w2 = SP.dma(None, None, how=lambda e, i: load_w(e, i, dw, 4096, 2048))
        t_g = PO.dma(None, None, t_ix, how=lambda e, i: e.indirect_dma_start(
            XB[:, 0, :], None, dram["h2d"], bass.IndirectOffsetOnAxis(ap=IA[:, 113:114], axis=0), bounds_check=511,
            oob_is_err=False))
        fr = {n: [] for n in ("xb", "xt", "hs", "hd", "ye")}
        t_gu, t_dn, ys = expert(128, [(gw, t_w1, 0)], [(dw, t_w2, 0)], XB[:, 0, :], t_g, fr,
                                cut(XT[:, 0, :], 8), HS[:, 0, :], cut(HD[:, 0, :], 2), YE[:, 0, :])
        t_last = PO.dma(None, None, ys, how=lambda e, i: e.indirect_dma_start(
            dram["ya"], bass.IndirectOffsetOnAxis(ap=IA[:, 112:113], axis=0), YE[:, 0, :], None, bounds_check=1023,
            oob_is_err=False))
        for lane in inner:
            if lane.n:
                gain[id(lane.sem)] = lane.n
            for q in lane.dma_sems:
                gain[id(q)] = 16
        ends = [(lane.sem, lane.n) for lane in inner if lane.n] + [(q, 16) for lane in inner for q in lane.dma_sems]
        PE, DV, AC, PO, SP = outer
        banks = banks_outer

        pe_end = [(inner[0].sem, inner[0].n)]
        awaited = {id(inner[1]): ends, id(inner[3]): ends, id(inner[4]): pe_end}
        begin = {id(inner[4]): PE.pending()}

        def loop_of(body):
            def run(e):
                n = e.value_load(IA[0:1, 95:96], min_val=0, max_val=NOV)
                with e.If(n > 0):
                    for t in begin.get(id(body), oend[0]):
                        e.wait_ge(*t)
                    with e.Fori(0, n) as i:
                        for op in body.ops:
                            op(e, i)
                        for q, v in awaited.get(id(body), ()):
                            body.until(e, q, i * v + v)
            return run

        for lane, body in zip(outer, inner):
            lane.wait(t_be, t_tok)
            lane.ops.append(loop_of(body))

        YC = [AR[:, o:o + 2048].rearrange("p (j d) -> p j d", j=2) for o in GUs[0:4]]
        ya = dram["ya"].rearrange("(t j) d -> t j d", j=2)
        for i in range(4):
            t_c = PO.dma(YC[i], ya[128 * i:128 * i + 128], oend[0], t_ya)
            m = stt(X[:, i, :], YC[i][:, 0, :], v1[:, i:i + 1], X[:, i, :], ALU.mult, ALU.add, t_c, t_gate)
            m = stt(X[:, i, :], YC[i][:, 1, :], v2[:, i:i + 1], X[:, i, :], ALU.mult, ALU.add, m)
            SP.dma(out[128 * i:128 * i + 128, :], X[:, i, :], m)
        for lane in (SP, AC, PO):
            SP.wait(lane.pending())

        block = ctx.enter_context(nc.Block())

        @block.sync
        def _(e):
            SP.play(e)

        @block.gpsimd
        def _(e):
            PO.play(e)

        @block.scalar
        def _(e):
            AC.play(e)

        @block.tensor
        def _(e):
            PE.play(e)

        @block.vector
        def _(e):
            DV.play(e)


def constants():
    f = np.float32
    i = np.arange(128)
    c = np.zeros((128, NCS), f)

    def put(name, v):
        o, w = CS[name]
        c[:, o:o + w] = v

    put("ident", np.eye(128, dtype=f))
    put("triu", (i[:, None] <= i[None, :]).astype(f))
    put("stri", (i[:, None] < i[None, :]).astype(f))
    put("ones", 1.0)
    put("e32", (CAP * np.arange(64)).astype(f)[None])
    put("rev64", (64 - np.arange(64)).astype(f)[None])
    put("rev8", (8 - np.arange(8)).astype(f)[None])
    put("iob", np.arange(31).astype(f)[None])
    put("invf", (f(500000.0) ** (-np.arange(0, 16, 2, dtype=f) / f(16))).astype(f)[None])
    put("half", -0.5)
    n = 511 - np.arange(512)
    nf = np.maximum(n, 16).astype(f)
    large = 16 + (np.log(nf / f(16)) / f(math.log(1024 / 16)) * f(16)).astype(np.int32)
    bucket = np.where(n < 16, n, np.minimum(large, 31))
    onehot = (bucket[None, :] == np.arange(32)[:, None]).astype(f)
    diag = np.where(i[:, None] >= i[None, :], 0.0, NEG).astype(f)
    prev = np.where(i[None, :] > i[:, None], 0.0, NEG).astype(f)
    mask2 = np.concatenate([diag, prev, diag, prev, diag, prev, diag], axis=1)
    tokid = (np.arange(4)[None, :] * 128 + i[:, None]).astype(np.int32)
    tokid = np.concatenate([2 * tokid, 2 * tokid + 1], axis=1)
    return c, onehot, mask2, tokid


def kernel(**inputs):
    import numpy as _np
    import concourse.bacc as _bacc
    from concourse import mybir as _mybir
    from concourse.bass_utils import run_bass_kernel_spmd as _run

    g = {k: _np.asarray(v) for k, v in inputs.items()}

    def tiles(w, c0=0, c1=None):
        w = w[:, c0:c1]
        return w.reshape(-1, 128, w.shape[1]).transpose(1, 0, 2).reshape(128, -1)

    def quarters(w, c0=0, c1=None, n=128):
        w = w[:, c0:c1]
        return w.reshape(-1, 128, w.shape[1] // n, n).transpose(1, 2, 0, 3).reshape(128, -1)

    w_in, w2 = g["w_in"][0], g["w_in_2"][0]
    pack = _np.zeros((len(SLOTS), 128, 4096), _np.float32)

    def put(name, a):
        pack[SLOT[name], :, 0:a.shape[1]] = a

    for n, o in (("cb", 0), ("cc", 512), ("cv", 1024), ("q", 1536), ("k", 2048), ("v", 2560), ("qm", 3072),
                 ("ga0", 3584), ("ga1", 4096), ("gb0", 4608), ("gb1", 5120), ("gc0", 5632), ("gc1", 6144)):
        put(n, (tiles if n == "v" else quarters)(w_in, o, o + 512))
    put("mk", quarters(g["w_mem_kv"][0], 0, 512))
    put("mv", tiles(g["w_mem_kv"][0], 512, 1024))
    put("yconv", tiles(g["w_conv_out"][0]))
    put("yattn", tiles(g["w_attn_out"][0]))
    put("ymem", tiles(g["w_mem_out"][0]))
    for s in range(2):
        put(f"out{s}", quarters(g["w_out"][0], 512 * s, 512 * s + 512, 256))
        put(f"oo{s}", quarters(g["w_out_2"][0], 512 * s, 512 * s + 512, 256))
    up = g["w_up"][0]
    for s in range(11):
        a = _np.concatenate([up[:, 256 * s:256 * s + 256], up[:, 2816 + 256 * s:2816 + 256 * s + 256]], axis=1)
        put(f"up{s}", quarters(a))
    for s in range(6):
        put(f"down{s}", tiles(g["w_down"][0][512 * s:512 * s + 512]))
    xo = 2048
    for s in range(4):
        put(f"z{s}", tiles(w2, 512 * s, 512 * s + 512))
        put(f"xs{s}", quarters(w2, xo + 512 * s, xo + 512 * s + 512))
        put(f"so{s}", quarters(g["w_ssd_out_2"][0], 256 * s, 256 * s + 256))
    put("bm", quarters(w2, xo + 2048, xo + 2560))
    put("cm", quarters(w2, xo + 2560, xo + 3072))
    qo = xo + 3072 + 32
    wq = w2[:, qo:qo + 1024].reshape(1024, 16, 64)[:, HEADS2].reshape(1024, 1024)
    wa = g["w_attn_out_2"][0].reshape(16, 64, 1024)[HEADS2].reshape(1024, 1024)
    for s in range(2):
        put(f"q{s}", tiles(wq, 512 * s, 512 * s + 512))
        put(f"ao{s}", quarters(wa, 512 * s, 512 * s + 512))
        put(f"gs{s}", quarters(w2, qo + 1536 + 512 * s, qo + 2048 + 512 * s))
        put(f"gt{s}", quarters(w2, qo + 2560 + 512 * s, qo + 3072 + 512 * s))
    put("kv", tiles(w2, qo + 1024, qo + 1536))
    wsmall = _np.concatenate([tiles(w2, xo + 3072, xo + 3104), tiles(_np.concatenate(
        [g["w_router_group_2"][0], g["w_router_expert_2"][0].transpose(1, 0, 2).reshape(1024, 64)], axis=1))], axis=1)
    we = _np.concatenate([g["w_gate_e_2"][0], g["w_up_e_2"][0]], axis=2)
    we = we.reshape(64, 8, 128, 512).transpose(0, 2, 1, 3).reshape(64, 128, 4096)
    wd = g["w_down_e_2"][0].reshape(64, 2, 128, 1024).transpose(0, 2, 1, 3).reshape(64, 128, 2048)
    wexp = _np.concatenate([we, wd], axis=2)

    wdt = _np.zeros((1024, 128), _np.float32)
    wdt[:, 0:32] = w2[:, xo + 3072:xo + 3104]
    cols = _np.zeros((128, NCOL), _np.float32)
    for n, v in (("g_pre_mix", g["g_pre_mix"]), ("g_mem", g["g_mem"]), ("b_gate", g["b_gate"]),
                 ("conv_mix", g["conv_mix_w"]), ("g_pre_ffn", g["g_pre_ffn"]), ("ffn_w", g["ffn_conv_w"]),
                 ("ffn_b", g["ffn_conv_b"]), ("norm1_g", g["norm1_g_2"]), ("conv_w", g["conv_w_2"]),
                 ("conv_b", g["conv_b_2"]), ("norm2_g", g["norm2_g_2"])):
        o, w = COL[n]
        cols[:, o:o + w] = v.reshape(w, 128).T
    rows = _np.zeros((1, NROW), _np.float32)
    for n, v in (("dt_bias", g["dt_bias_2"]), ("a_log", g["a_log_2"]), ("d_skip", g["d_skip_2"]),
                 ("q_g", g["q_norm_g_2"]), ("k_g", g["k_norm_g_2"]), ("sinks", g["sinks_2"][0][HEADS2]),
                 ("b_r", _np.concatenate([g["b_router_group_2"].reshape(-1), g["b_router_expert_2"].reshape(-1)]))):
        o, w = ROW[n]
        rows[0, o:o + w] = v.reshape(-1)
    gains = _np.concatenate([g["g_post_mix"], g["g_post_ffn"], g["norm2_g_2"]], axis=0)
    consts, onehot, mask2, tokid = constants()
    arrays = {
        "x": g["x"][0], "mem": g["mem"][0], "rel_bias": g["rel_bias"], "wpack": pack, "wexp": wexp,
        "wsmall": wsmall, "wdt": tiles(wdt), "cols": cols, "rows": rows, "gains": gains, "sng": g["ssd_norm_g_2"],
        "pos": g["positions_2"].reshape(4, 128).T, "consts": consts, "onehot": onehot, "mask2": mask2,
        "tokid": tokid,
    }
    nc = _bacc.Bacc("TRN2", target_bir_lowering=False, num_devices=1)
    ins, dram = {}, {}
    for name, a in arrays.items():
        a = _np.ascontiguousarray(a)
        ins[f"in_{name}"] = a
        dram[name] = nc.dram_tensor(f"in_{name}", a.shape, _mybir.dt.from_np(a.dtype), kind="ExternalInput").ap()
    for name, shape, dt in (("bvec", [8, 128, 640], F32), ("h2d", [512, 1024], F32),
                            ("x1d", [512, 1024], F32), ("x2d", [512, 1024], F32), ("tab", [NSLOT, 1], I32),
                            ("ya", [1024, 1024], F32)):
        dram[name] = nc.dram_tensor(name, shape, dt, kind="Internal").ap()
    out = nc.dram_tensor("out_0", [512, 1024], F32, kind="ExternalOutput").ap()
    with nc.allow_non_contiguous_dma(reason="a column of four-byte entries"):
        two_layers(nc, dram, out)
    r = _run(nc, [ins], core_ids=[0])
    return r.results[0]["out_0"].reshape(1, 512, 1024)
```
